# Optimizing a Trainium2 kernel written in Bass

```python
import math
import jax, jax.numpy as jnp
from jax import lax
import numpy as np

D_MODEL = 1024
BATCH = 1
SEQ = 512
DEPTH = 2

MEM_LEN = 256
D_FF = 2816
CONV_CH = 256
CONV_W = 31
SC_CH = 256
SC_W = 3
N_HEADS = 8
HEAD_DIM = 64
ATT_W = N_HEADS * HEAD_DIM
IDX_HEADS = 4
IDX_DIM = 64
TOPK_MAX = 256
Q_BLOCK = 128
ROPE_THETA = 10000.0
XA_HEADS = 4
XA_DIM = D_MODEL // XA_HEADS
MIX_W = CONV_CH + SC_CH + ATT_W
SPLIT_SIZES = (CONV_CH, CONV_CH,
               SC_CH, SC_CH, SC_CH,
               ATT_W, ATT_W, ATT_W,
               IDX_HEADS * IDX_DIM, IDX_DIM, IDX_HEADS)
N_IN = sum(SPLIT_SIZES)
SPLIT_POINTS = tuple(int(v) for v in np.cumsum(SPLIT_SIZES)[:-1])
IDX_SCALE = (IDX_HEADS ** -0.5) * (IDX_DIM ** -0.5)


def rms_norm(x, g, eps=1e-6):
    xf = x.astype(jnp.float32)
    y = xf * lax.rsqrt(jnp.mean(xf * xf, axis=-1, keepdims=True) + eps)
    return (y * g.astype(jnp.float32)).astype(x.dtype)

def layer_norm(x, g, b, eps=1e-5):
    xf = x.astype(jnp.float32)
    mu = jnp.mean(xf, axis=-1, keepdims=True)
    var = jnp.mean(jnp.square(xf - mu), axis=-1, keepdims=True)
    y = (xf - mu) * lax.rsqrt(var + eps)
    return (y * g.astype(jnp.float32) + b.astype(jnp.float32)).astype(x.dtype)

def swiglu(h, w_gate, w_up, w_down):
    return (jax.nn.silu(h @ w_gate) * (h @ w_up)) @ w_down

def causal_dwconv(x, w):
    width, ch = w.shape
    return lax.conv_general_dilated(
        x, w[:, None, :].astype(x.dtype), window_strides=(1,), padding=[(width - 1, 0)],
        dimension_numbers=('NWC', 'WIO', 'NWC'), feature_group_count=ch)

def rope_tables(positions, dim):
    inv_freq = ROPE_THETA ** (-jnp.arange(0, dim, 2, dtype=jnp.float32) / dim)
    ang = positions.astype(jnp.float32)[..., None] * inv_freq
    return jnp.cos(ang), jnp.sin(ang)

def apply_rope(t, cos, sin):
    tf = t.astype(jnp.float32)
    half = tf.shape[-1] // 2
    t1, t2 = tf[..., :half], tf[..., half:]
    c, s = cos[:, :, None, :], sin[:, :, None, :]
    return jnp.concatenate([t1 * c - t2 * s, t2 * c + t1 * s], axis=-1).astype(t.dtype)

def conformer_conv(a_val, a_gate, dw, dw_b, ln_g, ln_b):
    h = a_val * jax.nn.sigmoid(a_gate)
    h = causal_dwconv(h, dw) + dw_b
    return jax.nn.silu(layer_norm(h, ln_g, ln_b))

def short_gated_conv(b_gate, c_gate, h, w):
    return b_gate * causal_dwconv(c_gate * h, w)

def dsa_attention(q, k, v, q_idx, k_idx, w_idx):
    bsz, seq, nh, dh = q.shape
    topk = min(TOPK_MAX, seq // 4)
    nb = seq // Q_BLOCK
    key_pos = jnp.arange(seq)
    b_ar = jnp.arange(bsz)[:, None, None]

    def to_blocks(t):
        return jnp.moveaxis(t.reshape(bsz, nb, Q_BLOCK, *t.shape[2:]), 1, 0)

    q_pos = jnp.arange(seq).reshape(nb, Q_BLOCK)

    def one_block(args):
        qb, qib, wb, tb = args
        logits = jnp.einsum('bqhd,bsd->bqhs', qib, k_idx).astype(jnp.float32)
        score = jnp.einsum('bqh,bqhs->bqs', wb.astype(jnp.float32), jax.nn.relu(logits)) * IDX_SCALE
        causal = key_pos[None, :] <= tb[:, None]
        score = jnp.where(causal[None], score, -jnp.inf)
        top_val, top_idx = lax.top_k(score, topk)
        k_sel = k[b_ar, top_idx]
        v_sel = v[b_ar, top_idx]
        s = jnp.einsum('bqhd,bqkhd->bqhk', qb, k_sel).astype(jnp.float32) * (dh ** -0.5)
        s = jnp.where(jnp.isfinite(top_val)[:, :, None, :], s, -jnp.inf)
        p = jax.nn.softmax(s, axis=-1).astype(v.dtype)
        return jnp.einsum('bqhk,bqkhd->bqhd', p, v_sel)

    out = lax.map(one_block, (to_blocks(q), to_blocks(q_idx), to_blocks(w_idx), q_pos))
    return jnp.moveaxis(out, 0, 1).reshape(bsz, seq, nh * dh)

def memory_cross_attention(h, mem_n, wq, wkv, wo):
    bsz, seq, _ = h.shape
    m = mem_n.shape[1]
    q = (h @ wq).reshape(bsz, seq, XA_HEADS, XA_DIM)
    k, v = jnp.split(mem_n @ wkv, 2, axis=-1)
    k = k.reshape(bsz, m, XA_HEADS, XA_DIM)
    v = v.reshape(bsz, m, XA_HEADS, XA_DIM)
    s = jnp.einsum('bshd,bmhd->bhsm', q, k).astype(jnp.float32) * (XA_DIM ** -0.5)
    p = jax.nn.softmax(s, axis=-1).astype(v.dtype)
    o = jnp.einsum('bhsm,bmhd->bshd', p, v).reshape(bsz, seq, D_MODEL)
    return o @ wo

def first_inputs(seed: int = 0) -> dict:
    key = jax.random.key(seed)
    ks = iter(jax.random.split(key, 32))
    L, D, F = DEPTH, D_MODEL, D_FF

    def w(shape, fan_in):
        return jax.random.normal(next(ks), shape, jnp.float32) * (fan_in ** -0.5)

    def gain(shape):
        return 1.0 + 0.01 * jax.random.normal(next(ks), shape, jnp.float32)

    def bias(shape):
        return 0.01 * jax.random.normal(next(ks), shape, jnp.float32)

    x = jax.random.normal(next(ks), (BATCH, SEQ, D), jnp.float32)
    mem = jax.random.normal(next(ks), (BATCH, MEM_LEN, D), jnp.float32)
    start = jax.random.randint(next(ks), (BATCH, 1), 0, 1024, dtype=jnp.int32)
    positions = (start + jnp.arange(SEQ, dtype=jnp.int32)[None, :]).astype(jnp.int32)
    return {
        "x": x, "mem": mem, "positions": positions,
        "ffn1_norm": gain((L, D)), "ffn1_w_gate": w((L, D, F), D), "ffn1_w_up": w((L, D, F), D),
        "ffn1_w_down": w((L, F, D), F),
        "mix_norm": gain((L, D)), "w_in": w((L, D, N_IN), D),
        "conf_dw": w((L, CONV_W, CONV_CH), CONV_W), "conf_dw_b": bias((L, CONV_CH)),
        "conf_ln_g": gain((L, CONV_CH)), "conf_ln_b": bias((L, CONV_CH)),
        "sc_dw": w((L, SC_W, SC_CH), SC_W),
        "w_out": w((L, MIX_W, D), MIX_W),
        "xa_norm": gain((L, D)), "mem_norm": gain((L, D)),
        "xa_wq": w((L, D, D), D), "xa_wkv": w((L, D, 2 * D), D), "xa_wo": w((L, D, D), D),
        "ffn2_norm": gain((L, D)), "ffn2_w_gate": w((L, D, F), D), "ffn2_w_up": w((L, D, F), D),
        "ffn2_w_down": w((L, F, D), F),
        "final_norm": gain((D,)),
    }

def first_block(x, mem, positions, ffn1_norm, ffn1_w_gate, ffn1_w_up, ffn1_w_down, mix_norm, w_in,
              conf_dw, conf_dw_b, conf_ln_g, conf_ln_b, sc_dw, w_out, xa_norm, mem_norm,
              xa_wq, xa_wkv, xa_wo, ffn2_norm, ffn2_w_gate, ffn2_w_up, ffn2_w_down, final_norm):
    bsz, seq, _ = x.shape
    cos, sin = rope_tables(positions, HEAD_DIM)
    for l in range(DEPTH):
        x = x + 0.5 * swiglu(rms_norm(x, ffn1_norm[l]), ffn1_w_gate[l], ffn1_w_up[l], ffn1_w_down[l])
        h = rms_norm(x, mix_norm[l])
        (a_val, a_gate, b_gate, c_gate, b_h, q, k, v,
         q_idx, k_idx, w_idx) = jnp.split(h @ w_in[l], SPLIT_POINTS, axis=-1)
        y_a = conformer_conv(a_val, a_gate, conf_dw[l], conf_dw_b[l], conf_ln_g[l], conf_ln_b[l])
        y_b = short_gated_conv(b_gate, c_gate, b_h, sc_dw[l])
        q = apply_rope(q.reshape(bsz, seq, N_HEADS, HEAD_DIM), cos, sin)
        k = apply_rope(k.reshape(bsz, seq, N_HEADS, HEAD_DIM), cos, sin)
        v = v.reshape(bsz, seq, N_HEADS, HEAD_DIM)
        q_idx = apply_rope(q_idx.reshape(bsz, seq, IDX_HEADS, IDX_DIM), cos, sin)
        k_idx = apply_rope(k_idx[:, :, None, :], cos, sin)[:, :, 0, :]
        y_c = dsa_attention(q, k, v, q_idx, k_idx, w_idx)
        x = x + jnp.concatenate([y_a, y_b, y_c], axis=-1) @ w_out[l]
        x = x + memory_cross_attention(rms_norm(x, xa_norm[l]), rms_norm(mem, mem_norm[l]),
                                       xa_wq[l], xa_wkv[l], xa_wo[l])
        x = x + 0.5 * swiglu(rms_norm(x, ffn2_norm[l]), ffn2_w_gate[l], ffn2_w_up[l], ffn2_w_down[l])
    return rms_norm(x, final_norm)


EPS = 1e-6
MLA_HEADS = 4
MLA_NOPE = 128
MLA_ROPE = 64
MLA_V = 128
MLA_Q_RANK = 384
MLA_KV_RANK = 256
MLA_ROPE_BASE = 10000.0
GLA_HEADS = 4
GLA_DK = 32
GLA_DV = 64
GLA_GATE_RANK = 16
GLA_GATE_NORM = 16.0
GLA_CHUNK = 64
RET_HEADS = 4
RET_DK = 32
RET_DV = 64
RET_CHUNK = 64
RET_ROPE_BASE = 10000.0
D_MIX = MLA_HEADS * MLA_V + GLA_HEADS * GLA_DV + RET_HEADS * RET_DV
IN_SIZES = (MLA_Q_RANK, MLA_KV_RANK, MLA_ROPE,
            GLA_HEADS * GLA_DK, GLA_HEADS * GLA_DK, GLA_HEADS * GLA_DV, GLA_GATE_RANK, GLA_HEADS * GLA_DV,
            RET_HEADS * RET_DK, RET_HEADS * RET_DK, RET_HEADS * RET_DV, RET_HEADS * RET_DV)
D_IN = sum(IN_SIZES)
CONV_W_2 = 3


def rmsnorm(x, gain):
    xf = x.astype(jnp.float32)
    y = xf * lax.rsqrt(jnp.mean(xf * xf, axis=-1, keepdims=True) + EPS)
    return (y * gain.astype(jnp.float32)).astype(x.dtype)

def head_rmsnorm(x, gain):
    H, d = x.shape[-2], x.shape[-1]
    return rmsnorm(x, gain.reshape(H, d))

def rope_tables_2(S, dim, base):
    inv = base ** (-(jnp.arange(0, dim, 2, dtype=jnp.float32) / dim))
    ang = jnp.arange(S, dtype=jnp.float32)[:, None] * inv[None, :]
    return jnp.cos(ang), jnp.sin(ang)

def apply_rope_2(x, cos, sin):
    half = x.shape[-1] // 2
    c = cos[None, :, None, :].astype(x.dtype)
    s = sin[None, :, None, :].astype(x.dtype)
    x1, x2 = x[..., :half], x[..., half:]
    return jnp.concatenate([x1 * c - x2 * s, x2 * c + x1 * s], axis=-1)

def mla_attention(q_nope, q_rope, k_nope, k_rope, v):
    B, S, H, dn = q_nope.shape
    dr = q_rope.shape[-1]
    nb = S // Q_BLOCK
    scale = (MLA_NOPE + MLA_ROPE) ** -0.5
    qn = q_nope.reshape(B, nb, Q_BLOCK, H, dn).transpose(1, 0, 2, 3, 4)
    qr = q_rope.reshape(B, nb, Q_BLOCK, H, dr).transpose(1, 0, 2, 3, 4)
    key_pos = jnp.arange(S)

    def one_block(args):
        qn_b, qr_b, start = args
        s = (jnp.einsum('bqhd,bkhd->bhqk', qn_b, k_nope)
             + jnp.einsum('bqhd,bkd->bhqk', qr_b, k_rope)).astype(jnp.float32) * scale
        q_pos = start + jnp.arange(Q_BLOCK)
        mask = key_pos[None, :] <= q_pos[:, None]
        s = jnp.where(mask[None, None], s, jnp.finfo(jnp.float32).min)
        p = jax.nn.softmax(s, axis=-1).astype(v.dtype)
        return jnp.einsum('bhqk,bkhd->bqhd', p, v)

    out = lax.map(one_block, (qn, qr, jnp.arange(nb) * Q_BLOCK))
    return out.transpose(1, 0, 2, 3, 4).reshape(B, S, H, v.shape[-1])

def mla_branch(c_q, c_kv, k_rope, q_norm, w_uq, kv_norm, w_ukv, cos, sin):
    B, S, _ = c_q.shape
    q = (rmsnorm(c_q, q_norm) @ w_uq).reshape(B, S, MLA_HEADS, MLA_NOPE + MLA_ROPE)
    q_nope, q_rope = q[..., :MLA_NOPE], apply_rope_2(q[..., MLA_NOPE:], cos, sin)
    kv = (rmsnorm(c_kv, kv_norm) @ w_ukv).reshape(B, S, MLA_HEADS, MLA_NOPE + MLA_V)
    k_nope, v = kv[..., :MLA_NOPE], kv[..., MLA_NOPE:]
    k_r = apply_rope_2(k_rope[:, :, None, :], cos, sin)[:, :, 0, :]
    return mla_attention(q_nope, q_rope, k_nope, k_r, v)

def gla_chunked(q, k, v, log_a):
    B, S, H, dk = q.shape
    dv = v.shape[-1]
    C = GLA_CHUNK
    n = S // C
    to_chunks = lambda t: t.astype(jnp.float32).reshape(B, n, C, H, t.shape[-1]).transpose(1, 0, 3, 2, 4)
    qc, kc, vc, gc = to_chunks(q), to_chunks(k), to_chunks(v), to_chunks(log_a)
    tril = jnp.tril(jnp.ones((C, C), dtype=bool))

    def step(state, inp):
        qb, kb, vb, gb = inp
        b = jnp.cumsum(gb, axis=-2)
        inter = jnp.einsum('bhik,bhkv->bhiv', qb * jnp.exp(b), state)
        diff = b[..., :, None, :] - b[..., None, :, :]
        dec = jnp.where(tril[:, :, None], jnp.exp(jnp.where(tril[:, :, None], diff, 0.0)), 0.0)
        A = jnp.einsum('bhik,bhjk,bhijk->bhij', qb, kb, dec)
        intra = jnp.einsum('bhij,bhjv->bhiv', A, vb)
        b_end = b[..., -1:, :]
        new_state = state * jnp.exp(b_end)[..., 0, :, None] + jnp.einsum(
            'bhjk,bhjv->bhkv', kb * jnp.exp(b_end - b), vb)
        return new_state, inter + intra

    state0 = jnp.zeros((B, H, dk, dv), jnp.float32)
    _, out = lax.scan(step, state0, (qc, kc, vc, gc))
    return out.transpose(1, 0, 3, 2, 4).reshape(B, S, H, dv).astype(v.dtype)

def gla_branch(q, k, v, gate_lr, g, w_gate, b_gate, out_norm):
    B, S, _ = q.shape
    qh = q.reshape(B, S, GLA_HEADS, GLA_DK) * (GLA_DK ** -0.5)
    kh = k.reshape(B, S, GLA_HEADS, GLA_DK)
    vh = v.reshape(B, S, GLA_HEADS, GLA_DV)
    gk = (gate_lr @ w_gate + b_gate).astype(jnp.float32)
    log_a = (jax.nn.log_sigmoid(gk) / GLA_GATE_NORM).reshape(B, S, GLA_HEADS, GLA_DK)
    o = gla_chunked(qh, kh, vh, log_a)
    o = head_rmsnorm(o, out_norm).reshape(B, S, GLA_HEADS * GLA_DV)
    return o * jax.nn.silu(g)

def retention_chunked(q, k, v):
    B, S, H, dk = q.shape
    dv = v.shape[-1]
    C = RET_CHUNK
    n = S // C
    to_chunks = lambda t: t.astype(jnp.float32).reshape(B, n, C, H, t.shape[-1]).transpose(0, 3, 1, 2, 4)
    qc, kc, vc = to_chunks(q), to_chunks(k), to_chunks(v)
    log_g = jnp.log(1.0 - 2.0 ** (-5.0 - jnp.arange(H, dtype=jnp.float32)))
    idx = jnp.arange(C, dtype=jnp.float32)
    diff = idx[:, None] - idx[None, :]
    D = jnp.where(diff >= 0, jnp.exp(log_g[:, None, None] * jnp.maximum(diff, 0.0)), 0.0)
    scores = jnp.einsum('bhnid,bhnjd->bhnij', qc, kc) * D[None, :, None]
    intra = jnp.einsum('bhnij,bhnjv->bhniv', scores, vc)
    k_dec = kc * jnp.exp(log_g[:, None] * (C - 1 - idx)[None, :])[None, :, None, :, None]
    U = jnp.einsum('bhnjd,bhnjv->nbhdv', k_dec, vc)
    chunk_decay = jnp.exp(log_g * C)[None, :, None, None]

    def step(R, u):
        return R * chunk_decay + u, R

    _, R_prev = lax.scan(step, jnp.zeros((B, H, dk, dv), jnp.float32), U)
    q_dec = qc * jnp.exp(log_g[:, None] * (idx + 1.0)[None, :])[None, :, None, :, None]
    inter = jnp.einsum('bhnid,nbhdv->bhniv', q_dec, R_prev)
    out = (intra + inter).transpose(0, 2, 3, 1, 4).reshape(B, S, H, dv)
    return out.astype(v.dtype)

def retention_branch(q, k, v, g, out_norm, cos, sin):
    B, S, _ = q.shape
    qh = apply_rope_2(q.reshape(B, S, RET_HEADS, RET_DK), cos, sin)
    kh = apply_rope_2(k.reshape(B, S, RET_HEADS, RET_DK), cos, sin) * (RET_DK ** -0.5)
    vh = v.reshape(B, S, RET_HEADS, RET_DV)
    o = retention_chunked(qh, kh, vh)
    o = head_rmsnorm(o, out_norm).reshape(B, S, RET_HEADS * RET_DV)
    return o * jax.nn.silu(g)

def causal_dwconv_2(a, w, b):
    S = a.shape[1]
    p = jnp.pad(a, ((0, 0), (CONV_W_2 - 1, 0), (0, 0)))
    out = b
    for kk in range(CONV_W_2):
        out = out + p[:, kk:kk + S] * w[kk]
    return out

def second_inputs(seed: int = 0) -> dict:
    key = jax.random.key(seed)
    ks = jax.random.split(key, 19)
    f32 = jnp.float32
    nrm = lambda k, shape, scale: jax.random.normal(k, shape, f32) * scale
    gain = lambda k, shape: 1.0 + 0.02 * jax.random.normal(k, shape, f32)
    return {
        "x": nrm(ks[0], (BATCH, SEQ, D_MODEL), 1.0),
        "attn_norm": gain(ks[1], (DEPTH, D_MODEL)),
        "w_in": nrm(ks[2], (DEPTH, D_MODEL, D_IN), D_MODEL ** -0.5),
        "mla_q_norm": gain(ks[3], (DEPTH, MLA_Q_RANK)),
        "mla_w_uq": nrm(ks[4], (DEPTH, MLA_Q_RANK, MLA_HEADS * (MLA_NOPE + MLA_ROPE)), MLA_Q_RANK ** -0.5),
        "mla_kv_norm": gain(ks[5], (DEPTH, MLA_KV_RANK)),
        "mla_w_ukv": nrm(ks[6], (DEPTH, MLA_KV_RANK, MLA_HEADS * (MLA_NOPE + MLA_V)), MLA_KV_RANK ** -0.5),
        "mla_out_norm": gain(ks[7], (DEPTH, MLA_HEADS * MLA_V)),
        "gla_w_gate": nrm(ks[8], (DEPTH, GLA_GATE_RANK, GLA_HEADS * GLA_DK), GLA_GATE_RANK ** -0.5),
        "gla_b_gate": nrm(ks[9], (DEPTH, GLA_HEADS * GLA_DK), 0.02),
        "gla_out_norm": gain(ks[10], (DEPTH, GLA_HEADS * GLA_DV)),
        "ret_out_norm": gain(ks[11], (DEPTH, RET_HEADS * RET_DV)),
        "w_out": nrm(ks[12], (DEPTH, D_MIX, D_MODEL), D_MIX ** -0.5),
        "ffn_norm": gain(ks[13], (DEPTH, D_MODEL)),
        "ffn_w_up": nrm(ks[14], (DEPTH, D_MODEL, 2 * D_FF), D_MODEL ** -0.5),
        "ffn_conv_w": nrm(ks[15], (DEPTH, CONV_W_2, D_FF), CONV_W_2 ** -0.5),
        "ffn_conv_b": nrm(ks[16], (DEPTH, D_FF), 0.02),
        "ffn_w_down": nrm(ks[17], (DEPTH, D_FF, D_MODEL), D_FF ** -0.5),
        "final_norm": gain(ks[18], (D_MODEL,)),
    }

def second_block(x, attn_norm, w_in, mla_q_norm, mla_w_uq, mla_kv_norm, mla_w_ukv, mla_out_norm,
              gla_w_gate, gla_b_gate, gla_out_norm, ret_out_norm, w_out, ffn_norm, ffn_w_up,
              ffn_conv_w, ffn_conv_b, ffn_w_down, final_norm):
    B, S, _ = x.shape
    mla_cos, mla_sin = rope_tables_2(S, MLA_ROPE, MLA_ROPE_BASE)
    ret_cos, ret_sin = rope_tables_2(S, RET_DK, RET_ROPE_BASE)
    split_points = []
    acc = 0
    for sz in IN_SIZES[:-1]:
        acc += sz
        split_points.append(acc)

    for l in range(DEPTH):
        h = rmsnorm(x, attn_norm[l])
        z = h @ w_in[l]
        (c_q, c_kv, k_rope, g_q, g_k, g_v, g_lr, g_g, r_q, r_k, r_v, r_g) = jnp.split(z, split_points, axis=-1)
        y_a = mla_branch(c_q, c_kv, k_rope, mla_q_norm[l], mla_w_uq[l], mla_kv_norm[l], mla_w_ukv[l],
                         mla_cos, mla_sin)
        y_a = head_rmsnorm(y_a, mla_out_norm[l]).reshape(B, S, MLA_HEADS * MLA_V)
        y_b = gla_branch(g_q, g_k, g_v, g_lr, g_g, gla_w_gate[l], gla_b_gate[l], gla_out_norm[l])
        y_c = retention_branch(r_q, r_k, r_v, r_g, ret_out_norm[l], ret_cos, ret_sin)
        x = x + jnp.concatenate([y_a, y_b, y_c], axis=-1) @ w_out[l]
        h = rmsnorm(x, ffn_norm[l])
        u = h @ ffn_w_up[l]
        a, bv = u[..., :D_FF], u[..., D_FF:]
        a = causal_dwconv_2(a, ffn_conv_w[l], ffn_conv_b[l])
        x = x + (jax.nn.silu(a) * bv) @ ffn_w_down[l]

    return rmsnorm(x, final_norm)


def setup_inputs(seed=0):
    out = dict(first_inputs(seed))
    for name, value in second_inputs(seed + 1).items():
        if name != "x":
            out[name + "_2"] = value
    return out


def reference(
    x, mem, positions, ffn1_norm, ffn1_w_gate, ffn1_w_up, ffn1_w_down, mix_norm, w_in, conf_dw,
    conf_dw_b, conf_ln_g, conf_ln_b, sc_dw, w_out, xa_norm, mem_norm, xa_wq, xa_wkv, xa_wo,
    ffn2_norm, ffn2_w_gate, ffn2_w_up, ffn2_w_down, final_norm, attn_norm_2, w_in_2,
    mla_q_norm_2, mla_w_uq_2, mla_kv_norm_2, mla_w_ukv_2, mla_out_norm_2, gla_w_gate_2,
    gla_b_gate_2, gla_out_norm_2, ret_out_norm_2, w_out_2, ffn_norm_2, ffn_w_up_2, ffn_conv_w_2,
    ffn_conv_b_2, ffn_w_down_2, final_norm_2,
):
    x = first_block(
        x, mem, positions, ffn1_norm, ffn1_w_gate, ffn1_w_up, ffn1_w_down, mix_norm, w_in,
        conf_dw, conf_dw_b, conf_ln_g, conf_ln_b, sc_dw, w_out, xa_norm, mem_norm, xa_wq,
        xa_wkv, xa_wo, ffn2_norm, ffn2_w_gate, ffn2_w_up, ffn2_w_down, final_norm,
    )
    return second_block(
        x, attn_norm_2, w_in_2, mla_q_norm_2, mla_w_uq_2, mla_kv_norm_2, mla_w_ukv_2,
        mla_out_norm_2, gla_w_gate_2, gla_b_gate_2, gla_out_norm_2, ret_out_norm_2, w_out_2,
        ffn_norm_2, ffn_w_up_2, ffn_conv_w_2, ffn_conv_b_2, ffn_w_down_2, final_norm_2,
    )


_drawn_inputs = setup_inputs


def setup_inputs(seed=0):
    import zlib

    import numpy as np

    out = dict(_drawn_inputs(seed))
    spreads = {}
    factors = {'ffn1_norm': 3.982,
     'conf_ln_g': 4.667,
     'conf_ln_b': 3.669,
     'xa_norm': 8.0,
     'mem_norm': 8.0,
     'ffn2_norm': 3.561,
     'final_norm': 3.674,
     'mla_q_norm_2': 6.896,
     'mla_out_norm_2': 9.217,
     'gla_b_gate_2': 8.0,
     'gla_out_norm_2': 21.883,
     'ret_out_norm_2': 33.301,
     'ffn_norm_2': 3.228,
     'ffn_conv_b_2': 4.66,
     'final_norm_2': 21.581}
    for name, (base, spread) in spreads.items():
        noise = np.random.default_rng([zlib.crc32(name.encode()), seed]).standard_normal(out[name].shape)
        drawn = base * np.exp(spread * noise) if base else spread * noise
        out[name] = __import__('jax').numpy.asarray(drawn.astype(out[name].dtype))
    for name, factor in factors.items():
        out[name] = (out[name] * factor).astype(out[name].dtype)
    return out
```

```python
import numpy as np
import concourse.bass as bass
from concourse import mybir

F32 = mybir.dt.float32
F32R = mybir.dt.float32r
I32 = mybir.dt.int32
U8 = mybir.dt.uint8
ACT = mybir.ActivationFunctionType
ALU = mybir.AluOpType
AXX = mybir.AxisListType.X

P = 128
S = 512
T = S // P
D = 1024
KD = D // P
L = 2
F = 2816
KF = F // P
M = 256
MT = M // P
A = KD * P
KH = KF // 2
DN = KH * P
HEADS = 8
IDXH = 4
TOPK = 128
CONVW = 31
XH = 4
MH = 4
DK = 32
LEVELS = 8
NPAR1 = 5 * KD + 2 * CONVW + 3 * 2 + 2 * 3 + KD
NPAR2 = KD + 3 + 2 + 4 + 1 + 2 + 2 + KD + KD
MASKED = -1.0e30
TAKEN = -3.0e38
TAKEN_BELOW = -2.0e38
PI = float(np.pi)
TWO_PI_PARTS = (6.28125, 0.0019350051879882812, 3.019915981956752e-07)
ROUND = 1.5 * 2.0 ** 23
LEAD = 2
FIRST_BLOCK = (0, 4, 7, 9)
BLOCKS = [(a, c) for a in range(T) for c in range(a, T)]
BIAS_AT = (0, 128, 384, 768)
MIX1_CHUNKS = 25 + 8 + 16 + 8 + 8
MIX2_CHUNKS = 19 + 3 + 2 + 8
C1 = 2 * KF + 16 + 1 + MIX1_CHUNKS + 2 * KF + 16
C2 = MIX2_CHUNKS + 2 * KF + 16


class Signal:

    def __init__(self, sem, per_layer, lead):
        self.sem, self.per_layer, self.lead = sem, per_layer, lead

    def __call__(self, layer, n):
        return layer * self.per_layer + (n + self.lead)


class Chunk:

    def __init__(self, stack_start, per_layer, layer, c, i=0):
        self.n = layer * per_layer + i * 2 + (stack_start + c)
        self.half = layer * (per_layer // 2) + i + (stack_start + c) // 2
        self.slot = c % 2


def program(nc, x_in, mem_in, pos_in, par1, par2, convpar, consts, masks, gate_w,
            gu1, dn1, widx, mid, gu2, dn2, mix2, up2, dn3, y_out):
    leads = []

    def sig(name, per_layer, lead=0):
        s = Signal(nc.alloc_semaphore(name), per_layer, lead)
        if lead:
            leads.append((s.sem, lead))
        return s

    start = (nc.sbuf_base + 63) // 64 * 64
    arena = nc.alloc_sbuf_tensor("arena", [P, (nc.sbuf_usable_end - start) // 4 - 32], F32)
    top = [start]

    def place(name, shape, dt=F32, at=None):
        where = top[0] if at is None else at
        t = nc.alloc_sbuf_tensor_at(name, [P] + list(shape), dt, offset=where)
        if at is None:
            top[0] += (int(np.prod(shape)) * (1 if dt == U8 else 4) + 31) // 32 * 32
            assert top[0] <= nc.sbuf_usable_end, (name, top[0], nc.sbuf_usable_end)
        return t

    x = place("x", [KD, S])
    hh = place("h_hi", [KD, S], F32R)
    yf_at = top[0]
    hl = place("h_lo", [KD, S], F32R)
    yf = place("branch_out", [KD, S], at=yf_at)
    raw = place("w_raw", [2, DN])
    wh = place("w_hi", [2, DN], F32R)
    wl = place("w_lo", [2, DN], F32R)
    ones = place("ones", [P])
    halves = place("halves", [2, P])
    halfcol = place("halfcol", [2])
    ident = place("ident", [P])
    causal = place("causal", [S])
    cols = place("cols", [4])
    p1 = place("params1", [NPAR1])
    p2 = place("params2", [NPAR2])
    st = place("stats", [3, 48])
    sq = place("squares", [2, S])
    ssum = place("square_sum", [S])
    hf = place("scaled", [2, S])
    dg = place("diagonals", [2, 8, P])
    one = place("one", [4])
    gate_cells = place("gate_cells", [5])
    small = place("small", [2, 4])
    cpar = place("conv_par", [KF, 4])
    rt = dg[:, :, :, :].rearrange("p b e c -> p (b e c)")[:, 0:3 * S].rearrange("p (n s) -> p n s", n=3)
    region = top[0]

    ah = place("act_hi", [KF, S], F32R)
    al = place("act_lo", [KF, S], F32R)
    after_act = top[0]
    top[0] = keep1 = (nc.sbuf_usable_end - 64 - 4 * (2 * S + KD * M)) // 32 * 32
    cos1 = place("cos1", [S])
    sin1 = place("sin1", [S])
    memn = place("mem_normed", [KD, M])
    sg, af, cv = sq, hf, dg[:, :, :, :].rearrange("p b e c -> p b (e c)")
    top[0] = region
    qk_hi_at = top[0]
    qk_hi = place("qk_hi", [KD, S], F32R)
    qk_lo_at = top[0]
    qk_lo = place("qk_lo", [KD, S], F32R)
    qk_swap = place("qk_swap", [KD, S], at=qk_hi_at)
    qk_raw = place("qk_raw", [KD, S], at=qk_lo_at)
    v_at = top[0]
    v_hi = place("v_hi", [T, S], F32R)
    v_lo = place("v_lo", [T, S], F32R)
    ix_hi = place("ix_hi", [3, S], F32R, at=v_at)
    ix_lo = place("ix_lo", [3, S], F32R, at=v_at + 3 * S * 4)
    ix_swap = place("ix_swap", [3, S], at=v_at)
    ix_raw = place("ix_raw", [3, S], at=v_at + 3 * S * 4)
    bias = place("bias", [1280])
    best = place("best", [8])
    widx_tok = place("w_idx", [16])
    conv_at = top[0]
    aval = place("a_val", [2, S])
    asig = place("a_sig", [2, S])
    bgate = place("b_gate", [2, S])
    bh = place("b_h", [2, S])
    cgate = place("c_gate", [2, S])
    rbuf = place("relu", [2, S], at=top[0])
    xpad = place("conv_in", [2, CONVW - 1 + S])
    acc = place("conv_acc", [2, S])
    yb = bh
    assert top[0] <= keep1 and after_act <= keep1
    top[0] = conv_at
    pbuf = place("probs", [2, S])
    pt_hi = place("probsT_hi", [T, S], F32R)
    pt_lo = place("probsT_lo", [T, S], F32R)
    assert top[0] <= keep1
    top[0] = region
    mh_hi = place("mem_hi", [KD, M], F32R)
    mh_lo = place("mem_lo", [KD, M], F32R)
    mf = place("mem_scaled", [2, M])
    km_hi = place("kmem_hi", [KD, M], F32R)
    km_lo = place("kmem_lo", [KD, M], F32R)
    vm_hi = place("vmem_hi", [MT, D], F32R)
    vm_lo = place("vmem_lo", [MT, D], F32R)
    xp = place("xprobs", [2, S])
    xpt_hi = place("xprobsT_hi", [T, S], F32R)
    xpt_lo = place("xprobsT_lo", [T, S], F32R)
    assert top[0] <= keep1
    qx_hi = place("qx_hi", [KD, S], F32R, at=region)
    qx_lo = place("qx_lo", [KD, S], F32R, at=top[0])
    top[0] += KD * S * 4
    assert mf is not None and KD * S * 4 <= 2 * KD * M * 4 and top[0] <= keep1
    top[0] = region
    cq_hi = place("cq_hi", [3, S], F32R)
    cq_lo = place("cq_lo", [3, S], F32R)
    ck_hi = place("ck_hi", [2, S], F32R)
    ck_lo = place("ck_lo", [2, S], F32R)
    mpt_hi = place("mprobsT_hi", [T, S], F32R, at=region)
    mpt_lo = place("mprobsT_lo", [T, S], F32R, at=region + T * S * 4)
    assert region + 2 * T * S * 4 <= top[0]
    gates = place("gates", [4, S])
    kr_hi_at = top[0]
    kr_hi = place("kr_hi", [S], F32R)
    kr_lo = place("kr_lo", [S], F32R)
    kr_swap = place("kr_swap", [S], at=kr_hi_at)
    kr_raw = place("kr_raw", [S], at=kr_hi_at + S * 4)
    mcos = place("mcos", [S])
    msin = place("msin", [S])
    branch_at = top[0]
    glr = place("glr", [S])
    gw = place("gate_w", [P])
    gqk = place("gqk", [2, S])
    rqk = place("rqk", [2, S])
    ret_at_byte = top[0]
    rswap = place("rswap", [2, S])
    rcos = place("rcos", [S])
    rsin = place("rsin", [S])
    decay = place("decay", [T, MH, P])
    ret_end = top[0]
    top[0] = ret_at_byte
    diff = place("diff", [2, S])
    edec = place("edec", [2, S])
    qe = place("qe", [2, S])
    ke = place("ke", [2, S])
    top[0] = max(top[0], ret_end)
    vgr = place("vgr", [T, S])
    pair_at = top[0]
    pair = place("pair", [len(BLOCKS), MH, P])
    cq = place("c_q", [3, S], at=pair_at)
    ckv = place("c_kv", [2, S], at=pair_at + 3 * S * 4)
    lmask = place("lmask", [LEVELS, P], U8)
    zb = place("zb", [2, S])
    cum = place("cum", [S])
    k3 = place("k3", [3, P])
    etot = place("etot", [T])
    scanmask = place("scanmask", [S])
    top[0] = branch_at
    qn_hi = place("qn_hi", [MH, S], F32R)
    qn_lo = place("qn_lo", [MH, S], F32R)
    qr_hi_at = top[0]
    qr_hi = place("qr_hi", [2, S], F32R)
    qr_lo_at = top[0]
    qr_lo = place("qr_lo", [2, S], F32R)
    qr_swap = place("qr_swap", [2, S], at=qr_hi_at)
    qr_raw = place("qr_raw", [2, S], at=qr_lo_at)
    kn_hi = place("kn_hi", [MH, S], F32R)
    kn_lo = place("kn_lo", [MH, S], F32R)
    vm2_hi = place("vm2_hi", [T, S], F32R)
    vm2_lo = place("vm2_lo", [T, S], F32R)
    mp = place("mprobs", [2, S])

    banks = nc.alloc_psum_tensor("banks", [P, 8, S], F32)
    bank = [banks[:, i, :] for i in range(8)]

    class Ring:
        raw_in = [nc.alloc_semaphore("ring_raw_in0"), nc.alloc_semaphore("ring_raw_in1")]
        hi = nc.alloc_semaphore("ring_hi")
        split = nc.alloc_semaphore("ring_split")
        done = nc.alloc_semaphore("ring_done")

    leads += [(Ring.split, LEAD), (Ring.done, LEAD)]
    consts_in = nc.alloc_semaphore("consts_in")
    x_in_sem = nc.alloc_semaphore("x_in_sem")
    setup = nc.alloc_semaphore("setup_done")
    led = nc.alloc_semaphore("lead_given")
    tab = nc.alloc_semaphore("rope_table_steps")
    tab_sin = nc.alloc_semaphore("rope_sines")
    y_stored = nc.alloc_semaphore("y_stored")
    par1_in, par2_in = sig("par1_in", 16), sig("par2_in", 16)
    cpar_in = sig("cpar_in", 16)
    tables2_in = sig("tables2_in", 16 * 8)

    class NormSems:
        sq = sig("norm_squared", 0)
        sum = sig("norm_summed", 0, LEAD)
        spread = sig("norm_spread", 0)
        inv = sig("norm_inverse", 0)
        rstd = sig("norm_rstd", 0)
        dg = sig("norm_diag", 0)
        scaled = sig("norm_scaled", 0)
        hi = sig("norm_hi", 0, LEAD)
        lo = sig("norm_lo", 0, LEAD)

    class Norm:

        def __init__(self, k, norms, tiles_before, parts_before, per_norms=0, per_tiles=0, tiles=T):
            self.k, self.tiles = k, tiles
            self.sq = Signal(NormSems.sq.sem, per_tiles, tiles_before)
            self.sum = Signal(NormSems.sum.sem, per_tiles, tiles_before + LEAD)
            self.spread = Signal(NormSems.spread.sem, 2 * per_norms, 2 * norms)
            self.inv = Signal(NormSems.inv.sem, 5 * per_norms, 5 * norms)
            self.rstd = Signal(NormSems.rstd.sem, per_norms, norms)
            self.dg = Signal(NormSems.dg.sem, per_norms, norms)
            self.scaled = Signal(NormSems.scaled.sem, per_tiles, tiles_before)
            self.hi = Signal(NormSems.hi.sem, per_tiles, parts_before + LEAD)
            self.lo = Signal(NormSems.lo.sem, per_tiles, parts_before + LEAD)

    memnorm = Norm(KD, 0, 0, 0, tiles=MT)
    N1, N2 = 4 * KD, 2 * KD + 3 + 2
    ffn1norm, mixnorm, xanorm, ffn2norm = [Norm(KD, 1 + i, KD * (1 + i), KD * i, 4, N1) for i in range(4)]
    finalnorm = Norm(KD, 1 + 4 * L, KD + N1 * L, 0)
    attnorm, cqnorm, cknorm, ffn3norm = [
        Norm(k, 2 + 4 * L + i, 2 * KD + N1 * L + before, N1 * L + before, 4, N2)
        for i, (k, before) in enumerate([(KD, 0), (3, KD), (2, KD + 3), (KD, KD + 5)])]
    endnorm = Norm(KD, 2 + 8 * L, 2 * KD + (N1 + N2) * L, 0)

    class FfnSems:
        conv = sig("ffn_conv", 0)
        silu = sig("ffn_silu", 0, LEAD)
        act = sig("ffn_act", 0, LEAD)
        act_hi = sig("ffn_act_hi", 0, LEAD)
        act_lo = sig("ffn_act_lo", 0)

    class Ffn:

        def __init__(self, name, norm, before, per):
            self.norm = norm
            self.conv = Signal(FfnSems.conv.sem, 3 * KF, 0)
            self.silu = Signal(FfnSems.silu.sem, per * KF, before * KF + LEAD)
            self.act = Signal(FfnSems.act.sem, per * KF, before * KF + LEAD)
            self.act_hi = Signal(FfnSems.act_hi.sem, per * KF, before * KF + LEAD)
            self.act_lo = Signal(FfnSems.act_lo.sem, per * KF, before * KF)
            self.x = sig(name + "_x", KD, KD)

    class AttentionSems:
        score = sig("att_score", 0)
        max = sig("att_max", 0, LEAD)
        neg = sig("att_neg", 0)
        exp = sig("att_exp", 0, LEAD)
        inv = sig("att_inv", 0)
        prob = sig("att_prob", 0)
        turn = sig("att_turn", 0, LEAD)
        pt_hi = sig("att_pt_hi", 0)
        pt_lo = sig("att_pt_lo", 0, LEAD)
        out = sig("att_out", 0, LEAD)
        y_hi = sig("att_y_hi", 0, 2 * LEAD)
        y_lo = sig("att_y_lo", 0, 2 * LEAD)

    class Attention:

        def __init__(self, heads, outs, before, per):
            self.items, self.outs = heads * T, outs

            def item(s, lead=0):
                return Signal(s.sem, per[0] * T, before[0] * T + lead)

            self.score, self.neg = item(AttentionSems.score), item(AttentionSems.neg)
            self.max, self.exp = item(AttentionSems.max, LEAD), item(AttentionSems.exp, LEAD)
            self.inv, self.prob = item(AttentionSems.inv), item(AttentionSems.prob)
            self.turn, self.pt_hi = item(AttentionSems.turn, LEAD), item(AttentionSems.pt_hi)
            self.pt_lo = item(AttentionSems.pt_lo, LEAD)
            self.out = Signal(AttentionSems.out.sem, per[0], before[0] + LEAD)
            self.y_hi = Signal(AttentionSems.y_hi.sem, per[1], before[1] + 2 * LEAD)
            self.y_lo = Signal(AttentionSems.y_lo.sem, per[1], before[1] + 2 * LEAD)

    ffn1, ffn2, ffn3 = Ffn("ffn1", ffn1norm, 0, 2), Ffn("ffn2", ffn2norm, 1, 2), Ffn("ffn3", ffn3norm, 2 * L, 1)
    H1, O1 = HEADS + XH, HEADS + 2 * XH
    dsa, xat = Attention(HEADS, 1, (0, 0), (H1, O1)), Attention(XH, 2, (HEADS, HEADS), (H1, O1))
    mla = Attention(MH, 1, (H1 * L, O1 * L), (MH, MH))
    widx_tok_s = sig("widx_tok", 1)
    evicted = sig("proj_evicted", 21, LEAD)
    swap1 = [sig(f"swap1_{j}", 64) for j in range(11)]
    rope1 = sig("rope1", 11 * 5)
    logit, relu, score = sig("logit_ps", 12), sig("relu", 12, LEAD), sig("idx_score", 12, LEAD)
    cut = sig("idx_masked", 3)
    ROUNDS = TOPK // 8
    topk = sig("topk_steps", 3 * 2 * ROUNDS, LEAD)
    bias_s = sig("bias_ready", 4)
    v_hi_s, v_lo_s = sig("v_hi", T), sig("v_lo", T)
    glu, conv1 = sig("glu", 3), sig("conv1", 2 * CONVW)
    ln_mean, ln_dev, ln_sq = sig("ln_mean", 1), sig("ln_dev", 2), sig("ln_sq", 2)
    ln_var, ln_inv, ln_rstd = sig("ln_var_ps", 1), sig("ln_inv", 5), sig("ln_rstd", 1)
    ln_y, ya = sig("ln_y", 2), sig("ya", 2)
    scin, scconv, yb_s = sig("sc_in", 2), sig("sc_conv", 6), sig("yb", 2)
    yab_hi, yab_lo = sig("yab_hi", 4), sig("yab_lo", 4)
    out1_x = sig("out1_x", KD, LEAD)
    mscaled, mhi, mlo = sig("mem_scaled", KD), sig("mem_hi", KD, LEAD), sig("mem_lo", KD, LEAD)
    kv_hi, kv_lo = sig("kv_hi", 12), sig("kv_lo", 12, LEAD)
    qx_hi_s, qx_lo_s = sig("qx_hi", KD), sig("qx_lo", KD, LEAD)
    wo_x = sig("wo_x", KD, LEAD)
    z_ev = sig("z_evicted", 15, LEAD)
    vz_ev = sig("vz_evicted", T)
    rswap_s, krswap_s, qrswap_s = sig("rswap", 16 * 8), sig("krswap", 64), [sig(f"qrswap{j}", 64) for j in range(2)]
    rrope = sig("rrope", 6)
    krrope, qrrope = sig("krrope", 5), sig("qrrope", 8)
    gk_ps = sig("gk_ps", 1)
    gk_dve, gk_act = sig("gk_dve", 4), sig("gk_act", 2)
    ret_ps, ret_at = sig("ret_ps", len(BLOCKS)), sig("ret_at", len(BLOCKS), LEAD)
    ret_out, ret_y = sig("ret_out", MH), sig("ret_y", MH)
    lev_d, lev_e, lev_q = sig("lev_d", 15), sig("lev_e", 9), sig("lev_q", 2 * 9, 2 * LEAD)
    zero_at = sig("zero_at", 1)
    lev_ps, lev_at = sig("lev_ps", LEVELS * T), sig("lev_at", LEVELS * T, LEAD)
    etot_s, k3_s = sig("etot", 1), sig("k3", 3)
    far_ps, far_at = sig("far_ps", 6), sig("far_at", 6, LEAD)
    gla_out, gla_y = sig("gla_out", MH), sig("gla_y", MH)
    u_hi, u_lo = sig("u_hi", 14), sig("u_lo", 14, LEAD)
    hs_sq, hs_tot = sig("hs_sq", KD), sig("hs_tot", KD, LEAD)
    hs_var, hs_inv, hs_rstd = sig("hs_var", 2), sig("hs_inv", 4), sig("hs_rstd", 1)
    hs_dg, hs_bc = sig("hs_dg", KD), sig("hs_bc", KD, LEAD)
    hs_n, hs_g = sig("hs_n", KD, LEAD), sig("hs_g", 4)
    hs_hi, hs_lo = sig("hs_hi", KD, LEAD), sig("hs_lo", KD)
    out2_x = sig("out2_x", KD, LEAD)

    def par1_at(group, k):
        return p1[:, group * KD + k:group * KD + k + 1]

    CW0 = 5 * KD
    CB0, LG0, LB0, SC0 = CW0 + 2 * CONVW, CW0 + 2 * CONVW + 2, CW0 + 2 * CONVW + 4, CW0 + 2 * CONVW + 6
    FIN1 = SC0 + 6
    QN0, KN0, MO0, GB0, GO0, RO0, FN0 = KD, KD + 3, KD + 5, KD + 9, KD + 10, KD + 12, KD + 14
    FIN2 = FN0 + KD

    def f32(ap):
        return ap.bitcast(F32)

    def mm3(pe, out, w_hi, w_lo, m_hi, m_lo, start, stop):
        pe.matmul(out, w_hi, m_hi, start=start, stop=False, skip_group_check=True)
        pe.matmul(out, w_hi, m_lo, start=False, stop=False, skip_group_check=True)
        return pe.matmul(out, w_lo, m_hi, start=False, stop=stop, skip_group_check=True)

    def gate(v, cell):
        v.memset(gate_cells[:, cell:cell + 1], 0.0)

    def load(sp, ch, src, width):
        sp.wait_ge(Ring.split, ch.n + 1)
        sp.dma_start(raw[:, ch.slot, 0:width], src).then_inc(Ring.raw_in[ch.slot], 16)

    def split(g, ch, src, width):
        g.wait_ge(Ring.raw_in[ch.slot], ch.half * 16 + 16)
        g.wait_ge(Ring.done, ch.n + 1)
        g.tensor_tensor(wh[:, ch.slot, 0:width], raw[:, ch.slot, 0:width], one[:, 0:1].to_broadcast([P, width]),
                        ALU.mult).then_inc(Ring.hi, 1)
        g.wait_ge(Ring.hi, ch.n + 1)
        g.tensor_tensor(wl[:, ch.slot, 0:width], raw[:, ch.slot, 0:width], f32(wh[:, ch.slot, 0:width]),
                        ALU.subtract).then_inc(Ring.split, 1)

    def stack1_chunks(eng, l, visit):
        def at(c, i=0):
            return Chunk(0, C1, l, c, i)

        def ffn(c, gu, dn):
            with eng.Fori(0, KF) as i:
                for s in range(2):
                    visit(eng, at(c + s, i), gu[l * (2 * KF) + i * 2 + s, :, :], A)
            with eng.Fori(0, KD) as i:
                for s in range(2):
                    visit(eng, at(c + 2 * KF + s, i), dn[l * 16 + i * 2 + s, :, :], DN)

        ffn(0, gu1, dn1)
        visit(eng, at(60), widx[l, :, :], 4 * KD)
        visit(eng, at(61), mid[l * MIX1_CHUNKS, :, :], A)
        with eng.Fori(0, MIX1_CHUNKS // 2) as i:
            for s in range(2):
                visit(eng, at(62 + s, i), mid[l * MIX1_CHUNKS + i * 2 + (1 + s), :, :], A)
        ffn(61 + MIX1_CHUNKS, gu2, dn2)

    def stack2_chunks(eng, l, visit):
        def at(c, i=0):
            return Chunk(L * C1, C2, l, c, i)

        with eng.Fori(0, MIX2_CHUNKS // 2) as i:
            for s in range(2):
                visit(eng, at(s, i), mix2[l * MIX2_CHUNKS + i * 2 + s, :, :], A)
        with eng.Fori(0, KF) as i:
            for s in range(2):
                visit(eng, at(MIX2_CHUNKS + s, i), up2[l * (2 * KF) + i * 2 + s, :, :], A)
        with eng.Fori(0, KD) as i:
            for s in range(2):
                visit(eng, at(MIX2_CHUNKS + 2 * KF + s, i), dn3[l * 16 + i * 2 + s, :, :], DN)

    def swap_halves(act, dst, src, half, sem):
        for b in range(0, P, 2 * half):
            act.dma_start(dst[b:b + half], src[b + half:b + 2 * half]).then_inc(sem, 16)
            act.dma_start(dst[b + half:b + 2 * half], src[b:b + half]).then_inc(sem, 16)

    def norm_act_squares(act, n, l, src, ready, width=S):
        for k in range(n.k):
            ready(act, k)
            act.wait_ge(n.sum.sem, n.sum(l, max(k - 1, 0)))
            act.activation(sq[:, k % 2, 0:width], src(k), ACT.Square).then_inc(n.sq.sem, 1)

    def norm_act_root(act, n, l):
        act.wait_ge(n.inv.sem, n.inv(l, 2))
        act.activation(st[:, 2, 0:n.tiles], st[:, 1, 0:n.tiles], ACT.Sqrt).then_inc(n.rstd.sem, 1)

    def norm_act_hi(act, n, l, hi_dst, width=S):
        for k in range(n.k):
            act.wait_ge(n.scaled.sem, n.scaled(l, k + 1))
            act.activation(hi_dst(k), hf[:, k % 2, 0:width], ACT.Copy).then_inc(n.hi.sem, 1)

    def norm_dve_sum(v, n, l, width=S):
        for k in range(n.k):
            v.wait_ge(n.sq.sem, n.sq(l, k + 1))
            if k == 0:
                v.tensor_scalar(ssum[:, 0:width], sq[:, 0, 0:width], 1.0, None, ALU.mult).then_inc(n.sum.sem, 1)
            else:
                v.wait_ge(n.sum.sem, n.sum(l, k))
                v.tensor_tensor(ssum[:, 0:width], ssum[:, 0:width], sq[:, k % 2, 0:width], ALU.add)\
                    .then_inc(n.sum.sem, 1)

    def norm_dve_inverse(v, n, l):
        v.wait_ge(n.spread.sem, n.spread(l, 1))
        v.tensor_scalar(st[:, 0, 0:n.tiles], bank[6][:, 0:n.tiles], 1.0 / (n.k * P), 1e-6, ALU.mult, ALU.add)\
            .then_inc(n.inv.sem, 1)
        v.wait_ge(n.inv.sem, n.inv(l, 1))
        v.reciprocal(st[:, 1, 0:n.tiles], st[:, 0, 0:n.tiles]).then_inc(n.inv.sem, 1)

    def refine_root(v, root, square, tmp, sem, done):
        v.tensor_tensor(tmp, root, root, ALU.mult).then_inc(sem, 1)
        v.wait_ge(sem, done + 1)
        v.scalar_tensor_tensor(tmp, tmp, -0.5, square, ALU.mult, ALU.mult).then_inc(sem, 1)
        v.wait_ge(sem, done + 2)
        v.scalar_tensor_tensor(root, tmp, 1.5, root, ALU.add, ALU.mult).then_inc(sem, 1)
        v.wait_ge(sem, done + 3)

    def norm_dve_diagonals(v, n, l):
        v.wait_ge(n.rstd.sem, n.rstd(l, 1))
        refine_root(v, st[:, 2, 0:n.tiles], st[:, 0, 0:n.tiles], st[:, 1, 0:n.tiles], n.inv.sem, n.inv(l, 2))
        for t in range(n.tiles):
            last = v.tensor_scalar(dg[:, 0, t, :], ident[:, :], st[:, 2, t:t + 1], None, ALU.mult)
        last.then_inc(n.dg.sem, 1)

    def norm_dve_scale(v, n, l, src, gain, hi_dst, lo_dst, plain_dst=None, width=S):
        v.wait_ge(n.spread.sem, n.spread(l, 2))

        def lo(k):
            v.wait_ge(n.hi.sem, n.hi(l, k + 1))
            v.tensor_tensor(lo_dst(k), hf[:, k % 2, 0:width], f32(hi_dst(k)), ALU.subtract).then_inc(n.lo.sem, 1)

        for k in range(n.k):
            if plain_dst is None:
                v.wait_ge(n.lo.sem, n.lo(l, max(k - 1, 0)))
            out = hf[:, k % 2, 0:width] if plain_dst is None else plain_dst(k)
            if gain is None:
                v.tensor_tensor(out, src(k), bank[7][:, 0:width], ALU.mult).then_inc(n.scaled.sem, 1)
            else:
                v.scalar_tensor_tensor(out, src(k), gain(k), bank[7][:, 0:width], ALU.mult, ALU.mult)\
                    .then_inc(n.scaled.sem, 1)
            if plain_dst is None and k >= 1:
                lo(k - 1)
        if plain_dst is None:
            lo(n.k - 1)

    def norm_pe_totals(pe, n, l):
        pe.wait_ge(n.sum.sem, n.sum(l, n.k))
        for t in range(n.tiles):
            mm = pe.matmul(bank[6][:, t:t + 1], ssum[:, t * P:(t + 1) * P], ones[:, 0:1], start=True, stop=True)
        mm.then_inc(n.spread.sem, 1)

    def norm_pe_spread(pe, n, l):
        pe.wait_ge(n.dg.sem, n.dg(l, 1))
        for t in range(n.tiles):
            mm = pe.matmul(bank[7][:, t * P:(t + 1) * P], ones[:, :], dg[:, 0, t, :], start=True, stop=True)
        mm.then_inc(n.spread.sem, 1)

    def norm_act(act, n, l, src, ready, hi_dst=None, width=S):
        norm_act_squares(act, n, l, src, ready, width)
        norm_act_root(act, n, l)
        if hi_dst is not None:
            norm_act_hi(act, n, l, hi_dst, width)

    def norm_dve(v, n, l, src, gain, hi_dst=None, lo_dst=None, plain_dst=None, width=S):
        norm_dve_sum(v, n, l, width)
        norm_dve_inverse(v, n, l)
        norm_dve_diagonals(v, n, l)
        norm_dve_scale(v, n, l, src, gain, hi_dst, lo_dst, plain_dst, width)

    def norm_pe(pe, n, l):
        norm_pe_totals(pe, n, l)
        norm_pe_spread(pe, n, l)

    def x_tile(k):
        return x[:, k, :]

    def hh_tile(k):
        return hh[:, k, :]

    def hl_tile(k):
        return hl[:, k, :]

    def column_tile(pe, ch, out, k_tiles, m_hi, m_lo, first=0, ready=None):
        for k in range(k_tiles):
            if ready is not None:
                ready(k)
            b = (first + k) * P
            mm = mm3(pe, out, wh[:, ch.slot, b:b + P], wl[:, ch.slot, b:b + P], m_hi(k), m_lo(k),
                     k == 0, k == k_tiles - 1)
        return mm

    def landed(pe, ch):
        pe.wait_ge(Ring.split, ch.n + 1 + LEAD)

    def products_done(eng, ch):
        eng.wait_ge(Ring.done, ch.n + 1 + LEAD)

    def ffn_pe(pe, f, l, at):
        norm_pe(pe, f.norm, l)
        with pe.Fori(0, KF // 2) as i:
            for s in range(2):
                for part, ps, freed in ((0, 0, f.silu), (1, 2, f.act)):
                    ch = at(part, i * 2 + s)
                    landed(pe, ch)
                    pe.wait_ge(freed.sem, freed(l, i * 2 + (s - 1)))
                    column_tile(pe, ch, bank[ps + s][:, :], KD, hh_tile, hl_tile,
                                ready=lambda k: pe.wait_ge(f.norm.lo.sem, f.norm.lo(l, k + 1)))\
                        .then_inc(Ring.done, 1)
        with pe.Fori(0, KD // 2) as i:
            for s in range(2):
                pe.wait_ge(f.x.sem, f.x(l, i * 2 + (s - 1)))
                for half in range(2):
                    ch = at(2 * KF + half, i * 2 + s)
                    landed(pe, ch)
                    pe.wait_ge(f.act_lo.sem, f.act_lo(l, KH * (half + 1)))
                    for k in range(KH):
                        mm = mm3(pe, bank[4 + s][:, :], wh[:, ch.slot, k * P:(k + 1) * P],
                                 wl[:, ch.slot, k * P:(k + 1) * P], ah[:, KH * half + k, :], al[:, KH * half + k, :],
                                 half == 0 and k == 0, half == 1 and k == KH - 1)
                    mm.then_inc(Ring.done, 1)

    def ffn_act(act, f, l, at, ready, conv):
        norm_act(act, f.norm, l, x_tile, ready, hh_tile)
        with act.Fori(0, KF // 2) as i:
            for s in range(2):
                tile = i * 2 + s
                if conv:
                    products_done(act, at(0, tile))
                    act.wait_ge(f.act.sem, f.act(l, i * 2 + (s - 1)))
                    act.activation(cv[:, s, 0:S], bank[s][:, :], ACT.Identity, bias=cpar[:, bass.ds(tile, 1), 3],
                                   scale=cpar[:, bass.ds(tile, 1), 2]).then_inc(f.conv.sem, 1)
                    act.wait_ge(f.conv.sem, f.conv(l, tile * 3 + 3))
                    act.activation(sg[:, s, :], cv[:, s, 0:S], ACT.Silu).then_inc(f.silu.sem, 1)
                else:
                    products_done(act, at(0, tile))
                    act.wait_ge(f.act.sem, f.act(l, i * 2 + (s - 1)))
                    act.activation(sg[:, s, :], bank[s][:, :], ACT.Silu).then_inc(f.silu.sem, 1)
                act.wait_ge(f.act.sem, f.act(l, tile + 1))
                act.activation(ah[:, bass.ds(tile, 1), :], af[:, s, :], ACT.Copy).then_inc(f.act_hi.sem, 1)

    def ffn_dve(v, f, l, at, gain, conv, half):
        norm_dve(v, f.norm, l, x_tile, gain, hh_tile, hl_tile)
        with v.Fori(0, KF // 2) as i:
            for s in range(2):
                tile = i * 2 + s
                if conv:
                    for lag in (1, 2):
                        v.wait_ge(f.conv.sem, f.conv(l, tile * 3 + lag))
                        v.scalar_tensor_tensor(cv[:, s, lag:S], bank[s][:, 0:S - lag],
                                               cpar[:, bass.ds(tile, 1), 2 - lag], cv[:, s, lag:S],
                                               ALU.mult, ALU.add).then_inc(f.conv.sem, 1)
                products_done(v, at(1, tile))
                v.wait_ge(f.silu.sem, f.silu(l, tile + 1))
                v.wait_ge(f.act_hi.sem, f.act_hi(l, i * 2 + (s - 1)))
                v.tensor_tensor(af[:, s, :], sg[:, s, :], bank[2 + s][:, :], ALU.mult).then_inc(f.act.sem, 1)
                v.wait_ge(f.act_hi.sem, f.act_hi(l, tile + 1))
                v.tensor_tensor(al[:, bass.ds(tile, 1), :], af[:, s, :], f32(ah[:, bass.ds(tile, 1), :]),
                                ALU.subtract).then_inc(f.act_lo.sem, 1)
        for d in range(KD):
            products_done(v, at(2 * KF + 1, d))
            v.scalar_tensor_tensor(x[:, d, :], bank[4 + d % 2][:, :], half, x[:, d, :], ALU.mult, ALU.add)\
                .then_inc(f.x.sem, 1)

    def attention_pe(pe, a, l, emit_score, freed, probs, key_tiles, emit_out, emptied):
        for s in range(a.items + 2):
            if s < a.items:
                pe.wait_ge(freed.sem, freed(l, s - 1))
                emit_score(s // T, s % T, bank[s % 2]).then_inc(a.score.sem, 1)
            if s >= 5 and s % T == 1:
                h = (s - 5) // T
                pe.wait_ge(a.pt_lo.sem, a.pt_lo(l, T * (h + 1)))
                pe.wait_ge(emptied.sem, emptied(l, a.outs * (h - 1)))
                emit_out(h).then_inc(a.out.sem, 1)
            if 1 <= s <= a.items:
                i = s - 1
                pe.wait_ge(a.prob.sem, a.prob(l, i + 1))
                pe.wait_ge(a.pt_lo.sem, a.pt_lo(l, i - 1))
                for j in range(key_tiles(i % T)):
                    mm = pe.transpose(bank[2 + i % 2][:, j * P:(j + 1) * P], probs[:, i % 2, j * P:(j + 1) * P],
                                      ident[:, :])
                mm.then_inc(a.turn.sem, 1)

    def attention_act(act, a, l, scale, masked, probs, key_tiles, t_hi, emit_y):
        for s in range(a.items + 3):
            if s < a.items:
                n = key_tiles(s % T) * P
                act.wait_ge(a.neg.sem, a.neg(l, s + 1))
                act.wait_ge(a.turn.sem, a.turn(l, s - 1))
                src = probs[:, s % 2, 0:n] if masked else bank[s % 2][:, 0:n]
                act.activation(probs[:, s % 2, 0:n], src, ACT.Exp, bias=small[:, s % 2, 1:2], scale=scale,
                               accum_out=small[:, s % 2, 2:3]).then_inc(a.exp.sem, 1)
            if 1 <= s <= a.items:
                i, t = s - 1, (s - 1) % T
                n = key_tiles(t)
                act.wait_ge(a.out.sem, a.out(l, i // T))
                act.wait_ge(a.turn.sem, a.turn(l, i + 1))
                act.activation(t_hi[:, 0:n, t * P:(t + 1) * P],
                               bank[2 + i % 2][:, 0:n * P].rearrange("p (n q) -> p n q", n=n), ACT.Copy)\
                    .then_inc(a.pt_hi.sem, 1)
            if s >= 6 and (s - 6) % T == 0:
                h = (s - 6) // T
                act.wait_ge(a.out.sem, a.out(l, h + 1))
                emit_y(h)

    def attention_dve(v, a, l, scale, bias_of, probs, key_tiles, t_hi, t_lo, emit_y):
        for s in range(a.items + 4):
            if s < a.items:
                n = key_tiles(s % T) * P
                v.wait_ge(a.turn.sem, a.turn(l, s - 1))
                v.wait_ge(a.score.sem, a.score(l, s + 1))
                gate(v, 2 + s % 2)
                if bias_of is None:
                    v.tensor_reduce(small[:, s % 2, 0:1], bank[s % 2][:, 0:n], AXX, ALU.max).then_inc(a.max.sem, 1)
                else:
                    v.tensor_tensor_reduce(probs[:, s % 2, 0:n], bank[s % 2][:, 0:n], bias_of(s % T), 1.0, TAKEN,
                                           ALU.add, ALU.max, small[:, s % 2, 0:1]).then_inc(a.max.sem, 1)
                v.wait_ge(a.max.sem, a.max(l, s + 1))
                v.tensor_scalar(small[:, s % 2, 1:2], small[:, s % 2, 0:1], -scale, None, ALU.mult)\
                    .then_inc(a.neg.sem, 1)
            if 1 <= s <= a.items:
                i = s - 1
                n = key_tiles(i % T) * P
                v.wait_ge(a.exp.sem, a.exp(l, i + 1))
                v.reciprocal(small[:, i % 2, 3:4], small[:, i % 2, 2:3]).then_inc(a.inv.sem, 1)
                v.wait_ge(a.inv.sem, a.inv(l, i + 1))
                v.tensor_scalar(probs[:, i % 2, 0:n], probs[:, i % 2, 0:n], small[:, i % 2, 3:4], None, ALU.mult)\
                    .then_inc(a.prob.sem, 1)
            if 2 <= s <= a.items + 1:
                i, t = s - 2, (s - 2) % T
                n = key_tiles(t)
                v.wait_ge(a.pt_hi.sem, a.pt_hi(l, i + 1))
                v.tensor_tensor(t_lo[:, 0:n, t * P:(t + 1) * P],
                                bank[2 + i % 2][:, 0:n * P].rearrange("p (n q) -> p n q", n=n),
                                f32(t_hi[:, 0:n, t * P:(t + 1) * P]), ALU.subtract).then_inc(a.pt_lo.sem, 1)
            if emit_y is not None and s >= 7 and (s - 7) % T == 0:
                emit_y((s - 7) // T)

    def causal_tiles(t):
        return t + 1

    def at1(l):
        return lambda c, i=0: Chunk(0, C1, l, c, i)

    def mid_chunk(l, m):
        return Chunk(0, C1, l, 61 + m)

    def tile_chunk(j):
        return j if j < 15 else j + 4

    V_CHUNK, OUT_CHUNK, MEMK_CHUNK, MEMV_CHUNK, XQ_CHUNK, XO_CHUNK = 15, 25, 33, 41, 49, 57
    IDX_SCALE = IDXH ** -0.5 * 64 ** -0.5

    def head_rows(h):
        return slice(64 * (h % 2), 64 * (h % 2) + 64)

    def dsa_bias(t):
        return bias[:, BIAS_AT[t]:BIAS_AT[t] + (t + 1) * P]

    def kv_bank(i):
        return bank[2 + i % 2] if i < 8 else bank[(4, 5, 2, 3)[i - 8]]

    def kv_parts(i):
        if i < 8:
            return km_hi[:, i, :], km_lo[:, i, :], M
        half, mt = (i - 8) // 2, (i - 8) % 2
        return vm_hi[:, mt, half * S:(half + 1) * S], vm_lo[:, mt, half * S:(half + 1) * S], S

    def kv_chunk(l, i):
        return mid_chunk(l, MEMK_CHUNK + i if i < 8 else MEMV_CHUNK + 4 * ((i - 8) // 2) + 3)

    def mix1_pe(pe, l):
        norm_pe(pe, mixnorm, l)

        def tile(j, ready=None):
            ch = mid_chunk(l, tile_chunk(j))
            landed(pe, ch)
            pe.wait_ge(evicted.sem, evicted(l, j - 1))
            column_tile(pe, ch, bank[j % 2][:, :], KD, hh_tile, hl_tile).then_inc(Ring.done, 1)

        ch = at1(l)(60)
        landed(pe, ch)
        for t in range(T):
            for k in range(KD):
                if t == 0:
                    pe.wait_ge(mixnorm.lo.sem, mixnorm.lo(l, k + 1))
                rows = slice(t * P, (t + 1) * P)
                mm = mm3(pe, bank[4][:, 4 * t:4 * t + 4], hh[:, k, rows], hl[:, k, rows],
                         wh[:, ch.slot, 4 * k:4 * k + 4], wl[:, ch.slot, 4 * k:4 * k + 4], k == 0, k == KD - 1)
        mm.then_inc(Ring.done, 1)
        for j in range(7):
            tile(j)
        for i in range(12):
            t, h = 1 + i // IDXH, i % IDXH
            r, q = head_rows(h), slice(t * P, (t + 1) * P)
            n = (t + 1) * P
            pe.wait_ge(rope1.sem, rope1(l, 15))
            pe.wait_ge(relu.sem, relu(l, i - 1))
            mm3(pe, bank[2 + i % 2][:, 0:n], ix_hi[r, h // 2, q], ix_lo[r, h // 2, q], ix_hi[r, 2, 0:n],
                ix_lo[r, 2, 0:n], True, True).then_inc(logit.sem, 1)
        for j in range(7, 15):
            tile(j)
        pe.wait_ge(widx_tok_s.sem, widx_tok_s(l, 1))
        for c in range(4):
            ch = mid_chunk(l, V_CHUNK + c)
            landed(pe, ch)
            for kk in range(2):
                for t in range(T):
                    rows = slice(t * P, (t + 1) * P)
                    mm = mm3(pe, bank[4 + t][:, :], hh[:, 2 * c + kk, rows], hl[:, 2 * c + kk, rows],
                             wh[:, ch.slot, kk * S:(kk + 1) * S], wl[:, ch.slot, kk * S:(kk + 1) * S],
                             c == 0 and kk == 0, c == 3 and kk == 1)
            mm.then_inc(Ring.done, 1)
        for j in range(15, 21):
            tile(j)
        pe.wait_ge(conv1.sem, conv1(l, 2 * CONVW))
        pe.wait_ge(score.sem, score(l, 12))
        for k in range(2):
            mm = pe.matmul(bank[2][:, :], ones[:, :], acc[:, k, :], start=(k == 0), stop=(k == 1))
        mm.then_inc(ln_mean.sem, 1)
        for k in range(2):
            pe.wait_ge(ln_sq.sem, ln_sq(l, k + 1))
            mm = pe.matmul(bank[3][:, :], ones[:, :], sq[:, k, :], start=(k == 0), stop=(k == 1))
        mm.then_inc(ln_var.sem, 1)

        pe.wait_ge(rope1.sem, rope1(l, 55))
        pe.wait_ge(evicted.sem, evicted(l, 21))
        pe.wait_ge(v_lo_s.sem, v_lo_s(l, T))
        pe.wait_ge(ln_inv.sem, ln_inv(l, 2))

        def scores(h, t, out):
            r, q = head_rows(h), slice(t * P, (t + 1) * P)
            n = (t + 1) * P
            return mm3(pe, out[:, 0:n], qk_hi[r, 4 + h // 2, q], qk_lo[r, 4 + h // 2, q], qk_hi[r, h // 2, 0:n],
                       qk_lo[r, h // 2, 0:n], True, True)

        def outputs(h):
            out = bank[4 + h % 2]
            pairs = slice(h // 2 * P, (h // 2 + 1) * P)
            for j in range(T):
                mm = mm3(pe, out[:, j * P:S], v_hi[:, j, pairs], v_lo[:, j, pairs], pt_hi[:, j, j * P:S],
                         pt_lo[:, j, j * P:S], j == 0, j == T - 1)
            return mm

        attention_pe(pe, dsa, l, scores, dsa.max, pbuf, causal_tiles, outputs, dsa.y_lo)

        pe.wait_ge(dsa.y_lo.sem, dsa.y_lo(l, HEADS))
        pe.wait_ge(yab_lo.sem, yab_lo(l, 4))
        for d in range(KD):
            ch = mid_chunk(l, OUT_CHUNK + d)
            landed(pe, ch)
            pe.wait_ge(out1_x.sem, out1_x(l, d - 1))
            column_tile(pe, ch, bank[d % 2][:, :], KD, hh_tile, hl_tile).then_inc(Ring.done, 1)

    def xat_pe(pe, l):
        def mem_key(i):
            ch = kv_chunk(l, i)
            landed(pe, ch)
            pe.wait_ge(mlo.sem, mlo(l, KD))
            pe.wait_ge(kv_lo.sem, kv_lo(l, i - 1))
            column_tile(pe, ch, kv_bank(i)[:, 0:M], KD, lambda k: mh_hi[:, k, :], lambda k: mh_lo[:, k, :])\
                .then_inc(Ring.done, 1)

        for i in range(4):
            mem_key(i)
        norm_pe_totals(pe, xanorm, l)
        for i in range(4, 8):
            mem_key(i)
        norm_pe_spread(pe, xanorm, l)
        for half in range(2):
            if half == 1:
                pe.wait_ge(kv_lo.sem, kv_lo(l, 8))
            for c in range(4):
                ch = mid_chunk(l, MEMV_CHUNK + 4 * half + c)
                landed(pe, ch)
                for kk in range(2):
                    for mt in range(MT):
                        rows = slice(mt * P, (mt + 1) * P)
                        mm = mm3(pe, kv_bank(8 + 2 * half + mt)[:, :], mh_hi[:, 2 * c + kk, rows],
                                 mh_lo[:, 2 * c + kk, rows], wh[:, ch.slot, kk * S:(kk + 1) * S],
                                 wl[:, ch.slot, kk * S:(kk + 1) * S], c == 0 and kk == 0, c == 3 and kk == 1)
                mm.then_inc(Ring.done, 1)
        for d in range(KD):
            ch = mid_chunk(l, XQ_CHUNK + d)
            landed(pe, ch)
            pe.wait_ge(qx_lo_s.sem, qx_lo_s(l, d - 1))
            column_tile(pe, ch, bank[d % 2][:, :], KD, hh_tile, hl_tile,
                        ready=lambda k: pe.wait_ge(xanorm.lo.sem, xanorm.lo(l, k + 1))).then_inc(Ring.done, 1)

        pe.wait_ge(qx_lo_s.sem, qx_lo_s(l, KD))
        pe.wait_ge(kv_lo.sem, kv_lo(l, 12))

        def scores(h, t, out):
            q = slice(t * P, (t + 1) * P)
            for e in range(2):
                mm = mm3(pe, out[:, 0:M], qx_hi[:, 2 * h + e, q], qx_lo[:, 2 * h + e, q], km_hi[:, 2 * h + e, :],
                         km_lo[:, 2 * h + e, :], e == 0, e == 1)
            return mm

        def outputs(h):
            for e in range(2):
                feats = slice((2 * h + e) * P, (2 * h + e + 1) * P)
                for j in range(MT):
                    mm = mm3(pe, bank[4 + 2 * (h % 2) + e][:, :], vm_hi[:, j, feats], vm_lo[:, j, feats],
                             xpt_hi[:, j, :], xpt_lo[:, j, :], j == 0, j == MT - 1)
            return mm

        attention_pe(pe, xat, l, scores, xat.exp, xp, lambda t: MT, outputs, xat.y_lo)
        pe.wait_ge(xat.y_lo.sem, xat.y_lo(l, 2 * XH))
        for d in range(KD):
            ch = mid_chunk(l, XO_CHUNK + d)
            landed(pe, ch)
            pe.wait_ge(wo_x.sem, wo_x(l, d - 1))
            column_tile(pe, ch, bank[d % 2][:, :], KD, hh_tile, hl_tile).then_inc(Ring.done, 1)

    def mix1_act(act, l):
        norm_act(act, mixnorm, l, x_tile, lambda a, k: a.wait_ge(ffn1.x.sem, ffn1.x(l, k + 1)), hh_tile)
        products_done(act, at1(l)(60))
        act.activation(widx_tok[:, :], bank[4][:, 0:16], ACT.Copy, scale=IDX_SCALE).then_inc(widx_tok_s.sem, 1)

        def evict(j):
            products_done(act, mid_chunk(l, tile_chunk(j)))
            if j < 3:
                dst = ix_raw[:, j, :]
            elif j < 11:
                dst = qk_raw[:, j - 3, :]
            else:
                dst = (aval, asig, cgate, bh, bgate)[(j - 11) // 2][:, (j - 11) % 2, :]
            func = ACT.Sigmoid if j in (13, 14) else ACT.Copy
            act.activation(dst, bank[j % 2][:, :], func).then_inc(evicted.sem, 1)
            if j < 11:
                act.wait_ge(evicted.sem, evicted(l, j + 1))
                swapped = ix_swap[:, j, :] if j < 3 else qk_swap[:, j - 3, :]
                swap_halves(act, swapped, dst, 32, swap1[j].sem)

        for j in range(7):
            evict(j)
        for i in range(12):
            n = (2 + i // IDXH) * P
            act.wait_ge(logit.sem, logit(l, i + 1))
            act.wait_ge(score.sem, score(l, i - 1))
            act.activation(rbuf[:, i % 2, 0:n], bank[2 + i % 2][:, 0:n], ACT.Relu).then_inc(relu.sem, 1)
        for j in range(7, 15):
            evict(j)
        products_done(act, mid_chunk(l, V_CHUNK + 3))
        for t in range(T):
            act.activation(v_hi[:, t, :], bank[4 + t][:, :], ACT.Copy).then_inc(v_hi_s.sem, 1)
        for j in range(15, 21):
            evict(j)
        for k in range(2):
            act.wait_ge(yb_s.sem, yb_s(l, k + 1))
            act.activation(hh[:, 2 + k, :], yb[:, k, :], ACT.Copy).then_inc(yab_hi.sem, 1)
        for k in range(2):
            act.wait_ge(ln_dev.sem, ln_dev(l, k + 1))
            act.activation(sq[:, k, :], acc[:, k, :], ACT.Square).then_inc(ln_sq.sem, 1)
        act.wait_ge(ln_inv.sem, ln_inv(l, 2))
        act.activation(aval[:, 0, :], asig[:, 1, :], ACT.Sqrt).then_inc(ln_rstd.sem, 1)
        act.wait_ge(par1_in.sem, par1_in(l, 16))
        for k in range(2):
            act.wait_ge(ln_y.sem, ln_y(l, k + 1))
            act.activation(acc[:, k, :], acc[:, k, :], ACT.Silu, bias=p1[:, LB0 + k:LB0 + k + 1],
                           scale=p1[:, LG0 + k:LG0 + k + 1]).then_inc(ya.sem, 1)
            act.wait_ge(ya.sem, ya(l, k + 1))
            act.activation(hh[:, k, :], acc[:, k, :], ACT.Copy).then_inc(yab_hi.sem, 1)
        act.wait_ge(yab_lo.sem, yab_lo(l, 4))

        def out_hi(h):
            r = head_rows(h)
            act.activation(hh[r, 4 + h // 2, :], bank[4 + h % 2][r, :], ACT.Copy).then_inc(dsa.y_hi.sem, 1)

        attention_act(act, dsa, l, 64 ** -0.5, True, pbuf, causal_tiles, pt_hi, out_hi)

    def xat_act(act, l):
        for k in range(KD):
            act.wait_ge(mscaled.sem, mscaled(l, k + 1))
            act.activation(mh_hi[:, k, :], mf[:, k % 2, :], ACT.Copy).then_inc(mhi.sem, 1)
        norm_act_squares(act, xanorm, l, x_tile, lambda a, k: a.wait_ge(out1_x.sem, out1_x(l, k + 1)))

        def kv(i):
            hi, _, n = kv_parts(i)
            products_done(act, kv_chunk(l, i))
            act.activation(hi, kv_bank(i)[:, 0:n], ACT.Copy).then_inc(kv_hi.sem, 1)

        for i in range(4):
            kv(i)
        norm_act_root(act, xanorm, l)
        for i in range(4, 8):
            kv(i)
        norm_act_hi(act, xanorm, l, hh_tile)
        for i in range(8, 12):
            kv(i)
        for d in range(KD):
            products_done(act, mid_chunk(l, XQ_CHUNK + d))
            act.activation(qx_hi[:, d, :], bank[d % 2][:, :], ACT.Copy).then_inc(qx_hi_s.sem, 1)

        def out_hi(h):
            for e in range(2):
                act.activation(hh[:, 2 * h + e, :], bank[4 + 2 * (h % 2) + e][:, :], ACT.Copy)\
                    .then_inc(xat.y_hi.sem, 1)

        attention_act(act, xat, l, 256 ** -0.5, False, xp, lambda t: MT, xpt_hi, out_hi)

    def rotate(v, raw_tile, swapped, cos, sin, tmp, hi, lo, sem, n, ready):
        v.tensor_tensor(tmp[:, 0, :], raw_tile, cos, ALU.mult).then_inc(sem, 1)
        ready()
        v.tensor_tensor(tmp[:, 1, :], swapped, sin, ALU.mult).then_inc(sem, 1)
        v.wait_ge(sem, n + 2)
        v.tensor_tensor(tmp[:, 2, :], tmp[:, 0, :], tmp[:, 1, :], ALU.add).then_inc(sem, 1)
        v.wait_ge(sem, n + 3)
        v.tensor_scalar(hi, tmp[:, 2, :], 1.0, None, ALU.mult).then_inc(sem, 1)
        v.wait_ge(sem, n + 4)
        return v.tensor_tensor(lo, tmp[:, 2, :], f32(hi), ALU.subtract)

    def mix1_dve(v, l):
        norm_dve(v, mixnorm, l, x_tile, lambda k: par1_at(1, k), hh_tile, hl_tile)
        v.wait_ge(tab_sin, 2)

        def rope(j):
            hi = ix_hi[:, j, :] if j < 3 else qk_hi[:, j - 3, :]
            lo = ix_lo[:, j, :] if j < 3 else qk_lo[:, j - 3, :]
            raw_tile = ix_raw[:, j, :] if j < 3 else qk_raw[:, j - 3, :]
            swapped = ix_swap[:, j, :] if j < 3 else qk_swap[:, j - 3, :]
            v.wait_ge(evicted.sem, evicted(l, j + 1))
            rotate(v, raw_tile, swapped, cos1[:, :], sin1[:, :], rt, hi, lo, rope1.sem,
                   rope1(l, 5 * j), lambda: v.wait_ge(swap1[j].sem, swap1[j](l, 64))).then_inc(rope1.sem, 1)

        for j in range(3):
            rope(j)
        v.wait_ge(widx_tok_s.sem, widx_tok_s(l, 1))
        for i in range(12):
            t, h = 1 + i // IDXH, i % IDXH
            n = (t + 1) * P
            w = widx_tok[:, 4 * t + h:4 * t + h + 1]
            v.wait_ge(relu.sem, relu(l, i + 1))
            if h == 0:
                v.tensor_scalar(dsa_bias(t), rbuf[:, i % 2, 0:n], w, None, ALU.mult).then_inc(score.sem, 1)
            else:
                v.wait_ge(score.sem, score(l, i))
                v.scalar_tensor_tensor(dsa_bias(t), rbuf[:, i % 2, 0:n], w, dsa_bias(t), ALU.mult, ALU.add)\
                    .then_inc(score.sem, 1)
        v.wait_ge(score.sem, score(l, 12))
        for t in range(1, T):
            diag = bias[:, BIAS_AT[t] + t * P:BIAS_AT[t] + (t + 1) * P]
            v.tensor_tensor(diag, diag, causal[:, 3 * P:S], ALU.add).then_inc(cut.sem, 1)
        v.wait_ge(cut.sem, cut(l, 3))
        gate(v, 1)
        for t in range(1, T):
            with v.Fori(0, ROUNDS) as r:
                steps = r * 2 + (t - 1) * 2 * ROUNDS
                v.wait_ge(topk.sem, topk(l, steps))
                gate(v, 0)
                v.max(best[:, :], dsa_bias(t)).then_inc(topk.sem, 1)
                v.wait_ge(topk.sem, topk(l, steps + 1))
                gate(v, 0)
                v.match_replace(dsa_bias(t), best[:, :], dsa_bias(t), TAKEN).then_inc(topk.sem, 1)
        v.tensor_scalar(dsa_bias(0), causal[:, 3 * P:S], 1.0, None, ALU.mult).then_inc(bias_s.sem, 1)
        v.wait_ge(topk.sem, topk(l, 3 * 2 * ROUNDS))
        for t in range(1, T):
            v.tensor_scalar(dsa_bias(t), dsa_bias(t), TAKEN_BELOW, MASKED, ALU.is_gt, ALU.mult)\
                .then_inc(bias_s.sem, 1)
        for j in range(3, 11):
            rope(j)
        for t in range(T):
            v.wait_ge(v_hi_s.sem, v_hi_s(l, t + 1))
            v.tensor_tensor(v_lo[:, t, :], bank[4 + t][:, :], f32(v_hi[:, t, :]), ALU.subtract)\
                .then_inc(v_lo_s.sem, 1)
        v.memset(xpad[:, :, 0:CONVW - 1], 0.0).then_inc(glu.sem, 1)
        v.wait_ge(evicted.sem, evicted(l, 15))
        for k in range(2):
            v.tensor_tensor(xpad[:, k, CONVW - 1:], aval[:, k, :], asig[:, k, :], ALU.mult).then_inc(glu.sem, 1)
        v.wait_ge(glu.sem, glu(l, 3))
        for j in range(CONVW):
            for k in range(2):
                w = p1[:, CW0 + 2 * j + k:CW0 + 2 * j + k + 1]
                if j == 0:
                    v.tensor_scalar(acc[:, k, :], xpad[:, k, 0:S], w, p1[:, CB0 + k:CB0 + k + 1], ALU.mult, ALU.add)\
                        .then_inc(conv1.sem, 1)
                else:
                    v.wait_ge(conv1.sem, conv1(l, 2 * j + k - 1))
                    v.scalar_tensor_tensor(acc[:, k, :], xpad[:, k, j:j + S], w, acc[:, k, :], ALU.mult, ALU.add)\
                        .then_inc(conv1.sem, 1)
        v.wait_ge(evicted.sem, evicted(l, 21))
        for k in range(2):
            v.tensor_tensor(cgate[:, k, :], cgate[:, k, :], bh[:, k, :], ALU.mult).then_inc(scin.sem, 1)
        v.wait_ge(scin.sem, scin(l, 2))
        for lag in range(3):
            for k in range(2):
                w = p1[:, SC0 + 2 * (2 - lag) + k:SC0 + 2 * (2 - lag) + k + 1]
                if lag == 0:
                    v.tensor_scalar(yb[:, k, :], cgate[:, k, :], w, None, ALU.mult).then_inc(scconv.sem, 1)
                else:
                    v.wait_ge(scconv.sem, scconv(l, 2 * lag + k - 1))
                    v.scalar_tensor_tensor(yb[:, k, lag:S], cgate[:, k, 0:S - lag], w, yb[:, k, lag:S],
                                           ALU.mult, ALU.add).then_inc(scconv.sem, 1)
        v.wait_ge(scconv.sem, scconv(l, 6))
        for k in range(2):
            v.tensor_tensor(yb[:, k, :], yb[:, k, :], bgate[:, k, :], ALU.mult).then_inc(yb_s.sem, 1)
        for k in range(2):
            v.wait_ge(yab_hi.sem, yab_hi(l, k + 1))
            v.wait_ge(yb_s.sem, yb_s(l, k + 1))
            v.tensor_tensor(hl[:, 2 + k, :], yb[:, k, :], f32(hh[:, 2 + k, :]), ALU.subtract).then_inc(yab_lo.sem, 1)
        v.wait_ge(ln_mean.sem, ln_mean(l, 1))
        v.wait_ge(conv1.sem, conv1(l, 2 * CONVW))
        for k in range(2):
            v.scalar_tensor_tensor(acc[:, k, :], bank[2][:, :], -1.0 / 256, acc[:, k, :], ALU.mult, ALU.add)\
                .then_inc(ln_dev.sem, 1)
        v.wait_ge(ln_var.sem, ln_var(l, 1))
        v.tensor_scalar(asig[:, 0, :], bank[3][:, :], 1.0 / 256, 1e-5, ALU.mult, ALU.add).then_inc(ln_inv.sem, 1)
        v.wait_ge(ln_inv.sem, ln_inv(l, 1))
        v.reciprocal(asig[:, 1, :], asig[:, 0, :]).then_inc(ln_inv.sem, 1)
        v.wait_ge(ln_rstd.sem, ln_rstd(l, 1))
        refine_root(v, aval[:, 0, :], asig[:, 0, :], asig[:, 1, :], ln_inv.sem, ln_inv(l, 2))
        for k in range(2):
            v.tensor_tensor(acc[:, k, :], acc[:, k, :], aval[:, 0, :], ALU.mult).then_inc(ln_y.sem, 1)
        for k in range(2):
            v.wait_ge(yab_hi.sem, yab_hi(l, 3 + k))
            v.tensor_tensor(hl[:, k, :], acc[:, k, :], f32(hh[:, k, :]), ALU.subtract).then_inc(yab_lo.sem, 1)
        v.wait_ge(bias_s.sem, bias_s(l, 4))
        v.wait_ge(yab_lo.sem, yab_lo(l, 4))

        def out_lo(h):
            r = head_rows(h)
            v.wait_ge(dsa.y_hi.sem, dsa.y_hi(l, h + 1))
            v.tensor_tensor(hl[r, 4 + h // 2, :], bank[4 + h % 2][r, :], f32(hh[r, 4 + h // 2, :]), ALU.subtract)\
                .then_inc(dsa.y_lo.sem, 1)

        attention_dve(v, dsa, l, 64 ** -0.5, dsa_bias, pbuf, causal_tiles, pt_hi, pt_lo, out_lo)

    def xat_dve(v, l):
        def mem_lo(k):
            v.wait_ge(mhi.sem, mhi(l, k + 1))
            v.tensor_tensor(mh_lo[:, k, :], mf[:, k % 2, :], f32(mh_hi[:, k, :]), ALU.subtract).then_inc(mlo.sem, 1)

        for k in range(KD):
            v.wait_ge(mlo.sem, mlo(l, max(k - 1, 0)))
            v.tensor_scalar(mf[:, k % 2, :], memn[:, k, :], par1_at(3, k), None, ALU.mult).then_inc(mscaled.sem, 1)
            if k >= 1:
                mem_lo(k - 1)
        mem_lo(KD - 1)
        for d in range(KD):
            products_done(v, mid_chunk(l, OUT_CHUNK + d))
            v.tensor_tensor(x[:, d, :], x[:, d, :], bank[d % 2][:, :], ALU.add).then_inc(out1_x.sem, 1)
        norm_dve_sum(v, xanorm, l)

        def kv(i):
            hi, lo, n = kv_parts(i)
            v.wait_ge(kv_hi.sem, kv_hi(l, i + 1))
            v.tensor_tensor(lo, kv_bank(i)[:, 0:n], f32(hi), ALU.subtract).then_inc(kv_lo.sem, 1)

        for i in range(4):
            kv(i)
        norm_dve_inverse(v, xanorm, l)
        norm_dve_diagonals(v, xanorm, l)
        for i in range(4, 8):
            kv(i)
        norm_dve_scale(v, xanorm, l, x_tile, lambda k: par1_at(2, k), hh_tile, hl_tile)
        for i in range(8, 12):
            kv(i)
        for d in range(KD):
            v.wait_ge(qx_hi_s.sem, qx_hi_s(l, d + 1))
            v.tensor_tensor(qx_lo[:, d, :], bank[d % 2][:, :], f32(qx_hi[:, d, :]), ALU.subtract)\
                .then_inc(qx_lo_s.sem, 1)

        def out_lo(h):
            for e in range(2):
                v.wait_ge(xat.y_hi.sem, xat.y_hi(l, 2 * h + e + 1))
                v.tensor_tensor(hl[:, 2 * h + e, :], bank[4 + 2 * (h % 2) + e][:, :], f32(hh[:, 2 * h + e, :]),
                                ALU.subtract).then_inc(xat.y_lo.sem, 1)

        attention_dve(v, xat, l, 256 ** -0.5, None, xp, lambda t: MT, xpt_hi, xpt_lo, out_lo)
        for d in range(KD):
            products_done(v, mid_chunk(l, XO_CHUNK + d))
            v.tensor_tensor(x[:, d, :], x[:, d, :], bank[d % 2][:, :], ALU.add).then_inc(wo_x.sem, 1)

    def mix2_chunk(l, m):
        return Chunk(L * C1, C2, l, m)

    def z_chunk(j):
        return j if j < 11 else j + 4

    VZ_CHUNK, U_CHUNK, OUT2_CHUNK = 11, 19, 24
    U_BANK = (0, 1, 2, 3, 0, 1, 4, 5, 6, 7, 2, 3, 0, 1)
    QK = DK ** -0.5
    FAR = [(0, 1), (1, 2), (2, 3), (0, 2), (1, 3), (0, 3)]

    def u_chunk(l, i):
        return mix2_chunk(l, U_CHUNK + (0, 0, 1, 1, 2, 2, 3, 3, 3, 3, 4, 4, 4, 4)[i])

    def u_parts(i):
        if i < 4:
            return qn_hi[:, i, :], qn_lo[:, i, :]
        if i < 6:
            return qr_hi[:, i - 4, :], qr_lo[:, i - 4, :]
        if i < 10:
            return kn_hi[:, i - 6, :], kn_lo[:, i - 6, :]
        return vm2_hi[:, i - 10, :], vm2_lo[:, i - 10, :]

    def key_rows(h):
        return slice(DK * h, DK * (h + 1))

    def pair_rows(a, h):
        return pair[:, FIRST_BLOCK[a]:FIRST_BLOCK[a] + T - a, h, :]

    def score_banks(n):
        return banks[:, 4 * (n % 2):4 * (n % 2) + MH, 0:P]

    def mix2_pe(pe, l):
        norm_pe(pe, attnorm, l)

        def tile(j):
            ch = mix2_chunk(l, z_chunk(j))
            landed(pe, ch)
            pe.wait_ge(z_ev.sem, z_ev(l, j - 1))
            column_tile(pe, ch, bank[j % 2][:, :], KD, hh_tile, hl_tile,
                        ready=lambda k: pe.wait_ge(attnorm.lo.sem, attnorm.lo(l, k + 1))).then_inc(Ring.done, 1)

        for j in range(6):
            tile(j)
        pe.wait_ge(tables2_in.sem, tables2_in(l, 16 * 8))
        pe.wait_ge(z_ev.sem, z_ev(l, 1))
        pe.matmul(bank[7][:, :], gw[0:16, :], glr[0:16, :], start=True, stop=True).then_inc(gk_ps.sem, 1)
        for j in range(6, 11):
            tile(j)
        for c in range(4):
            ch = mix2_chunk(l, VZ_CHUNK + c)
            landed(pe, ch)
            for kk in range(2):
                for t in range(T):
                    rows = slice(t * P, (t + 1) * P)
                    mm = mm3(pe, bank[2 + t][:, :], hh[:, 2 * c + kk, rows], hl[:, 2 * c + kk, rows],
                             wh[:, ch.slot, kk * S:(kk + 1) * S], wl[:, ch.slot, kk * S:(kk + 1) * S],
                             c == 0 and kk == 0, c == 3 and kk == 1)
            mm.then_inc(Ring.done, 1)
        for j in range(11, 15):
            tile(j)
        pe.wait_ge(gk_dve.sem, gk_dve(l, 1))
        norm_pe(pe, cqnorm, l)
        norm_pe(pe, cknorm, l)

        def key_query(n, k_tile, q_tile):
            for h in range(MH):
                r = key_rows(h)
                mm = pe.matmul(score_banks(n)[:, h, :], k_tile(r), q_tile(r), start=True, stop=True)
            return mm

        def values(v0, done, out_sig):
            for h in range(MH):
                for a in range(T):
                    mm = pe.matmul(bank[4 + h][:, a * P:S], vgr[:, a, v0 + h // 2 * P:v0 + (h // 2 + 1) * P],
                                   pair_rows(a, h), start=(a == 0), stop=(a == T - 1))
                mm.then_inc(out_sig.sem, 1)

        pe.wait_ge(vz_ev.sem, vz_ev(l, T))
        pe.wait_ge(z_ev.sem, z_ev(l, 15))
        pe.wait_ge(cknorm.scaled.sem, cknorm.scaled(l, 2))
        pe.wait_ge(rrope.sem, rrope(l, 6))
        for b, (a, c) in enumerate(BLOCKS):
            pe.wait_ge(ret_at.sem, ret_at(l, b - 1))
            key_query(b, lambda r: rqk[r, 1, a * P:(a + 1) * P], lambda r: rqk[r, 0, c * P:(c + 1) * P])\
                .then_inc(ret_ps.sem, 1)
        pe.wait_ge(ret_at.sem, ret_at(l, len(BLOCKS)))
        values(2 * P, ret_at, ret_out)
        pe.wait_ge(ret_y.sem, ret_y(l, MH))
        for lv in range(LEVELS):
            pe.wait_ge(lev_q.sem, lev_q(l, 2 * (lv + 1)))
            for a in range(T):
                n = lv * T + a
                pe.wait_ge(lev_at.sem, lev_at(l, n - 1))
                rows = slice(a * P, (a + 1) * P)
                key_query(n, lambda r: ke[r, lv % 2, rows], lambda r: qe[r, lv % 2, rows])\
                    .then_inc(lev_ps.sem, 1)
        pe.wait_ge(lev_at.sem, lev_at(l, LEVELS * T))
        pe.wait_ge(lev_q.sem, lev_q(l, 18))
        pe.wait_ge(k3_s.sem, k3_s(l, 3))
        for n, (a, c) in enumerate(FAR):
            pe.wait_ge(far_at.sem, far_at(l, n - 1))
            key = (lambda r: ke[r, 0, a * P:(a + 1) * P]) if c == a + 1 else (lambda r: k3[r, (0, 1, 2)[n - 3], :])
            key_query(n, key, lambda r: qe[r, 0, c * P:(c + 1) * P]).then_inc(far_ps.sem, 1)
        pe.wait_ge(far_at.sem, far_at(l, len(FAR)))
        values(0, far_at, gla_out)
        pe.wait_ge(cqnorm.lo.sem, cqnorm.lo(l, 3))
        for c in range(3):
            ch = mix2_chunk(l, U_CHUNK + c)
            landed(pe, ch)
            if c == 2:
                pe.wait_ge(u_lo.sem, u_lo(l, 2))
            for e in range(2):
                mm = column_tile(pe, ch, bank[U_BANK[2 * c + e]][:, :], 3, lambda k: cq_hi[:, k, :],
                                 lambda k: cq_lo[:, k, :], first=3 * e)
            mm.then_inc(Ring.done, 1)
        pe.wait_ge(cknorm.lo.sem, cknorm.lo(l, 2))
        pe.wait_ge(gla_y.sem, gla_y(l, MH))
        ch = mix2_chunk(l, U_CHUNK + 3)
        landed(pe, ch)
        for e in range(4):
            mm = column_tile(pe, ch, bank[4 + e][:, :], 2, lambda k: ck_hi[:, k, :], lambda k: ck_lo[:, k, :],
                             first=2 * e)
        mm.then_inc(Ring.done, 1)
        ch = mix2_chunk(l, U_CHUNK + 4)
        landed(pe, ch)
        pe.wait_ge(u_lo.sem, u_lo(l, 6))
        for t in range(T):
            rows = slice(t * P, (t + 1) * P)
            for k in range(2):
                mm = mm3(pe, bank[U_BANK[10 + t]][:, :], ck_hi[:, k, rows], ck_lo[:, k, rows],
                         wh[:, ch.slot, k * S:(k + 1) * S], wl[:, ch.slot, k * S:(k + 1) * S], k == 0, k == 1)
        mm.then_inc(Ring.done, 1)

        pe.wait_ge(u_lo.sem, u_lo(l, 14))
        pe.wait_ge(krrope.sem, krrope(l, 5))

        def scores(h, t, out):
            r, q = head_rows(h), slice(t * P, (t + 1) * P)
            n = (t + 1) * P
            mm3(pe, out[:, 0:n], qn_hi[:, h, q], qn_lo[:, h, q], kn_hi[:, h, 0:n], kn_lo[:, h, 0:n], True, False)
            return mm3(pe, out[:, 0:n], qr_hi[r, h // 2, q], qr_lo[r, h // 2, q], kr_hi[r, 0:n], kr_lo[r, 0:n],
                       False, True)

        def outputs(h):
            feats = slice(h * P, (h + 1) * P)
            for j in range(T):
                mm = mm3(pe, bank[4 + h % 2][:, j * P:S], vm2_hi[:, j, feats], vm2_lo[:, j, feats],
                         mpt_hi[:, j, j * P:S], mpt_lo[:, j, j * P:S], j == 0, j == T - 1)
            return mm

        attention_pe(pe, mla, l, scores, mla.max, mp, causal_tiles, outputs, mla.y_hi)
        for k in range(KD):
            pe.wait_ge(hs_sq.sem, hs_sq(l, k + 1))
            for t in range(T):
                rows = slice(t * P, (t + 1) * P)
                if k < 4:
                    mm = pe.matmul(bank[6][:, 4 * k + t:4 * k + t + 1], sq[:, k % 2, rows], ones[:, 0:1],
                                   start=True, stop=True)
                else:
                    c = 16 + 8 * (k - 4) + 2 * t
                    mm = pe.matmul(bank[6][:, c:c + 2], sq[:, k % 2, rows], halfcol[:, :], start=True, stop=True)
            mm.then_inc(hs_tot.sem, 1)
        pe.wait_ge(mla.pt_lo.sem, mla.pt_lo(l, mla.items))
        for k in range(KD):
            pe.wait_ge(hs_dg.sem, hs_dg(l, k + 1))
            pe.wait_ge(hs_n.sem, hs_n(l, k - 1))
            for t in range(T):
                out = bank[2 + k % 2][:, t * P:(t + 1) * P]
                if k < 4:
                    mm = pe.matmul(out, ones[:, :], dg[:, k % 2, t, :], start=True, stop=True)
                else:
                    pe.matmul(out, halves[:, 0, :], dg[:, k % 2, 2 * t, :], start=True, stop=False)
                    mm = pe.matmul(out, halves[:, 1, :], dg[:, k % 2, 2 * t + 1, :], start=False, stop=True)
            mm.then_inc(hs_bc.sem, 1)
        for d in range(KD):
            ch = mix2_chunk(l, OUT2_CHUNK + d)
            landed(pe, ch)
            pe.wait_ge(out2_x.sem, out2_x(l, d - 1))
            column_tile(pe, ch, bank[d % 2][:, :], KD, hh_tile, hl_tile,
                        ready=lambda k: pe.wait_ge(hs_lo.sem, hs_lo(l, k + 1))).then_inc(Ring.done, 1)

    def mix2_act(act, l):
        norm_act(act, attnorm, l, x_tile, lambda a, k: a.wait_ge(ffn3.x.sem, ffn3.x(l, k + 1 - KD)), hh_tile)

        def evict(j):
            products_done(act, mix2_chunk(l, z_chunk(j)))
            dst = (glr[:, :], gqk[:, 0, :], gqk[:, 1, :], rqk[:, 0, :], rqk[:, 1, :], kr_raw[:, :], cq[:, 0, :],
                   cq[:, 1, :], cq[:, 2, :], ckv[:, 0, :], ckv[:, 1, :], gates[:, 0, :], gates[:, 1, :],
                   gates[:, 2, :], gates[:, 3, :])[j]
            act.activation(dst, bank[j % 2][:, :], ACT.Silu if j >= 11 else ACT.Copy).then_inc(z_ev.sem, 1)

        for j in range(6):
            evict(j)
            if j == 4:
                act.wait_ge(z_ev.sem, z_ev(l, 5))
                swap_halves(act, rswap, rqk, DK // 2, rswap_s.sem)
            if j == 5:
                act.wait_ge(z_ev.sem, z_ev(l, 6))
                swap_halves(act, kr_swap, kr_raw, 32, krswap_s.sem)
        for j in range(6, 11):
            evict(j)
        products_done(act, mix2_chunk(l, VZ_CHUNK + 3))
        for t in range(T):
            act.activation(vgr[:, t, :], bank[2 + t][:, :], ACT.Copy).then_inc(vz_ev.sem, 1)
        act.wait_ge(gk_dve.sem, gk_dve(l, 2))
        act.activation(zb[:, 1, :], zb[:, 1, :], ACT.Exp).then_inc(gk_act.sem, 1)
        act.wait_ge(gk_act.sem, gk_act(l, 1))
        act.activation(zb[:, 1, :], zb[:, 1, :], ACT.Ln, bias=one[:, 0:1]).then_inc(gk_act.sem, 1)
        for j in range(11, 15):
            evict(j)
        norm_act(act, cqnorm, l, lambda k: cq[:, k, :], lambda a, k: a.wait_ge(z_ev.sem, z_ev(l, 7 + k)),
                 lambda k: cq_hi[:, k, :])
        norm_act(act, cknorm, l, lambda k: ckv[:, k, :], lambda a, k: a.wait_ge(z_ev.sem, z_ev(l, 10 + k)),
                 lambda k: ck_hi[:, k, :])

        def decay_exp(n):
            if n < 7:
                act.wait_ge(lev_d.sem, lev_d(l, 2 * n + 2))
                src = diff[:, n % 2, :]
            else:
                act.wait_ge(lev_d.sem, lev_d(l, 15))
                src = diff[:, 1, :] if n == 7 else cum[:, :]
            if n >= 2:
                act.wait_ge(lev_q.sem, lev_q(l, 2 * (min(n, 7) - 1)))
            act.activation(edec[:, n % 2, :], src, ACT.Exp, scale=1.0 / 16).then_inc(lev_e.sem, 1)

        def branch_out(h, tile, done, evicted_sig):
            r = head_rows(h)
            act.wait_ge(done.sem, done(l, h + 1))
            act.activation(yf[r, tile + h // 2, :], bank[4 + h][r, :], ACT.Copy).then_inc(evicted_sig.sem, 1)

        decay_exp(0)
        decay_exp(1)
        for h in range(MH):
            branch_out(h, 6, ret_out, ret_y)
        for n in range(2, 9):
            decay_exp(n)
        act.activation(etot[:, :], cum[:, P - 1:S:P], ACT.Exp, scale=1.0 / 16).then_inc(etot_s.sem, 1)
        for n, (a, c) in enumerate(FAR):
            act.wait_ge(far_ps.sem, far_ps(l, n + 1))
            act.activation(pair[:, FIRST_BLOCK[a] + c - a, :, :],
                           score_banks(n), ACT.Copy).then_inc(far_at.sem, 1)
        for h in range(MH):
            branch_out(h, 4, gla_out, gla_y)
        for i in range(14):
            products_done(act, u_chunk(l, i))
            dst = qr_raw[:, i - 4, :] if i in (4, 5) else u_parts(i)[0]
            act.activation(dst, bank[U_BANK[i]][:, :], ACT.Copy).then_inc(u_hi.sem, 1)
            if i in (4, 5):
                act.wait_ge(u_hi.sem, u_hi(l, i + 1))
                swap_halves(act, qr_swap[:, i - 4, :], qr_raw[:, i - 4, :], 32, qrswap_s[i - 4].sem)

        def out_plain(h):
            act.activation(yf[:, h, :], bank[4 + h % 2][:, :], ACT.Copy).then_inc(mla.y_hi.sem, 1)

        attention_act(act, mla, l, (128 + 64) ** -0.5, True, mp, causal_tiles, mpt_hi, out_plain)
        act.wait_ge(mla.y_hi.sem, mla.y_hi(l, MH))
        act.wait_ge(gla_y.sem, gla_y(l, MH))
        act.wait_ge(ret_y.sem, ret_y(l, MH))
        for k in range(KD):
            act.wait_ge(hs_tot.sem, hs_tot(l, k - 1))
            act.activation(sq[:, k % 2, :], yf[:, k, :], ACT.Square).then_inc(hs_sq.sem, 1)
        act.wait_ge(hs_inv.sem, hs_inv(l, 1))
        act.activation(st[:, 2, :], st[:, 1, :], ACT.Sqrt).then_inc(hs_rstd.sem, 1)
        for k in range(KD):
            if k < 4:
                act.wait_ge(hs_n.sem, hs_n(l, k + 1))
            else:
                act.wait_ge(hs_g.sem, hs_g(l, k - 3))
            act.activation(hh[:, k, :], hf[:, k % 2, :], ACT.Copy).then_inc(hs_hi.sem, 1)

    def mix2_dve(v, l):
        norm_dve(v, attnorm, l, x_tile, lambda k: p2[:, k:k + 1], hh_tile, hl_tile)
        v.wait_ge(tables2_in.sem, tables2_in(l, 16 * 8))
        v.wait_ge(gk_ps.sem, gk_ps(l, 1))
        v.tensor_scalar(zb[:, 0, :], bank[7][:, :], p2[:, GB0:GB0 + 1], None, ALU.add).then_inc(gk_dve.sem, 1)
        v.wait_ge(gk_dve.sem, gk_dve(l, 1))
        v.scalar_tensor_tensor(zb[:, 1, :], zb[:, 0, :], -1.0, zb[:, 0, :], ALU.mult, ALU.min)\
            .then_inc(gk_dve.sem, 1)
        v.wait_ge(rswap_s.sem, rswap_s(l, 16 * 8))
        for e in range(2):
            v.wait_ge(z_ev.sem, z_ev(l, 5))
            if e == 1:
                v.wait_ge(rrope.sem, rrope(l, 3))
            v.tensor_tensor(rt[:, 0, :], rqk[:, e, :], rcos[:, :], ALU.mult).then_inc(rrope.sem, 1)
            v.tensor_tensor(rt[:, 1, :], rswap[:, e, :], rsin[:, :], ALU.mult).then_inc(rrope.sem, 1)
            v.wait_ge(rrope.sem, rrope(l, 3 * e + 2))
            v.tensor_tensor(rqk[:, e, :], rt[:, 0, :], rt[:, 1, :], ALU.add).then_inc(rrope.sem, 1)
        v.wait_ge(z_ev.sem, z_ev(l, 6))
        v.wait_ge(rrope.sem, rrope(l, 6))
        rotate(v, kr_raw[:, :], kr_swap[:, :], mcos[:, :], msin[:, :], rt, kr_hi[:, :], kr_lo[:, :], krrope.sem,
               krrope(l, 0), lambda: v.wait_ge(krswap_s.sem, krswap_s(l, 64))).then_inc(krrope.sem, 1)
        v.wait_ge(gk_act.sem, gk_act(l, 2))
        v.scalar_tensor_tensor(zb[:, 0, :], zb[:, 0, :], 0.0, zb[:, 1, :], ALU.min, ALU.subtract)\
            .then_inc(gk_dve.sem, 1)
        v.wait_ge(gk_dve.sem, gk_dve(l, 3))
        v.tensor_tensor_scan(cum[:, :], scanmask[:, :], zb[:, 0, :], 0.0, ALU.mult, ALU.add).then_inc(gk_dve.sem, 1)
        norm_dve(v, cqnorm, l, lambda k: cq[:, k, :], lambda k: p2[:, QN0 + k:QN0 + k + 1],
                 lambda k: cq_hi[:, k, :], lambda k: cq_lo[:, k, :])
        norm_dve(v, cknorm, l, lambda k: ckv[:, k, :], lambda k: p2[:, KN0 + k:KN0 + k + 1],
                 lambda k: ck_hi[:, k, :], lambda k: ck_lo[:, k, :])

        for b, (a, c) in enumerate(BLOCKS):
            v.wait_ge(ret_ps.sem, ret_ps(l, b + 1))
            v.tensor_tensor(pair[:, b, :, :], score_banks(b), decay[:, c - a, :, :], ALU.mult)\
                .then_inc(ret_at.sem, 1)

        def level(lv):
            if lv < 7:
                size = P >> lv
                blocks = cum[:, :].rearrange("p (n b) -> p n b", b=size)
                middle = blocks[:, :, size // 2 - 1:size // 2].to_broadcast([P, S // size, size])
                v.wait_ge(gk_dve.sem, gk_dve(l, 4))
                v.tensor_tensor(diff[:, lv % 2, :].rearrange("p (n b) -> p n b", b=size), blocks, middle,
                                ALU.subtract).then_inc(lev_d.sem, 1)
                v.wait_ge(lev_d.sem, lev_d(l, 2 * lv + 1))
                v.scalar_tensor_tensor(diff[:, lv % 2, :], diff[:, lv % 2, :], -1.0, diff[:, lv % 2, :],
                                       ALU.mult, ALU.min).then_inc(lev_d.sem, 1)

        def level_qk(lv):
            if lv < 7:
                v.wait_ge(lev_e.sem, lev_e(l, lv + 1))
                v.scalar_tensor_tensor(qe[:, lv % 2, :], gqk[:, 0, :], QK, edec[:, lv % 2, :], ALU.mult, ALU.mult)\
                    .then_inc(lev_q.sem, 1)
                v.tensor_tensor(ke[:, lv % 2, :], gqk[:, 1, :], edec[:, lv % 2, :], ALU.mult).then_inc(lev_q.sem, 1)
            else:
                v.tensor_scalar(qe[:, 1, :], gqk[:, 0, :], QK, None, ALU.mult).then_inc(lev_q.sem, 1)
                v.tensor_scalar(ke[:, 1, :], gqk[:, 1, :], 1.0, None, ALU.mult).then_inc(lev_q.sem, 1)

        level(0)
        level(1)
        level_qk(0)
        level_qk(1)
        v.wait_ge(ret_out.sem, ret_out(l, MH))
        for a in range(T):
            last = v.memset(pair[:, FIRST_BLOCK[a], :, :], 0.0)
        last.then_inc(zero_at.sem, 1)
        v.wait_ge(zero_at.sem, zero_at(l, 1))
        for lv in range(LEVELS):
            if lv + 2 < 7:
                level(lv + 2)
            for a in range(T):
                n = lv * T + a
                v.wait_ge(lev_ps.sem, lev_ps(l, n + 1))
                v.wait_ge(lev_at.sem, lev_at(l, n))
                gate(v, 4)
                v.copy_predicated(pair[:, FIRST_BLOCK[a], :, :],
                                  lmask[:, lv:lv + 1, :].to_broadcast([P, MH, P]),
                                  score_banks(n)).then_inc(lev_at.sem, 1)
            if lv + 2 < LEVELS:
                level_qk(lv + 2)
            if lv == 5:
                tiles = cum[:, :].rearrange("p (n b) -> p n b", b=P)
                v.tensor_tensor(diff[:, 1, :].rearrange("p (n b) -> p n b", b=P),
                                tiles[:, :, P - 1:P].to_broadcast([P, T, P]), tiles, ALU.subtract)\
                    .then_inc(lev_d.sem, 1)
        v.wait_ge(lev_e.sem, lev_e(l, 9))
        v.scalar_tensor_tensor(qe[:, 0, :], gqk[:, 0, :], QK, edec[:, 0, :], ALU.mult, ALU.mult).then_inc(lev_q.sem, 1)
        v.tensor_tensor(ke[:, 0, :], gqk[:, 1, :], edec[:, 1, :], ALU.mult).then_inc(lev_q.sem, 1)
        v.wait_ge(etot_s.sem, etot_s(l, 1))
        v.wait_ge(lev_q.sem, lev_q(l, 18))
        v.tensor_scalar(k3[:, 0, :], ke[:, 0, 0:P], etot[:, 1:2], None, ALU.mult).then_inc(k3_s.sem, 1)
        v.tensor_scalar(k3[:, 1, :], ke[:, 0, P:2 * P], etot[:, 2:3], None, ALU.mult).then_inc(k3_s.sem, 1)
        v.wait_ge(k3_s.sem, k3_s(l, 1))
        v.tensor_scalar(k3[:, 2, :], k3[:, 0, :], etot[:, 2:3], None, ALU.mult).then_inc(k3_s.sem, 1)
        for i in range(14):
            hi, lo = u_parts(i)
            v.wait_ge(u_hi.sem, u_hi(l, i + 1))
            if i in (4, 5):
                e = i - 4
                rotate(v, qr_raw[:, e, :], qr_swap[:, e, :], mcos[:, :], msin[:, :], rt, hi, lo, qrrope.sem,
                       qrrope(l, 4 * e), lambda: v.wait_ge(qrswap_s[e].sem, qrswap_s[e](l, 64)))\
                    .then_inc(u_lo.sem, 1)
            else:
                v.tensor_tensor(lo, bank[U_BANK[i]][:, :], f32(hi), ALU.subtract).then_inc(u_lo.sem, 1)

        attention_dve(v, mla, l, (128 + 64) ** -0.5, lambda t: causal[:, (3 - t) * P:S], mp, causal_tiles, mpt_hi,
                      mpt_lo, None)
        v.wait_ge(hs_tot.sem, hs_tot(l, KD))
        v.tensor_scalar(st[:, 0, 0:16], bank[6][:, 0:16], 1.0 / 128, 1e-6, ALU.mult, ALU.add).then_inc(hs_var.sem, 1)
        v.tensor_scalar(st[:, 0, 16:48], bank[6][:, 16:48], 1.0 / 64, 1e-6, ALU.mult, ALU.add).then_inc(hs_var.sem, 1)
        v.wait_ge(hs_var.sem, hs_var(l, 2))
        v.reciprocal(st[:, 1, :], st[:, 0, :]).then_inc(hs_inv.sem, 1)
        v.wait_ge(hs_rstd.sem, hs_rstd(l, 1))
        refine_root(v, st[:, 2, :], st[:, 0, :], st[:, 1, :], hs_inv.sem, hs_inv(l, 1))

        def diagonals(k):
            v.wait_ge(hs_bc.sem, hs_bc(l, k - 1))
            for e in range(4 if k < 4 else 8):
                c = 4 * k + e if k < 4 else 16 + 8 * (k - 4) + e
                last = v.tensor_scalar(dg[:, k % 2, e, :], ident[:, :], st[:, 2, c:c + 1], None, ALU.mult)
            last.then_inc(hs_dg.sem, 1)

        def out_gain(k):
            return MO0 + k if k < 4 else GO0 + k - 4

        diagonals(0)
        for k in range(KD):
            if k + 1 < KD:
                diagonals(k + 1)
            gain = p2[:, out_gain(k):out_gain(k) + 1]
            v.wait_ge(hs_bc.sem, hs_bc(l, k + 1))
            v.wait_ge(hs_hi.sem, hs_hi(l, k - 1))
            v.scalar_tensor_tensor(hf[:, k % 2, :], yf[:, k, :], gain, bank[2 + k % 2][:, :], ALU.mult, ALU.mult)\
                .then_inc(hs_n.sem, 1)
            v.wait_ge(hs_n.sem, hs_n(l, k + 1))
            if k >= 4:
                v.tensor_tensor(hf[:, k % 2, :], hf[:, k % 2, :], gates[:, k - 4, :], ALU.mult).then_inc(hs_g.sem, 1)
                v.wait_ge(hs_g.sem, hs_g(l, k - 3))
            v.wait_ge(hs_hi.sem, hs_hi(l, k + 1))
            v.tensor_tensor(hl[:, k, :], hf[:, k % 2, :], f32(hh[:, k, :]), ALU.subtract).then_inc(hs_lo.sem, 1)
        for d in range(KD):
            products_done(v, mix2_chunk(l, OUT2_CHUNK + d))
            v.tensor_tensor(x[:, d, :], x[:, d, :], bank[d % 2][:, :], ALU.add).then_inc(out2_x.sem, 1)

    def ffn1_at(l):
        return lambda c, i=0: Chunk(0, C1, l, c, i)

    def ffn2_at(l):
        return lambda c, i=0: Chunk(0, C1, l, 61 + MIX1_CHUNKS + c, i)

    def ffn3_at(l):
        return lambda c, i=0: Chunk(L * C1, C2, l, MIX2_CHUNKS + c, i)

    CONST_LOADS = 7
    with nc.Block() as block:

        @block.sync
        def _(sp):
            sp.dma_start(x[:, :, :], x_in).then_inc(x_in_sem, 16)
            sp.dma_start(memn[:, :, :], mem_in).then_inc(x_in_sem, 16)
            for dst, c0, c1 in ((ident[:, :], *CONST["ident"]), (causal[:, :], *CONST["causal"]),
                                (halfcol[:, :], *CONST["halfcol"]), (cols[:, :], *CONST["cols"])):
                sp.dma_start(dst, consts[:, c0:c1]).then_inc(consts_in, 16)
            for e in range(2):
                c0 = CONST["halves"][0] + e * P
                sp.dma_start(halves[:, e, :], consts[:, c0:c0 + P]).then_inc(consts_in, 16)
            sp.dma_start(rt[:, 1, :].bitcast(I32), pos_in.partition_broadcast(P)).then_inc(consts_in, 16)
            sp.wait_ge(led, len(leads))
            with sp.Fori(0, L) as l:
                sp.wait_ge(ffn1.norm.hi.sem, ffn1.norm.hi(l, 0))
                sp.dma_start(p1[:, :], par1[l, :, :]).then_inc(par1_in.sem, 16)
                stack1_chunks(sp, l, load)
            with sp.Fori(0, L) as l:
                sp.wait_ge(finalnorm.scaled.sem, finalnorm.scaled(0, KD))
                sp.wait_ge(ffn3.x.sem, ffn3.x(l, 0))
                sp.dma_start(p2[:, :], par2[l, :, :]).then_inc(par2_in.sem, 16)
                sp.dma_start(cpar[:, :, :], convpar[l, :, :, :]).then_inc(cpar_in.sem, 16)
                for dst, name in ((mcos[:, :], "mcos"), (msin[:, :], "msin"), (rcos[:, :], "rcos"),
                                  (rsin[:, :], "rsin"), (scanmask[:, :], "scanmask")):
                    sp.dma_start(dst, consts[:, CONST[name][0]:CONST[name][1]]).then_inc(tables2_in.sem, 16)
                sp.dma_start(decay[:, :, :, :].rearrange("p d h q -> p (d h q)"),
                             consts[:, CONST["decay"][0]:CONST["decay"][1]]).then_inc(tables2_in.sem, 16)
                sp.dma_start(lmask[:, :, :].rearrange("p v q -> p (v q)").bitcast(I32), masks).then_inc(tables2_in.sem, 16)
                sp.dma_start(gw[0:16, :], gate_w[l, :, :]).then_inc(tables2_in.sem, 16)
                stack2_chunks(sp, l, load)
            for k in range(KD):
                sp.wait_ge(endnorm.scaled.sem, endnorm.scaled(0, k + 1))
                sp.dma_start(y_out[:, k, :], x[:, k, :]).then_inc(y_stored, 16)
            sp.wait_ge(y_stored, 16 * KD)

        @block.gpsimd
        def _(g):
            g.memset(one[:, :], 1.0).then_inc(setup, 1)
            for sem, lead in leads:
                g.sem_inc(sem, lead)
                g.sem_inc(led, 1)
            g.wait_ge(setup, 2)
            with g.Fori(0, L) as l:
                stack1_chunks(g, l, split)
            with g.Fori(0, L) as l:
                stack2_chunks(g, l, split)

        @block.scalar
        def _(act):
            act.wait_ge(led, len(leads))
            act.wait_ge(x_in_sem, 32)
            norm_act(act, memnorm, 0, lambda k: memn[:, k, :], lambda a, k: None, width=M)
            for e in range(2):
                act.wait_ge(tab, 17)
                act.activation((cos1, sin1)[e][:, :], rt[:, 2, :] if e == 0 else rbuf[:, 0, :], ACT.Sin)\
                    .then_inc(tab_sin, 1)
            with act.Fori(0, L) as l:
                ffn_act(act, ffn1, l, ffn1_at(l), lambda a, k: a.wait_ge(ffn2.x.sem, ffn2.x(l, k + 1 - KD)), False)
                mix1_act(act, l)
                xat_act(act, l)
                ffn_act(act, ffn2, l, ffn2_at(l), lambda a, k: a.wait_ge(wo_x.sem, wo_x(l, k + 1)), False)
            norm_act(act, finalnorm, 0, x_tile, lambda a, k: a.wait_ge(ffn2.x.sem, ffn2.x(L - 1, k + 1)))
            act.wait_ge(finalnorm.scaled.sem, finalnorm.scaled(0, KD))
            with act.Fori(0, L) as l:
                act.wait_ge(cpar_in.sem, cpar_in(l, 16))
                mix2_act(act, l)
                ffn_act(act, ffn3, l, ffn3_at(l), lambda a, k: a.wait_ge(out2_x.sem, out2_x(l, k + 1)), True)
            norm_act(act, endnorm, 0, x_tile, lambda a, k: a.wait_ge(ffn3.x.sem, ffn3.x(L - 1, k + 1)))

        @block.vector
        def _(v):
            v.memset(ones[:, :], 1.0).then_inc(setup, 1)
            v.wait_ge(led, len(leads))
            v.wait_ge(consts_in, 16 * CONST_LOADS)
            v.wait_ge(x_in_sem, 32)
            norm_dve(v, memnorm, 0, lambda k: memn[:, k, :], None, plain_dst=lambda k: memn[:, k, :], width=M)
            steps = [0]

            def step(ins):
                steps[0] += 1
                ins.then_inc(tab, 1)
                v.wait_ge(tab, steps[0])

            pos, ang, turns = rt[:, 0, :], rt[:, 2, :], rbuf[:, 0, :]
            step(v.tensor_copy(pos, rt[:, 1, :].bitcast(I32)))
            step(v.tensor_scalar(ang, pos, cols[:, 0:1], None, ALU.mult))
            step(v.tensor_scalar(turns, ang, 1.0 / (2 * PI), ROUND, ALU.mult, ALU.add))
            step(v.tensor_scalar(turns, turns, -ROUND, None, ALU.add))
            for part in TWO_PI_PARTS:
                step(v.scalar_tensor_tensor(ang, turns, -part, ang, ALU.mult, ALU.add))
            over = rbuf[:, 1, :]
            step(v.tensor_scalar(over, ang, PI / 2, -2 * PI, ALU.is_gt, ALU.mult))
            step(v.tensor_scalar(turns, ang, PI, -PI, ALU.min, ALU.max))
            step(v.tensor_scalar(turns, turns, cols[:, 1:2], None, ALU.mult))
            step(v.tensor_scalar(ang, ang, PI / 2, None, ALU.add))
            step(v.tensor_tensor(ang, ang, over, ALU.add))
            step(v.tensor_scalar(ang, ang, PI, -PI, ALU.min, ALU.max))
            while steps[0] < 17:
                step(v.memset(over[:, 0:1], 0.0))
            with v.Fori(0, L) as l:
                v.wait_ge(par1_in.sem, par1_in(l, 16))
                ffn_dve(v, ffn1, l, ffn1_at(l), lambda k: par1_at(0, k), False, 0.5)
                mix1_dve(v, l)
                xat_dve(v, l)
                ffn_dve(v, ffn2, l, ffn2_at(l), lambda k: par1_at(4, k), False, 0.5)
            norm_dve(v, finalnorm, 0, x_tile, lambda k: p1[:, FIN1 + k:FIN1 + k + 1], plain_dst=x_tile)
            v.wait_ge(finalnorm.scaled.sem, finalnorm.scaled(0, KD))
            with v.Fori(0, L) as l:
                v.wait_ge(par2_in.sem, par2_in(l, 16))
                v.wait_ge(cpar_in.sem, cpar_in(l, 16))
                mix2_dve(v, l)
                ffn_dve(v, ffn3, l, ffn3_at(l), lambda k: p2[:, FN0 + k:FN0 + k + 1], True, 1.0)
            norm_dve(v, endnorm, 0, x_tile, lambda k: p2[:, FIN2 + k:FIN2 + k + 1], plain_dst=x_tile)

        @block.tensor
        def _(pe):
            pe.wait_ge(led, len(leads))
            pe.wait_ge(setup, 2)
            pe.wait_ge(consts_in, 16 * CONST_LOADS)
            norm_pe(pe, memnorm, 0)
            with pe.Fori(0, L) as l:
                ffn_pe(pe, ffn1, l, ffn1_at(l))
                mix1_pe(pe, l)
                xat_pe(pe, l)
                ffn_pe(pe, ffn2, l, ffn2_at(l))
            norm_pe(pe, finalnorm, 0)
            with pe.Fori(0, L) as l:
                mix2_pe(pe, l)
                ffn_pe(pe, ffn3, l, ffn3_at(l))
            norm_pe(pe, endnorm, 0)


CONST = {}
_at = 0
for _name, _width in (("ident", P), ("causal", S), ("halves", 2 * P), ("halfcol", 2), ("cols", 4), ("mcos", S),
                      ("msin", S), ("rcos", S), ("rsin", S), ("scanmask", S), ("decay", T * MH * P)):
    CONST[_name] = (_at, _at + _width)
    _at += _width
CONST_WIDTH = _at


def constants():
    c = np.zeros((P, CONST_WIDTH), np.float32)

    def put(name, a):
        c[:, CONST[name][0]:CONST[name][1]] = a

    row, col = np.arange(P)[:, None], np.arange(P)[None, :]
    put("ident", row == col)
    put("causal", np.concatenate([np.zeros((P, S - P)), np.where(col > row, MASKED, 0.0)], axis=1))
    put("halves", np.concatenate([np.broadcast_to(col < 64, (P, P)), np.broadcast_to(col >= 64, (P, P))], axis=1))
    put("halfcol", np.concatenate([row < 64, row >= 64], axis=1))

    def inverse_frequency(dim):
        return (10000.0 ** (-np.arange(0, dim, 2) / dim)).astype(np.float32)

    def rows_of(dim):
        r = np.arange(P) % dim
        return inverse_frequency(dim)[r % (dim // 2)], np.where(r < dim // 2, -1.0, 1.0).astype(np.float32)

    freq, sign = rows_of(64)
    put("cols", np.stack([freq, sign, sign * 0, sign * 0], axis=1))
    for cos, sin, dim in (("mcos", "msin", 64), ("rcos", "rsin", DK)):
        freq, sign = rows_of(dim)
        angle = freq[:, None] * np.arange(S, dtype=np.float32)[None, :]
        put(cos, np.cos(angle))
        put(sin, np.sin(angle) * sign[:, None])
    put("scanmask", np.broadcast_to(np.arange(S) % P != 0, (P, S)))
    log_g = np.log(1.0 - 2.0 ** (-5.0 - np.arange(MH)))
    dist = np.arange(T)[:, None, None, None] * P + col[0][None, None, None, :] - np.arange(P)[None, :, None, None]
    decay = np.where(dist >= 0, np.exp(log_g[None, None, :, None] * np.maximum(dist, 0)), 0.0) * DK ** -0.5
    put("decay", decay.transpose(1, 0, 2, 3).reshape(P, -1))
    masks = np.zeros((P, LEVELS, P), np.uint8)
    for lv in range(LEVELS - 1):
        size = P >> lv
        masks[:, lv, :] = ((row // size == col // size) & (row % size < size // 2) & (col % size >= size // 2))
    masks[:, LEVELS - 1, :] = row == col
    return c, masks.reshape(P, LEVELS * P).view(np.int32)


def layouts(inputs):
    a = {k: np.asarray(v) for k, v in inputs.items()}

    def rows(m):
        return m.reshape(-1, P, m.shape[-1]).transpose(1, 0, 2)

    def col_chunks(w):
        k, n = w.shape[0] // P, w.shape[1] // P
        return w.reshape(k, P, n, P).transpose(2, 1, 0, 3).reshape(n, P, k * P)

    def value_chunks(w):
        k = w.shape[0] // P
        return w.reshape(k // 2, 2, P, S).transpose(0, 2, 1, 3).reshape(k // 2, P, 2 * S)

    def gate_up(g, u):
        return np.concatenate([np.stack([col_chunks(g[l]), col_chunks(u[l])], axis=1).reshape(2 * KF, P, A)
                               for l in range(L)])

    def down(w):
        return np.concatenate([col_chunks(w[l]).reshape(KD, P, 2, DN).transpose(0, 2, 1, 3).reshape(2 * KD, P, DN)
                               for l in range(L)])

    def pieces(w, sizes):
        return np.split(w, np.cumsum(sizes)[:-1], axis=1)

    def columns(*vectors):
        return np.concatenate([v.reshape(-1, P).T for v in vectors], axis=1)

    mid, widx, par1 = [], [], []
    for l in range(L):
        a_val, a_gate, b_gate, c_gate, b_h, q, k, v, q_idx, k_idx, w_idx = pieces(
            a["w_in"][l], (256, 256, 256, 256, 256, 512, 512, 512, 256, 64, IDXH))
        mem_k, mem_v = a["xa_wkv"][l][:, :D], a["xa_wkv"][l][:, D:]
        mid += [col_chunks(q_idx), col_chunks(np.concatenate([k_idx, k_idx], axis=1)), col_chunks(k), col_chunks(q),
                col_chunks(a_val), col_chunks(a_gate), value_chunks(v), col_chunks(c_gate), col_chunks(b_h),
                col_chunks(b_gate), col_chunks(a["w_out"][l]), col_chunks(mem_k), value_chunks(mem_v[:, :S]),
                value_chunks(mem_v[:, S:]), col_chunks(a["xa_wq"][l]), col_chunks(a["xa_wo"][l])]
        widx.append(rows(w_idx).reshape(P, 4 * KD))
        par1.append(columns(a["ffn1_norm"][l], a["mix_norm"][l], a["xa_norm"][l], a["mem_norm"][l], a["ffn2_norm"][l],
                            a["conf_dw"][l].reshape(-1), a["conf_dw_b"][l], a["conf_ln_g"][l], a["conf_ln_b"][l],
                            a["sc_dw"][l].reshape(-1), a["final_norm"]))
    mix2, par2, convpar = [], [], []
    for l in range(L):
        c_q, c_kv, k_r, g_q, g_k, g_v, g_lr, g_g, r_q, r_k, r_v, r_g = pieces(
            a["w_in_2"][l], (384, 256, 64, 128, 128, 256, 16, 256, 128, 128, 256, 256))
        g_lr = np.concatenate([g_lr, np.zeros((D, P - 16), np.float32)], axis=1)
        uq = a["mla_w_uq_2"][l].reshape(384, MH, 192)
        nope, rope = uq[:, :, :128].reshape(384, 512), uq[:, :, 128:].reshape(384, 256)
        ukv = a["mla_w_ukv_2"][l].reshape(256, MH, 256)
        uk, uv = ukv[:, :, :128].reshape(256, 512), ukv[:, :, 128:].reshape(256, 512)
        uq = col_chunks(np.concatenate([nope, rope], axis=1)).reshape(3, 2, P, 3 * P).transpose(0, 2, 1, 3)
        uq = np.concatenate([uq.reshape(3, P, 6 * P), np.zeros((3, P, A - 6 * P), np.float32)], axis=2)
        uk = col_chunks(uk).transpose(1, 0, 2).reshape(1, P, A)
        mix2 += [col_chunks(np.concatenate([g_lr, g_q, g_k, r_q, r_k, k_r, k_r, c_q, c_kv], axis=1)),
                 value_chunks(np.concatenate([g_v, r_v], axis=1)), col_chunks(np.concatenate([g_g, r_g], axis=1)),
                 uq, uk, value_chunks(uv), col_chunks(a["w_out_2"][l])]
        par2.append(columns(a["attn_norm_2"][l], a["mla_q_norm_2"][l], a["mla_kv_norm_2"][l], a["mla_out_norm_2"][l],
                            a["gla_b_gate_2"][l], a["gla_out_norm_2"][l], a["ret_out_norm_2"][l], a["ffn_norm_2"][l],
                            a["final_norm_2"]))
        convpar.append(np.concatenate([a["ffn_conv_w_2"][l], a["ffn_conv_b_2"][l][None]]).reshape(4, KF, P)
                       .transpose(2, 1, 0))
    consts, masks = constants()
    return {
        "x_in": rows(a["x"][0].T), "mem_in": rows(a["mem"][0].T), "pos_in": a["positions"].reshape(1, S),
        "par1": np.stack(par1), "par2": np.stack(par2), "convpar": np.stack(convpar), "consts": consts,
        "masks": masks, "gate_w": a["gla_w_gate_2"],
        "gu1": gate_up(a["ffn1_w_gate"], a["ffn1_w_up"]), "dn1": down(a["ffn1_w_down"]),
        "widx": np.stack(widx), "mid": np.concatenate(mid),
        "gu2": gate_up(a["ffn2_w_gate"], a["ffn2_w_up"]), "dn2": down(a["ffn2_w_down"]),
        "mix2": np.concatenate(mix2), "up2": gate_up(a["ffn_w_up_2"][:, :, :F], a["ffn_w_up_2"][:, :, F:]),
        "dn3": down(a["ffn_w_down_2"]),
    }


def kernel(**inputs):
    import concourse.bacc as bacc
    from concourse.bass_utils import run_bass_kernel_spmd

    nc = bacc.Bacc("TRN2", target_bir_lowering=False, num_devices=1)
    arrays, args = {}, []
    for name, a in layouts(inputs).items():
        arrays[name] = np.ascontiguousarray(a)
        args.append(nc.dram_tensor(name, a.shape, mybir.dt.from_np(a.dtype), kind="ExternalInput").ap())
    y = nc.dram_tensor("y_out", (P, KD, S), F32, kind="ExternalOutput").ap()
    program(nc, *args, y)
    out = run_bass_kernel_spmd(nc, [arrays], core_ids=[0]).results[0]["y_out"]
    return out.transpose(2, 1, 0).reshape(1, S, D)
```

```python
import numpy as np
import concourse.bass as bass
from concourse import mybir

F32 = mybir.dt.float32
F32R = mybir.dt.float32r
I32 = mybir.dt.int32
U8 = mybir.dt.uint8
ACT = mybir.ActivationFunctionType
ALU = mybir.AluOpType
AXX = mybir.AxisListType.X

P = 128
S = 512
T = S // P
D = 1024
KD = D // P
L = 2
F = 2816
KF = F // P
M = 256
MT = M // P
A = KD * P
KH = KF // 2
DN = KH * P
HEADS = 8
IDXH = 4
TOPK = 128
CONVW = 31
XH = 4
MH = 4
DK = 32
LEVELS = 8
NPAR1 = 5 * KD + 2 * CONVW + 3 * 2 + 2 * 3 + KD
NPAR2 = KD + 3 + 2 + 4 + 1 + 2 + 2 + KD + KD
MASKED = -1.0e30
TAKEN = -3.0e38
TAKEN_BELOW = -2.0e38
PI = float(np.pi)
TWO_PI_PARTS = (6.28125, 0.0019350051879882812, 3.019915981956752e-07)
ROUND = 1.5 * 2.0 ** 23
AHEAD = 2
LAG = 1
SCORE_BANKS = (0, 1, 6)
XSCORE_BANKS = (0, 1)
LEAD = 2
FIRST_BLOCK = (0, 4, 7, 9)
BLOCKS = [(a, c) for a in range(T) for c in range(a, T)]
BIAS_AT = (0, 128, 384, 768)
MIX1_CHUNKS = 25 + 8 + 16 + 8 + 8
MIX2_CHUNKS = 19 + 3 + 2 + 8
C1 = 2 * KF + 16 + 1 + MIX1_CHUNKS + 2 * KF + 16
C2 = MIX2_CHUNKS + 2 * KF + 16


class Signal:

    def __init__(self, sem, per_layer, lead):
        self.sem, self.per_layer, self.lead = sem, per_layer, lead

    def __call__(self, layer, n):
        return layer * self.per_layer + (n + self.lead)


class Chunk:

    def __init__(self, stack_start, per_layer, layer, c, i=0):
        self.n = layer * per_layer + i * 2 + (stack_start + c)
        self.half = layer * (per_layer // 2) + i + (stack_start + c) // 2
        self.slot = c % 2


def program(nc, x_in, mem_in, pos_in, par1, par2, convpar, consts, masks, gate_w,
            gu1, dn1, widx, mid, gu2, dn2, mix2, up2, dn3, y_out):
    leads = []

    def sig(name, per_layer, lead=0):
        s = Signal(nc.alloc_semaphore(name), per_layer, lead)
        if lead:
            leads.append((s.sem, lead))
        return s

    start = (nc.sbuf_base + 63) // 64 * 64
    arena = nc.alloc_sbuf_tensor("arena", [P, (nc.sbuf_usable_end - start) // 4 - 32], F32)
    top = [start]

    def place(name, shape, dt=F32, at=None):
        where = top[0] if at is None else at
        t = nc.alloc_sbuf_tensor_at(name, [P] + list(shape), dt, offset=where)
        if at is None:
            top[0] += (int(np.prod(shape)) * (1 if dt == U8 else 4) + 31) // 32 * 32
            assert top[0] <= nc.sbuf_usable_end, (name, top[0], nc.sbuf_usable_end)
        return t

    x = place("x", [KD, S])
    hh_at = top[0]
    hh = place("h_hi", [KD, S], F32R)
    yf_at = top[0]
    hl = place("h_lo", [KD, S], F32R)
    yf = place("branch_out", [KD, S], at=yf_at)
    raw = place("w_raw", [2, DN])
    wh = place("w_hi", [2, DN], F32R)
    wl = place("w_lo", [2, DN], F32R)
    ones = place("ones", [P])
    halves = place("halves", [2, P])
    halfcol = place("halfcol", [2])
    ident = place("ident", [P])
    causal = place("causal", [S])
    cols = place("cols", [4])
    p1 = place("params1", [NPAR1])
    p2 = place("params2", [NPAR2])
    st = place("stats", [3, 48])
    sq_at = top[0]
    sq = place("squares", [2, S])
    hf = place("scaled", [2, S])
    probs = place("probs", [4, S], at=sq_at)
    ssum = place("square_sum", [S])
    widx_row = ssum
    dg = place("diagonals", [2, 8, P])
    one = place("one", [4])
    gate_cells = place("gate_cells", [8])
    small = place("small", [4, 4])
    cpar = place("conv_par", [KF, 4])
    rt = dg[:, :, :, :].rearrange("p b e c -> p (b e c)")[:, 0:3 * S].rearrange("p (n s) -> p n s", n=3)
    region = top[0]

    ah = place("act_hi", [KF, S], F32R)
    al = place("act_lo", [KF, S], F32R)
    after_act = top[0]
    top[0] = keep1 = (nc.sbuf_usable_end - 64 - 4 * (2 * S + KD * M)) // 32 * 32
    cos1 = place("cos1", [S])
    sin1 = place("sin1", [S])
    memn = place("mem_normed", [KD, M])
    sg, af, cv = sq, hf, dg[:, :, :, :].rearrange("p b e c -> p b (e c)")
    gs, rstd_rows = cv[:, :, S:2 * S], ssum
    top[0] = region
    qk_hi_at = top[0]
    qk_hi = place("qk_hi", [KD, S], F32R)
    qk_lo_at = top[0]
    qk_lo = place("qk_lo", [KD, S], F32R)
    qk_swap = place("qk_swap", [KD, S], at=qk_hi_at)
    qk_raw = place("qk_raw", [KD, S], at=qk_lo_at)
    v_at = top[0]
    v_hi = place("v_hi", [T, S], F32R)
    v_lo = place("v_lo", [T, S], F32R)
    ix_hi = place("ix_hi", [3, S], F32R, at=v_at)
    ix_lo = place("ix_lo", [3, S], F32R, at=v_at + 3 * S * 4)
    ix_swap = place("ix_swap", [3, S], at=v_at)
    ix_raw = place("ix_raw", [3, S], at=v_at + 3 * S * 4)
    bias = place("bias", [1280])
    best = place("best", [3 * 8])
    widx_tok = place("w_idx", [16])
    conv_at = top[0]
    aval = place("a_val", [2, S])
    asig = place("a_sig", [2, S])
    bgate_at = top[0]
    bgate = place("b_gate", [2, S])
    bh = place("b_h", [2, S])
    cgate = place("c_gate", [2, S])
    xpad = place("conv_in", [2, CONVW - 1 + S])
    acc = place("conv_acc", [2, S])
    yb = bh
    rbuf = place("relu", [2, S], at=bgate_at)
    assert top[0] <= keep1 and after_act <= keep1
    top[0] = conv_at
    pt_hi = [place(f"probsT_hi{e}", [T, S], F32R) for e in range(2)]
    pt_lo = [place(f"probsT_lo{e}", [T, S], F32R) for e in range(2)]
    assert top[0] <= keep1
    top[0] = region
    mh_hi = place("mem_hi", [KD, M], F32R)
    mh_lo = place("mem_lo", [KD, M], F32R)
    mf = place("mem_scaled", [2, M])
    km_hi = place("kmem_hi", [KD, M], F32R)
    km_lo = place("kmem_lo", [KD, M], F32R)
    vm_hi = place("vmem_hi", [MT, D], F32R)
    vm_lo = place("vmem_lo", [MT, D], F32R)
    xpt_hi = [place(f"xprobsT_hi{e}", [MT, S], F32R) for e in range(2)]
    xpt_lo = [place(f"xprobsT_lo{e}", [MT, S], F32R) for e in range(2)]
    assert top[0] <= keep1
    qx_hi = place("qx_hi", [KD, S], F32R, at=region)
    qx_lo = place("qx_lo", [KD, S], F32R, at=top[0])
    top[0] += KD * S * 4
    assert mf is not None and KD * S * 4 <= 2 * KD * M * 4 and top[0] <= keep1
    top[0] = region
    cq_hi = place("cq_hi", [3, S], F32R)
    cq_lo = place("cq_lo", [3, S], F32R)
    ck_hi = place("ck_hi", [2, S], F32R)
    ck_lo = place("ck_lo", [2, S], F32R)
    mpt_hi = [place(f"mprobsT_hi{e}", [T, S], F32R, at=(region, hh_at)[e]) for e in range(2)]
    mpt_lo = [place(f"mprobsT_lo{e}", [T, S], F32R, at=(region, hh_at)[e] + T * S * 4) for e in range(2)]
    assert region + 2 * T * S * 4 <= top[0]
    gates = place("gates", [4, S])
    kr_hi_at = top[0]
    kr_hi = place("kr_hi", [S], F32R)
    kr_lo = place("kr_lo", [S], F32R)
    kr_swap = place("kr_swap", [S], at=kr_hi_at)
    kr_raw = place("kr_raw", [S], at=kr_hi_at + S * 4)
    mcos = place("mcos", [S])
    msin = place("msin", [S])
    branch_at = top[0]
    glr = place("glr", [S])
    gw = place("gate_w", [P])
    gqk = place("gqk", [2, S])
    rqk = place("rqk", [2, S])
    ret_at_byte = top[0]
    rswap = place("rswap", [2, S])
    rcos = place("rcos", [S])
    rsin = place("rsin", [S])
    decay = place("decay", [T, MH, P])
    ret_end = top[0]
    top[0] = ret_at_byte
    diff = place("diff", [2, S])
    edec = place("edec", [2, S])
    qe = place("qe", [2, S])
    ke = place("ke", [2, S])
    top[0] = max(top[0], ret_end)
    vgr = place("vgr", [T, S])
    pair_at = top[0]
    pair = place("pair", [len(BLOCKS), MH, P])
    cq = place("c_q", [3, S], at=pair_at)
    ckv = place("c_kv", [2, S], at=pair_at + 3 * S * 4)
    lmask = place("lmask", [LEVELS, P], U8)
    zb = place("zb", [2, S])
    cum = place("cum", [S])
    k3 = place("k3", [3, P])
    etot = place("etot", [T])
    scanmask = place("scanmask", [S])
    top[0] = branch_at
    qn_hi = place("qn_hi", [MH, S], F32R)
    qn_lo = place("qn_lo", [MH, S], F32R)
    qr_hi_at = top[0]
    qr_hi = place("qr_hi", [2, S], F32R)
    qr_lo_at = top[0]
    qr_lo = place("qr_lo", [2, S], F32R)
    qr_swap = place("qr_swap", [2, S], at=qr_hi_at)
    qr_raw = place("qr_raw", [2, S], at=qr_lo_at)
    kn_hi = place("kn_hi", [MH, S], F32R)
    kn_lo = place("kn_lo", [MH, S], F32R)
    vm2_hi = place("vm2_hi", [T, S], F32R)
    vm2_lo = place("vm2_lo", [T, S], F32R)

    banks = nc.alloc_psum_tensor("banks", [P, 8, S], F32)
    bank = [banks[:, i, :] for i in range(8)]

    class Ring:
        raw_in = [nc.alloc_semaphore("ring_raw_in0"), nc.alloc_semaphore("ring_raw_in1")]
        hi = nc.alloc_semaphore("ring_hi")
        split = nc.alloc_semaphore("ring_split")
        done = nc.alloc_semaphore("ring_done")

    leads += [(Ring.split, LEAD), (Ring.done, LEAD)]
    consts_in = nc.alloc_semaphore("consts_in")
    x_in_sem = nc.alloc_semaphore("x_in_sem")
    setup = nc.alloc_semaphore("setup_done")
    led = nc.alloc_semaphore("lead_given")
    tab = nc.alloc_semaphore("rope_table_steps")
    tab_sin = nc.alloc_semaphore("rope_sines")
    y_stored = nc.alloc_semaphore("y_stored")
    par1_in, par2_in = sig("par1_in", 16), sig("par2_in", 16)
    cpar_in = sig("cpar_in", 16)
    tables2_in = sig("tables2_in", 16 * 8)

    class NormSems:
        sq = sig("norm_squared", 0)
        sum = sig("norm_summed", 0, LEAD)
        spread = sig("norm_spread", 0)
        inv = sig("norm_inverse", 0)
        rstd = sig("norm_rstd", 0)
        dg = sig("norm_diag", 0)
        scaled = sig("norm_scaled", 0)
        hi = sig("norm_hi", 0, LEAD)
        lo = sig("norm_lo", 0, LEAD)

    class Norm:

        def __init__(self, k, norms, tiles_before, parts_before, scaled_before, per_norms=0, per_tiles=0, per_scaled=0,
                     tiles=T):
            self.k, self.tiles = k, tiles
            self.sq = Signal(NormSems.sq.sem, per_tiles, tiles_before)
            self.sum = Signal(NormSems.sum.sem, per_tiles, tiles_before + LEAD)
            self.spread = Signal(NormSems.spread.sem, 2 * per_norms, 2 * norms)
            self.inv = Signal(NormSems.inv.sem, 5 * per_norms, 5 * norms)
            self.rstd = Signal(NormSems.rstd.sem, per_norms, norms)
            self.dg = Signal(NormSems.dg.sem, per_norms, norms)
            self.scaled = Signal(NormSems.scaled.sem, per_scaled, scaled_before)
            self.hi = Signal(NormSems.hi.sem, per_tiles, parts_before + LEAD)
            self.lo = Signal(NormSems.lo.sem, per_tiles, parts_before + LEAD)

    memnorm = Norm(KD, 0, 0, 0, 0, tiles=MT)
    N1, N2 = 4 * KD, 2 * KD + 3 + 2
    W1, W2 = 2 * KD, KD + 3 + 2
    ffn1norm, mixnorm, xanorm, ffn2norm = [
        Norm(KD, 1 + i, KD * (1 + i), KD * i, KD + KD * scaled, 4, N1, W1) for i, scaled in enumerate((0, 0, 1, 2))]
    finalnorm = Norm(KD, 1 + 4 * L, KD + N1 * L, 0, KD + W1 * L)
    attnorm, cqnorm, cknorm, ffn3norm = [
        Norm(k, 2 + 4 * L + i, 2 * KD + N1 * L + before, N1 * L + before, 2 * KD + W1 * L + before, 4, N2, W2)
        for i, (k, before) in enumerate([(KD, 0), (3, KD), (2, KD + 3), (KD, KD + 5)])]
    endnorm = Norm(KD, 2 + 8 * L, 2 * KD + (N1 + N2) * L, 0, 2 * KD + (W1 + W2) * L)

    class FfnSems:
        rstd = sig("ffn_rstd", 0)
        gate = sig("ffn_gate", 0, LEAD)
        gated = sig("ffn_gated", 0)
        conv = sig("ffn_conv", 0)
        silu = sig("ffn_silu", 0, LEAD)
        act = sig("ffn_act", 0, LEAD)
        act_hi = sig("ffn_act_hi", 0, LEAD)
        act_lo = sig("ffn_act_lo", 0)

    class Ffn:

        def __init__(self, name, norm, before, per):
            self.norm = norm
            self.rstd = Signal(FfnSems.rstd.sem, per, before)
            self.gate = Signal(FfnSems.gate.sem, per * KF, before * KF + LEAD)
            self.gated = Signal(FfnSems.gated.sem, per * KF, before * KF)
            self.conv = Signal(FfnSems.conv.sem, 3 * KF, 0)
            self.silu = Signal(FfnSems.silu.sem, per * KF, before * KF + LEAD)
            self.act = Signal(FfnSems.act.sem, per * KF, before * KF + LEAD)
            self.act_hi = Signal(FfnSems.act_hi.sem, per * KF, before * KF + LEAD)
            self.act_lo = Signal(FfnSems.act_lo.sem, per * KF, before * KF)
            self.x = sig(name + "_x", KD, KD)

    class AttentionSems:
        score = sig("att_score", 0)
        max = sig("att_max", 0, 4)
        neg = sig("att_neg", 0)
        exp = sig("att_exp", 0, 4)
        inv = sig("att_inv", 0)
        prob = sig("att_prob", 0)
        turn = sig("att_turn", 0, 4)
        pt_hi = sig("att_pt_hi", 0)
        pt_lo = sig("att_pt_lo", 0, LEAD)
        out = sig("att_out", 0, LEAD)
        y_hi = sig("att_y_hi", 0, 2 * LEAD)
        y_lo = sig("att_y_lo", 0, 2 * LEAD)

    class Attention:

        def __init__(self, heads, outs, before, per):
            self.items, self.outs = heads * T, outs

            def item(s, lead=0):
                return Signal(s.sem, per[0] * T, before[0] * T + lead)

            self.score, self.neg = item(AttentionSems.score), item(AttentionSems.neg)
            self.max, self.exp = item(AttentionSems.max, 4), item(AttentionSems.exp, 4)
            self.inv, self.prob = item(AttentionSems.inv), item(AttentionSems.prob)
            self.turn, self.pt_hi = item(AttentionSems.turn, 4), item(AttentionSems.pt_hi)
            self.pt_lo = item(AttentionSems.pt_lo, LEAD)
            self.out = Signal(AttentionSems.out.sem, per[0], before[0] + LEAD)
            self.y_hi = Signal(AttentionSems.y_hi.sem, per[1], before[1] + 2 * LEAD)
            self.y_lo = Signal(AttentionSems.y_lo.sem, per[1], before[1] + 2 * LEAD)

    ffn1, ffn2, ffn3 = Ffn("ffn1", ffn1norm, 0, 2), Ffn("ffn2", ffn2norm, 1, 2), Ffn("ffn3", ffn3norm, 2 * L, 1)
    H1, O1 = HEADS + XH, HEADS + 2 * XH
    dsa, xat = Attention(HEADS, 1, (0, 0), (H1, O1)), Attention(XH, 2, (HEADS, HEADS), (H1, O1))
    mla = Attention(MH, 1, (H1 * L, O1 * L), (MH, MH))
    widx_row_s, widx_ps, widx_tok_s = sig("widx_row", 1), sig("widx_ps", 1), sig("widx_tok", 1)
    evicted = sig("proj_evicted", 21, LEAD)
    swap1 = [sig(f"swap1_{j}", 64) for j in range(11)]
    rope1 = sig("rope1", 11 * 5)
    logit, relu, score = sig("logit_ps", 12), sig("relu", 12, LEAD), sig("idx_score", 12, LEAD)
    cut = sig("idx_masked", 3)
    ROUNDS = TOPK // 8
    topk = sig("topk_steps", 3 * 2 * ROUNDS, LEAD)
    bias_s = sig("bias_ready", 4)
    v_hi_s, v_lo_s = sig("v_hi", T), sig("v_lo", T)
    glu, conv1 = sig("glu", 3), sig("conv1", 2 * CONVW + 2)
    ln_mean, ln_dev, ln_sq = sig("ln_mean", 1), sig("ln_dev", 2), sig("ln_sq", 2)
    ln_var, ln_inv, ln_rstd = sig("ln_var_ps", 1), sig("ln_inv", 4), sig("ln_rstd", 2)
    ln_y, ya = sig("ln_y", 2), sig("ya", 2)
    scin, scconv, yb_s = sig("sc_in", 2), sig("sc_conv", 10), sig("yb", 2)
    yab_hi, yab_lo = sig("yab_hi", 4), sig("yab_lo", 4)
    out1_x = sig("out1_x", KD, LEAD)
    mscaled, mhi, mlo = sig("mem_scaled", KD), sig("mem_hi", KD, LEAD), sig("mem_lo", KD, LEAD)
    kv_hi, kv_lo = sig("kv_hi", 12), sig("kv_lo", 12, LEAD)
    qx_hi_s, qx_lo_s = sig("qx_hi", KD), sig("qx_lo", KD, LEAD)
    wo_x = sig("wo_x", KD, LEAD)
    z_ev = sig("z_evicted", 15, LEAD)
    vz_ev = sig("vz_evicted", T)
    rswap_s, krswap_s, qrswap_s = sig("rswap", 16 * 8), sig("krswap", 64), [sig(f"qrswap{j}", 64) for j in range(2)]
    rrope = sig("rrope", 6)
    krrope, qrrope = sig("krrope", 5), sig("qrrope", 8)
    gk_ps = sig("gk_ps", 1)
    gk_dve, gk_act = sig("gk_dve", 4), sig("gk_act", 2)
    ret_ps, ret_at = sig("ret_ps", len(BLOCKS)), sig("ret_at", len(BLOCKS), LEAD)
    ret_out, ret_y = sig("ret_out", MH), sig("ret_y", MH)
    lev_d, lev_e, lev_q = sig("lev_d", 15), sig("lev_e", 9), sig("lev_q", 2 * 9, 2 * LEAD)
    zero_at = sig("zero_at", 1)
    lev_ps, lev_at = sig("lev_ps", LEVELS * T), sig("lev_at", LEVELS * T, LEAD)
    etot_s, k3_s = sig("etot", 1), sig("k3", 3)
    far_ps, far_at = sig("far_ps", 6), sig("far_at", 6, LEAD)
    gla_out, gla_y = sig("gla_out", MH), sig("gla_y", MH)
    u_hi, u_lo = sig("u_hi", 14), sig("u_lo", 14, LEAD)
    hs_sq, hs_tot = sig("hs_sq", KD), sig("hs_tot", KD, LEAD)
    hs_var, hs_inv, hs_rstd = sig("hs_var", 2), sig("hs_inv", 4), sig("hs_rstd", 1)
    hs_dg, hs_bc = sig("hs_dg", KD), sig("hs_bc", KD, LEAD)
    hs_n, hs_g = sig("hs_n", KD, LEAD), sig("hs_g", 4)
    hs_hi, hs_lo = sig("hs_hi", KD, LEAD), sig("hs_lo", KD)
    out2_x = sig("out2_x", KD, LEAD)

    def par1_at(group, k):
        return p1[:, group * KD + k:group * KD + k + 1]

    CW0 = 5 * KD
    CB0, LG0, LB0, SC0 = CW0 + 2 * CONVW, CW0 + 2 * CONVW + 2, CW0 + 2 * CONVW + 4, CW0 + 2 * CONVW + 6
    FIN1 = SC0 + 6
    QN0, KN0, MO0, GB0, GO0, RO0, FN0 = KD, KD + 3, KD + 5, KD + 9, KD + 10, KD + 12, KD + 14
    FIN2 = FN0 + KD

    def f32(ap):
        return ap.bitcast(F32)

    def mm3(pe, out, w_hi, w_lo, m_hi, m_lo, start, stop):
        pe.matmul(out, w_hi, m_hi, start=start, stop=False, skip_group_check=True)
        pe.matmul(out, w_hi, m_lo, start=False, stop=False, skip_group_check=True)
        return pe.matmul(out, w_lo, m_hi, start=False, stop=stop, skip_group_check=True)

    def gate(v, cell):
        v.memset(gate_cells[:, cell:cell + 1], 0.0)

    def load(sp, ch, src, width):
        sp.wait_ge(Ring.split, ch.n + 1)
        sp.dma_start(raw[:, ch.slot, 0:width], src).then_inc(Ring.raw_in[ch.slot], 16)

    def split(g, ch, src, width):
        g.wait_ge(Ring.raw_in[ch.slot], ch.half * 16 + 16)
        g.wait_ge(Ring.done, ch.n + 1)
        g.tensor_tensor(wh[:, ch.slot, 0:width], raw[:, ch.slot, 0:width], one[:, 0:1].to_broadcast([P, width]),
                        ALU.mult).then_inc(Ring.hi, 1)
        g.wait_ge(Ring.hi, ch.n + 1)
        g.tensor_tensor(wl[:, ch.slot, 0:width], raw[:, ch.slot, 0:width], f32(wh[:, ch.slot, 0:width]),
                        ALU.subtract).then_inc(Ring.split, 1)

    def takes_over(eng, ch):
        eng.wait_ge(Ring.split, ch.n + LEAD)

    def split_hi(act, ch):
        act.wait_ge(Ring.raw_in[ch.slot], ch.half * 16 + 16)
        act.wait_ge(Ring.done, ch.n + 1)
        act.activation(wh[:, ch.slot, 0:A], raw[:, ch.slot, 0:A], ACT.Copy).then_inc(Ring.hi, 1)

    def split_lo(v, ch):
        v.wait_ge(Ring.hi, ch.n + 1)
        v.tensor_tensor(wl[:, ch.slot, 0:A], raw[:, ch.slot, 0:A], f32(wh[:, ch.slot, 0:A]), ALU.subtract)\
            .then_inc(Ring.split, 1)

    def stack1_chunks(eng, l, visit, after_inputs=None, shared=True):
        def at(c, i=0):
            return Chunk(0, C1, l, c, i)

        def ffn(c, gu, dn):
            with eng.Fori(0, KF) as i:
                for s in range(2):
                    visit(eng, at(c + s, i), gu[l * (2 * KF) + i * 2 + s, :, :], A)
            with eng.Fori(0, KD) as i:
                for s in range(2):
                    visit(eng, at(c + 2 * KF + s, i), dn[l * 16 + i * 2 + s, :, :], DN)

        ffn(0, gu1, dn1)
        for m in range(4):
            visit(eng, at(60 + m), mid[l * MIX1_CHUNKS + m, :, :], A)
        visit(eng, at(64), widx[l, :, :], 4 * KD)
        visit(eng, at(65), mid[l * MIX1_CHUNKS + 4, :, :], A)

        def pairs(first, end):
            with eng.Fori(0, (end - first) // 2) as i:
                for s in range(2):
                    visit(eng, at(61 + first + s, i), mid[l * MIX1_CHUNKS + i * 2 + (first + s), :, :], A)

        pairs(5, 25)
        if after_inputs is not None:
            after_inputs(eng, l)
        pairs(OUT_CHUNK, MEMK_CHUNK)
        visit(eng, at(61 + MEMK_CHUNK), mid[l * MIX1_CHUNKS + MEMK_CHUNK, :, :], A)
        if shared:
            pairs(MEMK_CHUNK + 1, XQ_CHUNK + 1)
        else:
            takes_over(eng, at(61 + XQ_CHUNK + 1))
        visit(eng, at(61 + XQ_CHUNK + 1), mid[l * MIX1_CHUNKS + XQ_CHUNK + 1, :, :], A)
        pairs(XQ_CHUNK + 2, MIX1_CHUNKS)
        ffn(61 + MIX1_CHUNKS, gu2, dn2)

    def stack2_chunks(eng, l, visit):
        def at(c, i=0):
            return Chunk(L * C1, C2, l, c, i)

        with eng.Fori(0, MIX2_CHUNKS // 2) as i:
            for s in range(2):
                visit(eng, at(s, i), mix2[l * MIX2_CHUNKS + i * 2 + s, :, :], A)
        with eng.Fori(0, KF) as i:
            for s in range(2):
                visit(eng, at(MIX2_CHUNKS + s, i), up2[l * (2 * KF) + i * 2 + s, :, :], A)
        with eng.Fori(0, KD) as i:
            for s in range(2):
                visit(eng, at(MIX2_CHUNKS + 2 * KF + s, i), dn3[l * 16 + i * 2 + s, :, :], DN)

    def swap_halves(act, dst, src, half, sem):
        for b in range(0, P, 2 * half):
            act.dma_start(dst[b:b + half], src[b + half:b + 2 * half]).then_inc(sem, 16)
            act.dma_start(dst[b + half:b + 2 * half], src[b:b + half]).then_inc(sem, 16)

    def norm_act_squares(act, n, l, src, ready, width=S, first=0, end=None):
        for k in range(first, n.k if end is None else end):
            ready(act, k)
            act.wait_ge(n.sum.sem, n.sum(l, max(k - 1, 0)))
            act.activation(sq[:, k % 2, 0:width], src(k), ACT.Square).then_inc(n.sq.sem, 1)

    def norm_act_root(act, n, l):
        act.wait_ge(n.inv.sem, n.inv(l, 2))
        act.activation(st[:, 2, 0:n.tiles], st[:, 1, 0:n.tiles], ACT.Sqrt).then_inc(n.rstd.sem, 1)

    def norm_act_hi(act, n, l, hi_dst, width=S, between=None):
        for k in range(n.k):
            if between is not None:
                between(k)
            act.wait_ge(n.scaled.sem, n.scaled(l, k + 1))
            act.activation(hi_dst(k), hf[:, k % 2, 0:width], ACT.Copy).then_inc(n.hi.sem, 1)

    def norm_dve_sum_tile(v, n, l, k, width=S):
        v.wait_ge(n.sq.sem, n.sq(l, k + 1))
        if k == 0:
            v.tensor_scalar(ssum[:, 0:width], sq[:, 0, 0:width], 1.0, None, ALU.mult).then_inc(n.sum.sem, 1)
        else:
            v.wait_ge(n.sum.sem, n.sum(l, k))
            v.tensor_tensor(ssum[:, 0:width], ssum[:, 0:width], sq[:, k % 2, 0:width], ALU.add)\
                .then_inc(n.sum.sem, 1)

    def norm_dve_sum(v, n, l, width=S):
        for k in range(n.k):
            norm_dve_sum_tile(v, n, l, k, width)

    def add_tiles(v, add, n, l, last=True):
        for d in range(KD):
            add(d)
            if d >= 1:
                norm_dve_sum_tile(v, n, l, d - 1)
        if last:
            norm_dve_sum_tile(v, n, l, KD - 1)

    def norm_dve_inverse(v, n, l):
        v.wait_ge(n.spread.sem, n.spread(l, 1))
        v.tensor_scalar(st[:, 0, 0:n.tiles], bank[6][:, 0:n.tiles], 1.0 / (n.k * P), 1e-6, ALU.mult, ALU.add)\
            .then_inc(n.inv.sem, 1)
        v.wait_ge(n.inv.sem, n.inv(l, 1))
        v.reciprocal(st[:, 1, 0:n.tiles], st[:, 0, 0:n.tiles]).then_inc(n.inv.sem, 1)

    def refine_root(v, root, square, tmp, sem, done):
        v.tensor_tensor(tmp, root, root, ALU.mult).then_inc(sem, 1)
        v.wait_ge(sem, done + 1)
        v.scalar_tensor_tensor(tmp, tmp, -0.5, square, ALU.mult, ALU.mult).then_inc(sem, 1)
        v.wait_ge(sem, done + 2)
        v.scalar_tensor_tensor(root, tmp, 1.5, root, ALU.add, ALU.mult).then_inc(sem, 1)
        v.wait_ge(sem, done + 3)

    def norm_dve_diagonals(v, n, l):
        v.wait_ge(n.rstd.sem, n.rstd(l, 1))
        refine_root(v, st[:, 2, 0:n.tiles], st[:, 0, 0:n.tiles], st[:, 1, 0:n.tiles], n.inv.sem, n.inv(l, 2))
        for t in range(n.tiles):
            last = v.tensor_scalar(dg[:, 0, t, :], ident[:, :], st[:, 2, t:t + 1], None, ALU.mult)
        last.then_inc(n.dg.sem, 1)

    def norm_dve_scale(v, n, l, src, gain, hi_dst, lo_dst, plain_dst=None, width=S, between=None):
        v.wait_ge(n.spread.sem, n.spread(l, 2))

        def lo(k):
            v.wait_ge(n.hi.sem, n.hi(l, k + 1))
            v.tensor_tensor(lo_dst(k), hf[:, k % 2, 0:width], f32(hi_dst(k)), ALU.subtract).then_inc(n.lo.sem, 1)

        for k in range(n.k):
            if plain_dst is None:
                v.wait_ge(n.lo.sem, n.lo(l, max(k - 1, 0)))
            out = hf[:, k % 2, 0:width] if plain_dst is None else plain_dst(k)
            if gain is None:
                v.tensor_tensor(out, src(k), bank[7][:, 0:width], ALU.mult).then_inc(n.scaled.sem, 1)
            else:
                v.scalar_tensor_tensor(out, src(k), gain(k), bank[7][:, 0:width], ALU.mult, ALU.mult)\
                    .then_inc(n.scaled.sem, 1)
            if plain_dst is None and k >= 1:
                lo(k - 1)
            if between is not None:
                between(k)
        if plain_dst is None:
            lo(n.k - 1)

    def norm_pe_totals(pe, n, l):
        pe.wait_ge(n.sum.sem, n.sum(l, n.k))
        for t in range(n.tiles):
            mm = pe.matmul(bank[6][:, t:t + 1], ssum[:, t * P:(t + 1) * P], ones[:, 0:1], start=True, stop=True)
        mm.then_inc(n.spread.sem, 1)

    def norm_pe_spread(pe, n, l):
        pe.wait_ge(n.dg.sem, n.dg(l, 1))
        for t in range(n.tiles):
            mm = pe.matmul(bank[7][:, t * P:(t + 1) * P], ones[:, :], dg[:, 0, t, :], start=True, stop=True)
        mm.then_inc(n.spread.sem, 1)

    def norm_act(act, n, l, src, ready, hi_dst=None, width=S):
        norm_act_squares(act, n, l, src, ready, width)
        norm_act_root(act, n, l)
        if hi_dst is not None:
            norm_act_hi(act, n, l, hi_dst, width)

    def norm_dve(v, n, l, src, gain, hi_dst=None, lo_dst=None, plain_dst=None, width=S):
        norm_dve_inverse(v, n, l)
        norm_dve_diagonals(v, n, l)
        norm_dve_scale(v, n, l, src, gain, hi_dst, lo_dst, plain_dst, width)

    def norm_pe(pe, n, l):
        norm_pe_totals(pe, n, l)
        norm_pe_spread(pe, n, l)

    def x_tile(k):
        return x[:, k, :]

    def hh_tile(k):
        return hh[:, k, :]

    def hl_tile(k):
        return hl[:, k, :]

    def column_tile(pe, ch, out, k_tiles, m_hi, m_lo, first=0, ready=None):
        for k in range(k_tiles):
            if ready is not None:
                ready(k)
            b = (first + k) * P
            mm = mm3(pe, out, wh[:, ch.slot, b:b + P], wl[:, ch.slot, b:b + P], m_hi(k), m_lo(k),
                     k == 0, k == k_tiles - 1)
        return mm

    def landed(pe, ch):
        pe.wait_ge(Ring.split, ch.n + 1 + LEAD)

    def products_done(eng, ch):
        eng.wait_ge(Ring.done, ch.n + 1 + LEAD)

    def ffn_pe(pe, f, l, at):
        def project(part, i, s, first=0):
            ps, freed = ((0, f.gate), (2, f.act))[part]
            ch = at(part, i * 2 + (s + first))
            landed(pe, ch)
            pe.wait_ge(freed.sem, freed(l, i * 2 + (s + first - 1)))
            column_tile(pe, ch, bank[ps + s][:, :], KD, hh_tile, hl_tile,
                        ready=lambda k: pe.wait_ge(f.norm.lo.sem, f.norm.lo(l, k + 1))).then_inc(Ring.done, 1)

        project(0, 0, 0)
        norm_pe_totals(pe, f.norm, l)
        project(1, 0, 0)
        norm_pe_spread(pe, f.norm, l)
        for part in range(2):
            project(part, 0, 1)
        with pe.Fori(0, KF // 2 - 1) as i:
            for s in range(2):
                for part in range(2):
                    project(part, i, s, first=2)
        with pe.Fori(0, KD // 2) as i:
            for s in range(2):
                pe.wait_ge(f.x.sem, f.x(l, i * 2 + (s - 1)))
                for half in range(2):
                    ch = at(2 * KF + half, i * 2 + s)
                    landed(pe, ch)
                    pe.wait_ge(f.act_lo.sem, f.act_lo(l, KH * (half + 1)))
                    for k in range(KH):
                        mm = mm3(pe, bank[4 + s][:, :], wh[:, ch.slot, k * P:(k + 1) * P],
                                 wl[:, ch.slot, k * P:(k + 1) * P], ah[:, KH * half + k, :], al[:, KH * half + k, :],
                                 half == 0 and k == 0, half == 1 and k == KH - 1)
                    mm.then_inc(Ring.done, 1)

    def ffn_act(act, f, l, gain, ready, conv):
        norm_act_squares(act, f.norm, l, x_tile, ready, end=KD - 1)
        ready(act, KD - 1)
        for k in range(KD):
            act.activation(hh[:, k, :], x[:, k, :], ACT.Copy, scale=gain(k)).then_inc(f.norm.hi.sem, 1)
        norm_act_squares(act, f.norm, l, x_tile, ready, first=KD - 1)
        norm_act_root(act, f.norm, l)
        with act.Fori(0, KF // 2) as i:
            for s in range(2):
                tile = i * 2 + s
                act.wait_ge(f.gate.sem, f.gate(l, tile + 1))
                if conv:
                    act.wait_ge(f.act.sem, f.act(l, i * 2 + (s - 1)))
                    act.activation(cv[:, s, 0:S], gs[:, s, :], ACT.Identity, bias=cpar[:, bass.ds(tile, 1), 3],
                                   scale=cpar[:, bass.ds(tile, 1), 2]).then_inc(f.conv.sem, 1)
                    act.wait_ge(f.conv.sem, f.conv(l, tile * 3 + 3))
                    act.activation(sg[:, s, :], cv[:, s, 0:S], ACT.Silu).then_inc(f.silu.sem, 1)
                else:
                    act.wait_ge(f.act.sem, f.act(l, i * 2 + (s - 1)))
                    act.activation(sg[:, s, :], gs[:, s, :], ACT.Silu).then_inc(f.silu.sem, 1)
                act.wait_ge(f.act.sem, f.act(l, tile + 1))
                act.activation(ah[:, bass.ds(tile, 1), :], af[:, s, :], ACT.Copy).then_inc(f.act_hi.sem, 1)

    def ffn_dve(v, f, l, at, gain, conv, half, next_norm, next_l, sum_last=True):
        for k in range(KD):
            v.wait_ge(f.norm.hi.sem, f.norm.hi(l, k + 1))
            v.scalar_tensor_tensor(hl[:, k, :], x[:, k, :], gain(k), f32(hh[:, k, :]), ALU.mult, ALU.subtract)\
                .then_inc(f.norm.lo.sem, 1)
        norm_dve_sum_tile(v, f.norm, l, KD - 1)
        norm_dve_inverse(v, f.norm, l)
        norm_dve_diagonals(v, f.norm, l)
        v.wait_ge(f.norm.spread.sem, f.norm.spread(l, 2))
        v.tensor_scalar(rstd_rows[:, :], bank[7][:, :], 1.0, None, ALU.mult).then_inc(f.rstd.sem, 1)
        v.wait_ge(f.rstd.sem, f.rstd(l, 1))
        gate(v, 7)
        with v.Fori(0, KF // 2) as i:
            for s in range(2):
                tile = i * 2 + s
                products_done(v, at(0, tile))
                v.tensor_tensor(gs[:, s, :], bank[s][:, :], rstd_rows[:, :], ALU.mult).then_inc(f.gate.sem, 1)
                if conv:
                    for lag in (1, 2):
                        v.wait_ge(f.conv.sem, f.conv(l, tile * 3 + lag))
                        v.scalar_tensor_tensor(cv[:, s, lag:S], gs[:, s, 0:S - lag],
                                               cpar[:, bass.ds(tile, 1), 2 - lag], cv[:, s, lag:S],
                                               ALU.mult, ALU.add).then_inc(f.conv.sem, 1)
                v.wait_ge(f.silu.sem, f.silu(l, tile + 1))
                v.tensor_tensor(sg[:, s, :], sg[:, s, :], rstd_rows[:, :], ALU.mult).then_inc(f.gated.sem, 1)
                products_done(v, at(1, tile))
                v.wait_ge(f.gated.sem, f.gated(l, tile + 1))
                v.wait_ge(f.act_hi.sem, f.act_hi(l, i * 2 + (s - 1)))
                v.tensor_tensor(af[:, s, :], sg[:, s, :], bank[2 + s][:, :], ALU.mult).then_inc(f.act.sem, 1)
                v.wait_ge(f.act_hi.sem, f.act_hi(l, tile + 1))
                v.tensor_tensor(al[:, bass.ds(tile, 1), :], af[:, s, :], f32(ah[:, bass.ds(tile, 1), :]),
                                ALU.subtract).then_inc(f.act_lo.sem, 1)

        def add(d):
            products_done(v, at(2 * KF + 1, d))
            v.scalar_tensor_tensor(x[:, d, :], bank[4 + d % 2][:, :], half, x[:, d, :], ALU.mult, ALU.add)\
                .then_inc(f.x.sem, 1)

        add_tiles(v, add, next_norm, next_l, last=sum_last)

    def attention_pe(pe, a, l, emit_score, score_banks, freed, key_tiles, emit_out, emptied):
        NB = len(score_banks)
        for s in range(a.items + AHEAD + LAG + 1):
            if s < a.items:
                pe.wait_ge(freed.sem, freed(l, s - NB + 1))
                emit_score(s // T, s % T, bank[score_banks[s % NB]]).then_inc(a.score.sem, 1)
            if AHEAD <= s < a.items + AHEAD:
                i = s - AHEAD
                pe.wait_ge(a.prob.sem, a.prob(l, i + 1))
                pe.wait_ge(a.pt_lo.sem, a.pt_lo(l, i - 1))
                for j in range(key_tiles(i % T)):
                    mm = pe.transpose(bank[2 + i % 2][:, j * P:(j + 1) * P], probs[:, i % 4, j * P:(j + 1) * P],
                                      ident[:, :])
                mm.then_inc(a.turn.sem, 1)
            if s >= T + AHEAD + LAG and (s - AHEAD - LAG) % T == 0:
                h = (s - AHEAD - LAG) // T - 1
                pe.wait_ge(a.pt_lo.sem, a.pt_lo(l, T * (h + 1)))
                pe.wait_ge(emptied.sem, emptied(l, a.outs * (h - 1)))
                emit_out(h).then_inc(a.out.sem, 1)

    def attention_act(act, a, l, scale, unmasked_banks, key_tiles, t_hi, emit_y):
        for s in range(a.items + AHEAD + LAG + 2):
            if s < a.items:
                n = key_tiles(s % T) * P
                act.wait_ge(a.neg.sem, a.neg(l, s + 1))
                act.wait_ge(a.turn.sem, a.turn(l, s - 3))
                src = probs[:, s % 4, 0:n]
                if unmasked_banks is not None:
                    src = bank[unmasked_banks[s % len(unmasked_banks)]][:, 0:n]
                act.activation(probs[:, s % 4, 0:n], src, ACT.Exp, bias=small[:, s % 4, 1:2], scale=scale,
                               accum_out=small[:, s % 4, 2:3]).then_inc(a.exp.sem, 1)
            if AHEAD <= s < a.items + AHEAD:
                i = s - AHEAD
                h, t = i // T, i % T
                n = key_tiles(t)
                act.wait_ge(a.out.sem, a.out(l, h - 1))
                act.wait_ge(a.turn.sem, a.turn(l, i + 1))
                act.activation(t_hi[h % 2][:, 0:n, t * P:(t + 1) * P],
                               bank[2 + i % 2][:, 0:n * P].rearrange("p (n q) -> p n q", n=n), ACT.Copy)\
                    .then_inc(a.pt_hi.sem, 1)
            if s >= T + AHEAD + LAG + 1 and (s - AHEAD - LAG - 1) % T == 0:
                h = (s - AHEAD - LAG - 1) // T - 1
                act.wait_ge(a.out.sem, a.out(l, h + 1))
                emit_y(h)

    def attention_dve(v, a, l, scale, score_banks, bias_of, key_tiles, t_hi, t_lo, emit_y):
        for s in range(a.items + AHEAD + LAG + 3):
            if s < a.items:
                n = key_tiles(s % T) * P
                scores = bank[score_banks[s % len(score_banks)]][:, 0:n]
                v.wait_ge(a.turn.sem, a.turn(l, s - 3))
                v.wait_ge(a.score.sem, a.score(l, s + 1))
                gate(v, 2 + s % 4)
                if bias_of is None:
                    v.tensor_reduce(small[:, s % 4, 0:1], scores, AXX, ALU.max).then_inc(a.max.sem, 1)
                else:
                    v.tensor_tensor_reduce(probs[:, s % 4, 0:n], scores, bias_of(s % T), 1.0, TAKEN,
                                           ALU.add, ALU.max, small[:, s % 4, 0:1]).then_inc(a.max.sem, 1)
                v.wait_ge(a.max.sem, a.max(l, s + 1))
                v.tensor_scalar(small[:, s % 4, 1:2], small[:, s % 4, 0:1], -scale, None, ALU.mult)\
                    .then_inc(a.neg.sem, 1)
            if 1 <= s <= a.items:
                i = s - 1
                n = key_tiles(i % T) * P
                v.wait_ge(a.exp.sem, a.exp(l, i + 1))
                v.reciprocal(small[:, i % 4, 3:4], small[:, i % 4, 2:3]).then_inc(a.inv.sem, 1)
                v.wait_ge(a.inv.sem, a.inv(l, i + 1))
                v.tensor_scalar(probs[:, i % 4, 0:n], probs[:, i % 4, 0:n], small[:, i % 4, 3:4], None, ALU.mult)\
                    .then_inc(a.prob.sem, 1)
            if AHEAD + 1 <= s <= a.items + AHEAD:
                i = s - AHEAD - 1
                h, t = i // T, i % T
                n = key_tiles(t)
                v.wait_ge(a.pt_hi.sem, a.pt_hi(l, i + 1))
                v.tensor_tensor(t_lo[h % 2][:, 0:n, t * P:(t + 1) * P],
                                bank[2 + i % 2][:, 0:n * P].rearrange("p (n q) -> p n q", n=n),
                                f32(t_hi[h % 2][:, 0:n, t * P:(t + 1) * P]), ALU.subtract).then_inc(a.pt_lo.sem, 1)
            if emit_y is not None and s >= T + AHEAD + LAG + 2 and (s - AHEAD - LAG - 2) % T == 0:
                emit_y((s - AHEAD - LAG - 2) // T - 1)

    def causal_tiles(t):
        return t + 1

    def at1(l):
        return lambda c, i=0: Chunk(0, C1, l, c, i)

    def mid_chunk(l, m):
        return Chunk(0, C1, l, 60 + m if m < 4 else 61 + m)

    def tile_chunk(j):
        return j

    CONV_TILE, IDX_TILE, SHORT_TILE = 0, 4, 15
    V_CHUNK, OUT_CHUNK, MEMK_CHUNK, MEMV_CHUNK, XQ_CHUNK, XO_CHUNK = 21, 25, 33, 41, 49, 57
    IDX_SCALE = IDXH ** -0.5 * 64 ** -0.5

    def head_rows(h):
        return slice(64 * (h % 2), 64 * (h % 2) + 64)

    def dsa_bias(t):
        return bias[:, BIAS_AT[t]:BIAS_AT[t] + (t + 1) * P]

    def kv_bank(i):
        return bank[2 + i % 2] if i < 8 else bank[(4, 5, 2, 3)[i - 8]]

    def kv_parts(i):
        if i < 8:
            return km_hi[:, i, :], km_lo[:, i, :], M
        half, mt = (i - 8) // 2, (i - 8) % 2
        return vm_hi[:, mt, half * S:(half + 1) * S], vm_lo[:, mt, half * S:(half + 1) * S], S

    def kv_chunk(l, i):
        return mid_chunk(l, MEMK_CHUNK + i if i < 8 else MEMV_CHUNK + 4 * ((i - 8) // 2) + 3)

    def mem_w_chunk(l, i):
        return mid_chunk(l, MEMK_CHUNK + i)

    def mix1_pe(pe, l):
        norm_pe(pe, mixnorm, l)

        def tile(j, ready=None):
            ch = mid_chunk(l, tile_chunk(j))
            landed(pe, ch)
            pe.wait_ge(evicted.sem, evicted(l, j - 1))
            column_tile(pe, ch, bank[j % 2][:, :], KD, hh_tile, hl_tile, ready=ready).then_inc(Ring.done, 1)

        tile(0, lambda k: pe.wait_ge(mixnorm.lo.sem, mixnorm.lo(l, k + 1)))
        for j in range(1, 4):
            tile(j)
        ch = at1(l)(64)
        landed(pe, ch)
        for k in range(KD):
            mm = mm3(pe, bank[4][0:IDXH, :], wh[:, ch.slot, 4 * k:4 * k + 4], wl[:, ch.slot, 4 * k:4 * k + 4],
                     hh[:, k, :], hl[:, k, :], k == 0, k == KD - 1)
        mm.then_inc(Ring.done, 1)
        for j in range(4, 6):
            tile(j)
        pe.wait_ge(widx_row_s.sem, widx_row_s(l, 1))
        for t in range(T):
            mm = pe.matmul(bank[5][:, 4 * t:4 * t + 4], widx_row[0:IDXH, t * P:(t + 1) * P], ident[0:IDXH, 0:IDXH],
                           start=True, stop=True)
        mm.then_inc(widx_ps.sem, 1)
        for j in range(6, 11):
            tile(j)
        for i in range(12):
            t, h = 1 + i // IDXH, i % IDXH
            r, q = head_rows(h), slice(t * P, (t + 1) * P)
            n = (t + 1) * P
            pe.wait_ge(rope1.sem, rope1(l, 15))
            pe.wait_ge(relu.sem, relu(l, i - 1))
            mm3(pe, bank[2 + i % 2][:, 0:n], ix_hi[r, h // 2, q], ix_lo[r, h // 2, q], ix_hi[r, 2, 0:n],
                ix_lo[r, 2, 0:n], True, True).then_inc(logit.sem, 1)
        for j in range(11, SHORT_TILE):
            tile(j)
        pe.wait_ge(conv1.sem, conv1(l, 2 * CONVW + 2))
        pe.wait_ge(relu.sem, relu(l, 12))
        for k in range(2):
            mm = pe.matmul(bank[2][:, :], ones[:, :], acc[:, k, :], start=(k == 0), stop=(k == 1))
        mm.then_inc(ln_mean.sem, 1)
        for j in range(SHORT_TILE, 21):
            tile(j)
        pe.wait_ge(widx_tok_s.sem, widx_tok_s(l, 1))
        for c in range(4):
            if c == 2:
                for k in range(2):
                    pe.wait_ge(ln_sq.sem, ln_sq(l, k + 1))
                    mm = pe.matmul(bank[3][:, :], ones[:, :], sq[:, k, :], start=(k == 0), stop=(k == 1))
                mm.then_inc(ln_var.sem, 1)
            ch = mid_chunk(l, V_CHUNK + c)
            landed(pe, ch)
            for kk in range(2):
                for t in range(T):
                    rows = slice(t * P, (t + 1) * P)
                    mm = mm3(pe, bank[4 + t][:, :], hh[:, 2 * c + kk, rows], hl[:, 2 * c + kk, rows],
                             wh[:, ch.slot, kk * S:(kk + 1) * S], wl[:, ch.slot, kk * S:(kk + 1) * S],
                             c == 0 and kk == 0, c == 3 and kk == 1)
            mm.then_inc(Ring.done, 1)

        pe.wait_ge(rope1.sem, rope1(l, 55))
        pe.wait_ge(evicted.sem, evicted(l, 21))
        pe.wait_ge(v_lo_s.sem, v_lo_s(l, T))
        pe.wait_ge(ln_inv.sem, ln_inv(l, 1))

        def scores(h, t, out):
            r, q = head_rows(h), slice(t * P, (t + 1) * P)
            n = (t + 1) * P
            return mm3(pe, out[:, 0:n], qk_hi[r, 4 + h // 2, q], qk_lo[r, 4 + h // 2, q], qk_hi[r, h // 2, 0:n],
                       qk_lo[r, h // 2, 0:n], True, True)

        def outputs(h):
            out = bank[4 + h % 2]
            pairs = slice(h // 2 * P, (h // 2 + 1) * P)
            for j in range(T):
                mm = mm3(pe, out[:, j * P:S], v_hi[:, j, pairs], v_lo[:, j, pairs], pt_hi[h % 2][:, j, j * P:S],
                         pt_lo[h % 2][:, j, j * P:S], j == 0, j == T - 1)
            return mm

        attention_pe(pe, dsa, l, scores, SCORE_BANKS, dsa.max, causal_tiles, outputs, dsa.y_lo)

        pe.wait_ge(dsa.y_lo.sem, dsa.y_lo(l, HEADS))
        pe.wait_ge(yab_lo.sem, yab_lo(l, 4))
        for d in range(KD):
            ch = mid_chunk(l, OUT_CHUNK + d)
            landed(pe, ch)
            pe.wait_ge(out1_x.sem, out1_x(l, d - 1))
            column_tile(pe, ch, bank[d % 2][:, :], KD, hh_tile, hl_tile).then_inc(Ring.done, 1)

    def short_conv(g, l):
        g.wait_ge(evicted.sem, evicted(l, 21))
        g.wait_ge(mixnorm.lo.sem, mixnorm.lo(l, KD))
        for k in range(2):
            g.tensor_tensor(cgate[:, k, :], cgate[:, k, :], bh[:, k, :], ALU.mult).then_inc(scin.sem, 1)
        g.wait_ge(scin.sem, scin(l, 2))

        def tap(dst, k, lag):
            c = SC0 + 2 * (2 - lag) + k
            g.tensor_tensor(dst, cgate[:, k, :], p1[:, c:c + 1].to_broadcast([P, S]), ALU.mult).then_inc(scconv.sem, 1)

        for k in range(2):
            tap(yb[:, k, :], k, 0)
        for lag in range(1, 3):
            first = 4 * lag - 2
            g.wait_ge(scconv.sem, scconv(l, first))
            for k in range(2):
                tap(hf[:, k, :], k, lag)
            for k in range(2):
                g.wait_ge(scconv.sem, scconv(l, first + k + 1))
                g.tensor_tensor(yb[:, k, lag:S], yb[:, k, lag:S], hf[:, k, 0:S - lag], ALU.add)\
                    .then_inc(scconv.sem, 1)
        g.wait_ge(scconv.sem, scconv(l, 10))
        for k in range(2):
            g.tensor_tensor(yb[:, k, :], yb[:, k, :], bgate[:, k, :], ALU.mult).then_inc(yb_s.sem, 1)

    def xat_pe(pe, l):
        def mem_key(i):
            ch = kv_chunk(l, i)
            landed(pe, ch)
            pe.wait_ge(mlo.sem, mlo(l, KD))
            pe.wait_ge(kv_lo.sem, kv_lo(l, i - 1))
            column_tile(pe, ch, kv_bank(i)[:, 0:M], KD, lambda k: mh_hi[:, k, :], lambda k: mh_lo[:, k, :])\
                .then_inc(Ring.done, 1)

        for i in range(4):
            mem_key(i)
        norm_pe_totals(pe, xanorm, l)
        for i in range(4, 8):
            mem_key(i)
        norm_pe_spread(pe, xanorm, l)
        for half in range(2):
            if half == 1:
                pe.wait_ge(kv_lo.sem, kv_lo(l, 8))
            for c in range(4):
                ch = mid_chunk(l, MEMV_CHUNK + 4 * half + c)
                landed(pe, ch)
                for kk in range(2):
                    for mt in range(MT):
                        rows = slice(mt * P, (mt + 1) * P)
                        mm = mm3(pe, kv_bank(8 + 2 * half + mt)[:, :], mh_hi[:, 2 * c + kk, rows],
                                 mh_lo[:, 2 * c + kk, rows], wh[:, ch.slot, kk * S:(kk + 1) * S],
                                 wl[:, ch.slot, kk * S:(kk + 1) * S], c == 0 and kk == 0, c == 3 and kk == 1)
                mm.then_inc(Ring.done, 1)
        for d in range(KD):
            ch = mid_chunk(l, XQ_CHUNK + d)
            landed(pe, ch)
            pe.wait_ge(qx_lo_s.sem, qx_lo_s(l, d - 1))
            column_tile(pe, ch, bank[d % 2][:, :], KD, hh_tile, hl_tile,
                        ready=lambda k: pe.wait_ge(xanorm.lo.sem, xanorm.lo(l, k + 1))).then_inc(Ring.done, 1)

        pe.wait_ge(qx_lo_s.sem, qx_lo_s(l, KD))
        pe.wait_ge(kv_lo.sem, kv_lo(l, 12))

        def scores(h, t, out):
            q = slice(t * P, (t + 1) * P)
            for e in range(2):
                mm = mm3(pe, out[:, 0:M], qx_hi[:, 2 * h + e, q], qx_lo[:, 2 * h + e, q], km_hi[:, 2 * h + e, :],
                         km_lo[:, 2 * h + e, :], e == 0, e == 1)
            return mm

        def outputs(h):
            for e in range(2):
                feats = slice((2 * h + e) * P, (2 * h + e + 1) * P)
                for j in range(MT):
                    mm = mm3(pe, bank[4 + 2 * (h % 2) + e][:, :], vm_hi[:, j, feats], vm_lo[:, j, feats],
                             xpt_hi[h % 2][:, j, :], xpt_lo[h % 2][:, j, :], j == 0, j == MT - 1)
            return mm

        attention_pe(pe, xat, l, scores, XSCORE_BANKS, xat.exp, lambda t: MT, outputs, xat.y_lo)
        pe.wait_ge(xat.y_lo.sem, xat.y_lo(l, 2 * XH))
        for d in range(KD):
            ch = mid_chunk(l, XO_CHUNK + d)
            landed(pe, ch)
            pe.wait_ge(wo_x.sem, wo_x(l, d - 1))
            column_tile(pe, ch, bank[d % 2][:, :], KD, hh_tile, hl_tile).then_inc(Ring.done, 1)

    def mix1_act(act, l):
        norm_act(act, mixnorm, l, x_tile, lambda a, k: a.wait_ge(ffn1.x.sem, ffn1.x(l, k + 1)), hh_tile)
        def evict(j):
            products_done(act, mid_chunk(l, tile_chunk(j)))
            rotary = j - IDX_TILE if IDX_TILE <= j < SHORT_TILE else None
            if j < IDX_TILE:
                dst = (aval, asig)[j % 2][:, j // 2, :]
            elif rotary is None:
                dst = (cgate, bh, bgate)[(j - SHORT_TILE) // 2][:, (j - SHORT_TILE) % 2, :]
            elif rotary < 3:
                dst = ix_raw[:, rotary, :]
            else:
                dst = qk_raw[:, rotary - 3, :]
            func = ACT.Sigmoid if j in (1, 3) else ACT.Copy
            act.activation(dst, bank[j % 2][:, :], func).then_inc(evicted.sem, 1)
            if rotary is not None:
                act.wait_ge(evicted.sem, evicted(l, j + 1))
                swapped = ix_swap[:, rotary, :] if rotary < 3 else qk_swap[:, rotary - 3, :]
                swap_halves(act, swapped, dst, 32, swap1[rotary].sem)

        for j in range(4):
            evict(j)
        products_done(act, at1(l)(64))
        act.activation(widx_row[0:IDXH, :], bank[4][0:IDXH, :], ACT.Copy, scale=IDX_SCALE).then_inc(widx_row_s.sem, 1)
        for j in range(4, 7):
            evict(j)
        act.wait_ge(widx_ps.sem, widx_ps(l, 1))
        act.activation(widx_tok[:, :], bank[5][:, 0:16], ACT.Copy).then_inc(widx_tok_s.sem, 1)
        for j in range(7, 11):
            evict(j)
        for i in range(12):
            n = (2 + i // IDXH) * P
            act.wait_ge(logit.sem, logit(l, i + 1))
            act.wait_ge(score.sem, score(l, i - 1))
            act.activation(rbuf[:, i % 2, 0:n], bank[2 + i % 2][:, 0:n], ACT.Relu).then_inc(relu.sem, 1)
        act.wait_ge(score.sem, score(l, 12))
        for j in range(11, 21):
            evict(j)
        for k in range(2):
            act.wait_ge(ln_dev.sem, ln_dev(l, k + 1))
            act.activation(sq[:, k, :], acc[:, k, :], ACT.Square).then_inc(ln_sq.sem, 1)
        act.wait_ge(ln_inv.sem, ln_inv(l, 1))
        act.activation(asig[:, 1, :], asig[:, 0, :], ACT.Ln).then_inc(ln_rstd.sem, 1)
        act.wait_ge(ln_rstd.sem, ln_rstd(l, 1))
        act.activation(aval[:, 0, :], asig[:, 1, :], ACT.Exp, scale=-0.5).then_inc(ln_rstd.sem, 1)
        act.wait_ge(par1_in.sem, par1_in(l, 16))
        for k in range(2):
            act.wait_ge(ln_y.sem, ln_y(l, k + 1))
            act.activation(acc[:, k, :], acc[:, k, :], ACT.Silu, bias=p1[:, LB0 + k:LB0 + k + 1],
                           scale=p1[:, LG0 + k:LG0 + k + 1]).then_inc(ya.sem, 1)
        products_done(act, mid_chunk(l, V_CHUNK + 3))
        for t in range(T):
            act.activation(v_hi[:, t, :], bank[4 + t][:, :], ACT.Copy).then_inc(v_hi_s.sem, 1)
        act.wait_ge(ya.sem, ya(l, 2))
        for k in range(2):
            act.activation(hh[:, k, :], acc[:, k, :], ACT.Copy).then_inc(yab_hi.sem, 1)
        for k in range(2):
            act.wait_ge(yb_s.sem, yb_s(l, k + 1))
            act.activation(hh[:, 2 + k, :], yb[:, k, :], ACT.Copy).then_inc(yab_hi.sem, 1)
        act.wait_ge(yab_lo.sem, yab_lo(l, 4))

        def out_hi(h):
            r = head_rows(h)
            act.activation(hh[r, 4 + h // 2, :], bank[4 + h % 2][r, :], ACT.Copy).then_inc(dsa.y_hi.sem, 1)

        attention_act(act, dsa, l, 64 ** -0.5, None, causal_tiles, pt_hi, out_hi)

    def xat_act(act, l):
        for k in range(KD):
            act.wait_ge(mscaled.sem, mscaled(l, k + 1))
            act.activation(mh_hi[:, k, :], mf[:, k % 2, :], ACT.Copy).then_inc(mhi.sem, 1)

        def ready(a, k):
            if k == KD - 1:
                takes_over(a, mem_w_chunk(l, 1))
                split_hi(a, mem_w_chunk(l, 1))
            a.wait_ge(out1_x.sem, out1_x(l, k + 1))

        norm_act_squares(act, xanorm, l, x_tile, ready)

        def kv(i):
            if i < 8:
                split_hi(act, mem_w_chunk(l, i + 2))
            hi, _, n = kv_parts(i)
            products_done(act, kv_chunk(l, i))
            act.activation(hi, kv_bank(i)[:, 0:n], ACT.Copy).then_inc(kv_hi.sem, 1)

        for i in range(4):
            kv(i)
        norm_act_root(act, xanorm, l)
        for i in range(4, 8):
            kv(i)
        norm_act_hi(act, xanorm, l, hh_tile,
                    between=lambda k: split_hi(act, mem_w_chunk(l, 10 + k)) if k < KD - 1 else None)
        for i in range(8, 12):
            kv(i)
        for d in range(KD):
            products_done(act, mid_chunk(l, XQ_CHUNK + d))
            act.activation(qx_hi[:, d, :], bank[d % 2][:, :], ACT.Copy).then_inc(qx_hi_s.sem, 1)

        def out_hi(h):
            for e in range(2):
                act.activation(hh[:, 2 * h + e, :], bank[4 + 2 * (h % 2) + e][:, :], ACT.Copy)\
                    .then_inc(xat.y_hi.sem, 1)

        attention_act(act, xat, l, 256 ** -0.5, XSCORE_BANKS, lambda t: MT, xpt_hi, out_hi)

    def rotate(v, raw_tile, swapped, cos, sin, tmp, hi, lo, sem, n, ready):
        v.tensor_tensor(tmp[:, 0, :], raw_tile, cos, ALU.mult).then_inc(sem, 1)
        ready()
        v.tensor_tensor(tmp[:, 1, :], swapped, sin, ALU.mult).then_inc(sem, 1)
        v.wait_ge(sem, n + 2)
        v.tensor_tensor(tmp[:, 2, :], tmp[:, 0, :], tmp[:, 1, :], ALU.add).then_inc(sem, 1)
        v.wait_ge(sem, n + 3)
        v.tensor_scalar(hi, tmp[:, 2, :], 1.0, None, ALU.mult).then_inc(sem, 1)
        v.wait_ge(sem, n + 4)
        return v.tensor_tensor(lo, tmp[:, 2, :], f32(hi), ALU.subtract)

    def mix1_dve(v, l):
        norm_dve(v, mixnorm, l, x_tile, lambda k: par1_at(1, k), hh_tile, hl_tile)
        v.wait_ge(tab_sin, 2)

        def rope(j):
            hi = ix_hi[:, j, :] if j < 3 else qk_hi[:, j - 3, :]
            lo = ix_lo[:, j, :] if j < 3 else qk_lo[:, j - 3, :]
            raw_tile = ix_raw[:, j, :] if j < 3 else qk_raw[:, j - 3, :]
            swapped = ix_swap[:, j, :] if j < 3 else qk_swap[:, j - 3, :]
            v.wait_ge(evicted.sem, evicted(l, IDX_TILE + j + 1))
            rotate(v, raw_tile, swapped, cos1[:, :], sin1[:, :], rt, hi, lo, rope1.sem,
                   rope1(l, 5 * j), lambda: v.wait_ge(swap1[j].sem, swap1[j](l, 64))).then_inc(rope1.sem, 1)

        v.memset(xpad[:, :, 0:CONVW - 1], 0.0).then_inc(glu.sem, 1)
        for k in range(2):
            first = k * (CONVW + 1)
            v.wait_ge(evicted.sem, evicted(l, 2 * k + 2))
            v.tensor_tensor(xpad[:, k, CONVW - 1:], aval[:, k, :], asig[:, k, :], ALU.mult).then_inc(glu.sem, 1)
            v.wait_ge(glu.sem, glu(l, k + 2))
            for j in range(CONVW):
                w = p1[:, CW0 + 2 * j + k:CW0 + 2 * j + k + 1]
                part = acc[:, k, :] if j % 2 == 0 else rt[:, k, :]
                if j == 0:
                    v.tensor_scalar(part, xpad[:, k, 0:S], w, p1[:, CB0 + k:CB0 + k + 1], ALU.mult, ALU.add)\
                        .then_inc(conv1.sem, 1)
                elif j == 1:
                    v.tensor_scalar(part, xpad[:, k, 1:1 + S], w, None, ALU.mult).then_inc(conv1.sem, 1)
                else:
                    v.wait_ge(conv1.sem, conv1(l, first + j - 1))
                    v.scalar_tensor_tensor(part, xpad[:, k, j:j + S], w, part, ALU.mult, ALU.add).then_inc(conv1.sem, 1)
            v.wait_ge(conv1.sem, conv1(l, first + CONVW))
            v.tensor_tensor(acc[:, k, :], acc[:, k, :], rt[:, k, :], ALU.add).then_inc(conv1.sem, 1)
        v.wait_ge(conv1.sem, conv1(l, 2 * CONVW + 2))
        for j in range(3):
            rope(j)
        v.wait_ge(widx_tok_s.sem, widx_tok_s(l, 1))
        for i in range(12):
            t, h = 1 + i // IDXH, i % IDXH
            n = (t + 1) * P
            w = widx_tok[:, 4 * t + h:4 * t + h + 1]
            v.wait_ge(relu.sem, relu(l, i + 1))
            if h == 0:
                v.tensor_scalar(dsa_bias(t), rbuf[:, i % 2, 0:n], w, None, ALU.mult).then_inc(score.sem, 1)
            else:
                v.wait_ge(score.sem, score(l, i))
                v.scalar_tensor_tensor(dsa_bias(t), rbuf[:, i % 2, 0:n], w, dsa_bias(t), ALU.mult, ALU.add)\
                    .then_inc(score.sem, 1)
        v.wait_ge(score.sem, score(l, 12))
        for t in range(1, T):
            diag = bias[:, BIAS_AT[t] + t * P:BIAS_AT[t] + (t + 1) * P]
            v.tensor_tensor(diag, diag, causal[:, 3 * P:S], ALU.add).then_inc(cut.sem, 1)
        v.wait_ge(cut.sem, cut(l, 3))
        gate(v, 1)
        with v.Fori(0, ROUNDS) as r:
            v.wait_ge(topk.sem, topk(l, r * 6))
            gate(v, 0)
            for t in range(1, T):
                v.max(best[:, 8 * (t - 1):8 * t], dsa_bias(t)).then_inc(topk.sem, 1)
            v.wait_ge(topk.sem, topk(l, r * 6 + 3))
            gate(v, 0)
            for t in range(1, T):
                v.match_replace(dsa_bias(t), best[:, 8 * (t - 1):8 * t], dsa_bias(t), TAKEN).then_inc(topk.sem, 1)
        v.tensor_scalar(dsa_bias(0), causal[:, 3 * P:S], 1.0, None, ALU.mult).then_inc(bias_s.sem, 1)
        v.wait_ge(topk.sem, topk(l, 3 * 2 * ROUNDS))
        for t in range(1, T):
            v.tensor_scalar(dsa_bias(t), dsa_bias(t), TAKEN_BELOW, MASKED, ALU.is_gt, ALU.mult)\
                .then_inc(bias_s.sem, 1)
        v.wait_ge(ln_mean.sem, ln_mean(l, 1))
        for k in range(2):
            v.scalar_tensor_tensor(acc[:, k, :], bank[2][:, :], -1.0 / 256, acc[:, k, :], ALU.mult, ALU.add)\
                .then_inc(ln_dev.sem, 1)
        for j in range(3, 7):
            rope(j)
        v.wait_ge(ln_var.sem, ln_var(l, 1))
        v.tensor_scalar(asig[:, 0, :], bank[3][:, :], 1.0 / 256, 1e-5, ALU.mult, ALU.add).then_inc(ln_inv.sem, 1)
        for j in range(7, 9):
            rope(j)
        v.wait_ge(ln_rstd.sem, ln_rstd(l, 2))
        refine_root(v, aval[:, 0, :], asig[:, 0, :], asig[:, 1, :], ln_inv.sem, ln_inv(l, 1))
        for k in range(2):
            v.tensor_tensor(acc[:, k, :], acc[:, k, :], aval[:, 0, :], ALU.mult).then_inc(ln_y.sem, 1)
        for j in range(9, 11):
            rope(j)
        for t in range(T):
            v.wait_ge(v_hi_s.sem, v_hi_s(l, t + 1))
            v.tensor_tensor(v_lo[:, t, :], bank[4 + t][:, :], f32(v_hi[:, t, :]), ALU.subtract)\
                .then_inc(v_lo_s.sem, 1)
        for k in range(4):
            v.wait_ge(yab_hi.sem, yab_hi(l, k + 1))
            v.wait_ge(yb_s.sem, yb_s(l, 2))
            v.tensor_tensor(hl[:, k, :], acc[:, k, :] if k < 2 else yb[:, k - 2, :], f32(hh[:, k, :]), ALU.subtract)\
                .then_inc(yab_lo.sem, 1)
        v.wait_ge(bias_s.sem, bias_s(l, 4))
        v.wait_ge(yab_lo.sem, yab_lo(l, 4))

        def out_lo(h):
            r = head_rows(h)
            v.wait_ge(dsa.y_hi.sem, dsa.y_hi(l, h + 1))
            v.tensor_tensor(hl[r, 4 + h // 2, :], bank[4 + h % 2][r, :], f32(hh[r, 4 + h // 2, :]), ALU.subtract)\
                .then_inc(dsa.y_lo.sem, 1)

        attention_dve(v, dsa, l, 64 ** -0.5, SCORE_BANKS, dsa_bias, causal_tiles, pt_hi, pt_lo, out_lo)

    def xat_dve(v, l):
        def mem_lo(k):
            v.wait_ge(mhi.sem, mhi(l, k + 1))
            v.tensor_tensor(mh_lo[:, k, :], mf[:, k % 2, :], f32(mh_hi[:, k, :]), ALU.subtract).then_inc(mlo.sem, 1)

        for k in range(KD):
            v.wait_ge(mlo.sem, mlo(l, max(k - 1, 0)))
            v.tensor_scalar(mf[:, k % 2, :], memn[:, k, :], par1_at(3, k), None, ALU.mult).then_inc(mscaled.sem, 1)
            if k >= 1:
                mem_lo(k - 1)
        mem_lo(KD - 1)

        def add_mix(d):
            products_done(v, mid_chunk(l, OUT_CHUNK + d))
            v.tensor_tensor(x[:, d, :], x[:, d, :], bank[d % 2][:, :], ALU.add).then_inc(out1_x.sem, 1)
            if d == KD - 1:
                split_lo(v, mem_w_chunk(l, 1))

        add_tiles(v, add_mix, xanorm, l)

        def kv(i):
            if i < 8:
                split_lo(v, mem_w_chunk(l, i + 2))
            hi, lo, n = kv_parts(i)
            v.wait_ge(kv_hi.sem, kv_hi(l, i + 1))
            v.tensor_tensor(lo, kv_bank(i)[:, 0:n], f32(hi), ALU.subtract).then_inc(kv_lo.sem, 1)

        for i in range(4):
            kv(i)
        norm_dve_inverse(v, xanorm, l)
        norm_dve_diagonals(v, xanorm, l)
        for i in range(4, 8):
            kv(i)
        norm_dve_scale(v, xanorm, l, x_tile, lambda k: par1_at(2, k), hh_tile, hl_tile,
                       between=lambda k: split_lo(v, mem_w_chunk(l, 10 + k)) if k < KD - 1 else None)
        for i in range(8, 12):
            kv(i)
        for d in range(KD):
            v.wait_ge(qx_hi_s.sem, qx_hi_s(l, d + 1))
            v.tensor_tensor(qx_lo[:, d, :], bank[d % 2][:, :], f32(qx_hi[:, d, :]), ALU.subtract)\
                .then_inc(qx_lo_s.sem, 1)

        def out_lo(h):
            for e in range(2):
                v.wait_ge(xat.y_hi.sem, xat.y_hi(l, 2 * h + e + 1))
                v.tensor_tensor(hl[:, 2 * h + e, :], bank[4 + 2 * (h % 2) + e][:, :], f32(hh[:, 2 * h + e, :]),
                                ALU.subtract).then_inc(xat.y_lo.sem, 1)

        attention_dve(v, xat, l, 256 ** -0.5, XSCORE_BANKS, None, lambda t: MT, xpt_hi, xpt_lo, out_lo)

        def add_cross(d):
            products_done(v, mid_chunk(l, XO_CHUNK + d))
            v.tensor_tensor(x[:, d, :], x[:, d, :], bank[d % 2][:, :], ALU.add).then_inc(wo_x.sem, 1)

        add_tiles(v, add_cross, ffn2norm, l, last=False)

    def mix2_chunk(l, m):
        return Chunk(L * C1, C2, l, m)

    def z_chunk(j):
        return j if j < 11 else j + 4

    VZ_CHUNK, U_CHUNK, OUT2_CHUNK = 11, 19, 24
    U_BANK = (0, 1, 2, 3, 0, 1, 4, 5, 6, 7, 2, 3, 0, 1)
    QK = DK ** -0.5
    FAR = [(0, 1), (1, 2), (2, 3), (0, 2), (1, 3), (0, 3)]

    def u_chunk(l, i):
        return mix2_chunk(l, U_CHUNK + (0, 0, 1, 1, 2, 2, 3, 3, 3, 3, 4, 4, 4, 4)[i])

    def u_parts(i):
        if i < 4:
            return qn_hi[:, i, :], qn_lo[:, i, :]
        if i < 6:
            return qr_hi[:, i - 4, :], qr_lo[:, i - 4, :]
        if i < 10:
            return kn_hi[:, i - 6, :], kn_lo[:, i - 6, :]
        return vm2_hi[:, i - 10, :], vm2_lo[:, i - 10, :]

    def key_rows(h):
        return slice(DK * h, DK * (h + 1))

    def pair_rows(a, h):
        return pair[:, FIRST_BLOCK[a]:FIRST_BLOCK[a] + T - a, h, :]

    def score_banks(n):
        return banks[:, 4 * (n % 2):4 * (n % 2) + MH, 0:P]

    def mix2_pe(pe, l):
        norm_pe(pe, attnorm, l)

        def tile(j):
            ch = mix2_chunk(l, z_chunk(j))
            landed(pe, ch)
            pe.wait_ge(z_ev.sem, z_ev(l, j - 1))
            column_tile(pe, ch, bank[j % 2][:, :], KD, hh_tile, hl_tile,
                        ready=lambda k: pe.wait_ge(attnorm.lo.sem, attnorm.lo(l, k + 1))).then_inc(Ring.done, 1)

        for j in range(6):
            tile(j)
        pe.wait_ge(tables2_in.sem, tables2_in(l, 16 * 8))
        pe.wait_ge(z_ev.sem, z_ev(l, 1))
        pe.matmul(bank[7][:, :], gw[0:16, :], glr[0:16, :], start=True, stop=True).then_inc(gk_ps.sem, 1)
        for j in range(6, 11):
            tile(j)
        for c in range(4):
            ch = mix2_chunk(l, VZ_CHUNK + c)
            landed(pe, ch)
            for kk in range(2):
                for t in range(T):
                    rows = slice(t * P, (t + 1) * P)
                    mm = mm3(pe, bank[2 + t][:, :], hh[:, 2 * c + kk, rows], hl[:, 2 * c + kk, rows],
                             wh[:, ch.slot, kk * S:(kk + 1) * S], wl[:, ch.slot, kk * S:(kk + 1) * S],
                             c == 0 and kk == 0, c == 3 and kk == 1)
            mm.then_inc(Ring.done, 1)
        norm_pe_totals(pe, cqnorm, l)
        tile(11)
        pe.wait_ge(gk_dve.sem, gk_dve(l, 1))
        norm_pe_spread(pe, cqnorm, l)
        tile(12)
        norm_pe_totals(pe, cknorm, l)
        tile(13)
        pe.wait_ge(cqnorm.scaled.sem, cqnorm.scaled(l, 3))
        norm_pe_spread(pe, cknorm, l)
        tile(14)

        def key_query(n, k_tile, q_tile):
            for h in range(MH):
                r = key_rows(h)
                mm = pe.matmul(score_banks(n)[:, h, :], k_tile(r), q_tile(r), start=True, stop=True)
            return mm

        def values(v0, done, out_sig):
            for h in range(MH):
                for a in range(T):
                    mm = pe.matmul(bank[4 + h][:, a * P:S], vgr[:, a, v0 + h // 2 * P:v0 + (h // 2 + 1) * P],
                                   pair_rows(a, h), start=(a == 0), stop=(a == T - 1))
                mm.then_inc(out_sig.sem, 1)

        pe.wait_ge(vz_ev.sem, vz_ev(l, T))
        pe.wait_ge(z_ev.sem, z_ev(l, 15))
        pe.wait_ge(cknorm.scaled.sem, cknorm.scaled(l, 2))
        pe.wait_ge(rrope.sem, rrope(l, 6))
        for b, (a, c) in enumerate(BLOCKS):
            pe.wait_ge(ret_at.sem, ret_at(l, b - 1))
            key_query(b, lambda r: rqk[r, 1, a * P:(a + 1) * P], lambda r: rqk[r, 0, c * P:(c + 1) * P])\
                .then_inc(ret_ps.sem, 1)
        pe.wait_ge(ret_at.sem, ret_at(l, len(BLOCKS)))
        values(2 * P, ret_at, ret_out)
        pe.wait_ge(ret_y.sem, ret_y(l, MH))
        for lv in range(LEVELS):
            pe.wait_ge(lev_q.sem, lev_q(l, 2 * (lv + 1)))
            for a in range(T):
                n = lv * T + a
                pe.wait_ge(lev_at.sem, lev_at(l, n - 1))
                rows = slice(a * P, (a + 1) * P)
                key_query(n, lambda r: ke[r, lv % 2, rows], lambda r: qe[r, lv % 2, rows])\
                    .then_inc(lev_ps.sem, 1)
        pe.wait_ge(lev_at.sem, lev_at(l, LEVELS * T))
        pe.wait_ge(lev_q.sem, lev_q(l, 18))
        pe.wait_ge(k3_s.sem, k3_s(l, 3))
        for n, (a, c) in enumerate(FAR):
            pe.wait_ge(far_at.sem, far_at(l, n - 1))
            key = (lambda r: ke[r, 0, a * P:(a + 1) * P]) if c == a + 1 else (lambda r: k3[r, (0, 1, 2)[n - 3], :])
            key_query(n, key, lambda r: qe[r, 0, c * P:(c + 1) * P]).then_inc(far_ps.sem, 1)
        pe.wait_ge(far_at.sem, far_at(l, len(FAR)))
        values(0, far_at, gla_out)
        pe.wait_ge(cqnorm.lo.sem, cqnorm.lo(l, 3))
        for c in range(3):
            ch = mix2_chunk(l, U_CHUNK + c)
            landed(pe, ch)
            if c == 2:
                pe.wait_ge(u_lo.sem, u_lo(l, 2))
            for e in range(2):
                mm = column_tile(pe, ch, bank[U_BANK[2 * c + e]][:, :], 3, lambda k: cq_hi[:, k, :],
                                 lambda k: cq_lo[:, k, :], first=3 * e)
            mm.then_inc(Ring.done, 1)
        pe.wait_ge(cknorm.lo.sem, cknorm.lo(l, 2))
        pe.wait_ge(gla_y.sem, gla_y(l, MH))
        ch = mix2_chunk(l, U_CHUNK + 3)
        landed(pe, ch)
        for e in range(4):
            mm = column_tile(pe, ch, bank[4 + e][:, :], 2, lambda k: ck_hi[:, k, :], lambda k: ck_lo[:, k, :],
                             first=2 * e)
        mm.then_inc(Ring.done, 1)
        ch = mix2_chunk(l, U_CHUNK + 4)
        landed(pe, ch)
        pe.wait_ge(u_lo.sem, u_lo(l, 6))
        for t in range(T):
            rows = slice(t * P, (t + 1) * P)
            for k in range(2):
                mm = mm3(pe, bank[U_BANK[10 + t]][:, :], ck_hi[:, k, rows], ck_lo[:, k, rows],
                         wh[:, ch.slot, k * S:(k + 1) * S], wl[:, ch.slot, k * S:(k + 1) * S], k == 0, k == 1)
        mm.then_inc(Ring.done, 1)

        pe.wait_ge(u_lo.sem, u_lo(l, 14))
        pe.wait_ge(krrope.sem, krrope(l, 5))

        def scores(h, t, out):
            r, q = head_rows(h), slice(t * P, (t + 1) * P)
            n = (t + 1) * P
            mm3(pe, out[:, 0:n], qn_hi[:, h, q], qn_lo[:, h, q], kn_hi[:, h, 0:n], kn_lo[:, h, 0:n], True, False)
            return mm3(pe, out[:, 0:n], qr_hi[r, h // 2, q], qr_lo[r, h // 2, q], kr_hi[r, 0:n], kr_lo[r, 0:n],
                       False, True)

        def outputs(h):
            feats = slice(h * P, (h + 1) * P)
            for j in range(T):
                mm = mm3(pe, bank[4 + h % 2][:, j * P:S], vm2_hi[:, j, feats], vm2_lo[:, j, feats],
                         mpt_hi[h % 2][:, j, j * P:S], mpt_lo[h % 2][:, j, j * P:S], j == 0, j == T - 1)
            return mm

        attention_pe(pe, mla, l, scores, SCORE_BANKS, mla.max, causal_tiles, outputs, mla.y_hi)
        for k in range(KD):
            pe.wait_ge(hs_sq.sem, hs_sq(l, k + 1))
            for t in range(T):
                rows = slice(t * P, (t + 1) * P)
                if k < 4:
                    mm = pe.matmul(bank[6][:, 4 * k + t:4 * k + t + 1], sq[:, k % 2, rows], ones[:, 0:1],
                                   start=True, stop=True)
                else:
                    c = 16 + 8 * (k - 4) + 2 * t
                    mm = pe.matmul(bank[6][:, c:c + 2], sq[:, k % 2, rows], halfcol[:, :], start=True, stop=True)
            mm.then_inc(hs_tot.sem, 1)
        pe.wait_ge(mla.pt_lo.sem, mla.pt_lo(l, mla.items))
        for k in range(KD):
            pe.wait_ge(hs_dg.sem, hs_dg(l, k + 1))
            pe.wait_ge(hs_n.sem, hs_n(l, k - 1))
            for t in range(T):
                out = bank[2 + k % 2][:, t * P:(t + 1) * P]
                if k < 4:
                    mm = pe.matmul(out, ones[:, :], dg[:, k % 2, t, :], start=True, stop=True)
                else:
                    pe.matmul(out, halves[:, 0, :], dg[:, k % 2, 2 * t, :], start=True, stop=False)
                    mm = pe.matmul(out, halves[:, 1, :], dg[:, k % 2, 2 * t + 1, :], start=False, stop=True)
            mm.then_inc(hs_bc.sem, 1)
        for d in range(KD):
            ch = mix2_chunk(l, OUT2_CHUNK + d)
            landed(pe, ch)
            pe.wait_ge(out2_x.sem, out2_x(l, d - 1))
            column_tile(pe, ch, bank[d % 2][:, :], KD, hh_tile, hl_tile,
                        ready=lambda k: pe.wait_ge(hs_lo.sem, hs_lo(l, k + 1))).then_inc(Ring.done, 1)

    def mix2_act(act, l):
        norm_act(act, attnorm, l, x_tile, lambda a, k: a.wait_ge(ffn3.x.sem, ffn3.x(l, k + 1 - KD)), hh_tile)

        def evict(j):
            products_done(act, mix2_chunk(l, z_chunk(j)))
            dst = (glr[:, :], gqk[:, 0, :], gqk[:, 1, :], rqk[:, 0, :], rqk[:, 1, :], kr_raw[:, :], cq[:, 0, :],
                   cq[:, 1, :], cq[:, 2, :], ckv[:, 0, :], ckv[:, 1, :], gates[:, 0, :], gates[:, 1, :],
                   gates[:, 2, :], gates[:, 3, :])[j]
            act.activation(dst, bank[j % 2][:, :], ACT.Silu if j >= 11 else ACT.Copy).then_inc(z_ev.sem, 1)

        for j in range(6):
            evict(j)
            if j == 4:
                act.wait_ge(z_ev.sem, z_ev(l, 5))
                swap_halves(act, rswap, rqk, DK // 2, rswap_s.sem)
            if j == 5:
                act.wait_ge(z_ev.sem, z_ev(l, 6))
                swap_halves(act, kr_swap, kr_raw, 32, krswap_s.sem)
        for j in range(6, 11):
            evict(j)
        act.wait_ge(gk_dve.sem, gk_dve(l, 2))
        act.activation(zb[:, 1, :], zb[:, 1, :], ACT.Exp).then_inc(gk_act.sem, 1)
        act.wait_ge(gk_act.sem, gk_act(l, 1))
        act.activation(zb[:, 1, :], zb[:, 1, :], ACT.Ln, bias=one[:, 0:1]).then_inc(gk_act.sem, 1)
        norm_act_squares(act, cqnorm, l, lambda k: cq[:, k, :], lambda a, k: a.wait_ge(z_ev.sem, z_ev(l, 7 + k)))
        products_done(act, mix2_chunk(l, VZ_CHUNK + 3))
        for t in range(T):
            act.activation(vgr[:, t, :], bank[2 + t][:, :], ACT.Copy).then_inc(vz_ev.sem, 1)
        norm_act_root(act, cqnorm, l)
        norm_act_squares(act, cknorm, l, lambda k: ckv[:, k, :], lambda a, k: a.wait_ge(z_ev.sem, z_ev(l, 10 + k)))
        evict(11)
        norm_act_hi(act, cqnorm, l, lambda k: cq_hi[:, k, :])
        evict(12)
        norm_act_root(act, cknorm, l)
        evict(13)
        norm_act_hi(act, cknorm, l, lambda k: ck_hi[:, k, :])
        evict(14)

        def decay_exp(n):
            if n < 7:
                act.wait_ge(lev_d.sem, lev_d(l, 2 * n + 2))
                src = diff[:, n % 2, :]
            else:
                act.wait_ge(lev_d.sem, lev_d(l, 15))
                src = diff[:, 1, :] if n == 7 else cum[:, :]
            if n >= 2:
                act.wait_ge(lev_q.sem, lev_q(l, 2 * (min(n, 7) - 1)))
            act.activation(edec[:, n % 2, :], src, ACT.Exp, scale=1.0 / 16).then_inc(lev_e.sem, 1)

        def branch_out(h, tile, done, evicted_sig):
            r = head_rows(h)
            act.wait_ge(done.sem, done(l, h + 1))
            act.activation(yf[r, tile + h // 2, :], bank[4 + h][r, :], ACT.Copy).then_inc(evicted_sig.sem, 1)

        decay_exp(0)
        decay_exp(1)
        for h in range(MH):
            branch_out(h, 6, ret_out, ret_y)
        for n in range(2, 9):
            decay_exp(n)
        act.activation(etot[:, :], cum[:, P - 1:S:P], ACT.Exp, scale=1.0 / 16).then_inc(etot_s.sem, 1)
        for n, (a, c) in enumerate(FAR):
            act.wait_ge(far_ps.sem, far_ps(l, n + 1))
            act.activation(pair[:, FIRST_BLOCK[a] + c - a, :, :],
                           score_banks(n), ACT.Copy).then_inc(far_at.sem, 1)
        for h in range(MH):
            branch_out(h, 4, gla_out, gla_y)
        for i in range(14):
            products_done(act, u_chunk(l, i))
            dst = qr_raw[:, i - 4, :] if i in (4, 5) else u_parts(i)[0]
            act.activation(dst, bank[U_BANK[i]][:, :], ACT.Copy).then_inc(u_hi.sem, 1)
            if i in (4, 5):
                act.wait_ge(u_hi.sem, u_hi(l, i + 1))
                swap_halves(act, qr_swap[:, i - 4, :], qr_raw[:, i - 4, :], 32, qrswap_s[i - 4].sem)

        def out_plain(h):
            act.activation(yf[:, h, :], bank[4 + h % 2][:, :], ACT.Copy).then_inc(mla.y_hi.sem, 1)

        attention_act(act, mla, l, (128 + 64) ** -0.5, None, causal_tiles, mpt_hi, out_plain)
        act.wait_ge(mla.y_hi.sem, mla.y_hi(l, MH))
        act.wait_ge(gla_y.sem, gla_y(l, MH))
        act.wait_ge(ret_y.sem, ret_y(l, MH))
        for k in range(KD):
            act.wait_ge(hs_tot.sem, hs_tot(l, k - 1))
            act.activation(sq[:, k % 2, :], yf[:, k, :], ACT.Square).then_inc(hs_sq.sem, 1)
        act.wait_ge(hs_inv.sem, hs_inv(l, 1))
        act.activation(st[:, 2, :], st[:, 1, :], ACT.Sqrt).then_inc(hs_rstd.sem, 1)
        for k in range(KD):
            if k < 4:
                act.wait_ge(hs_n.sem, hs_n(l, k + 1))
            else:
                act.wait_ge(hs_g.sem, hs_g(l, k - 3))
            act.activation(hh[:, k, :], hf[:, k % 2, :], ACT.Copy).then_inc(hs_hi.sem, 1)

    def mix2_dve(v, l):
        norm_dve(v, attnorm, l, x_tile, lambda k: p2[:, k:k + 1], hh_tile, hl_tile)
        v.wait_ge(tables2_in.sem, tables2_in(l, 16 * 8))
        v.wait_ge(gk_ps.sem, gk_ps(l, 1))
        v.tensor_scalar(zb[:, 0, :], bank[7][:, :], p2[:, GB0:GB0 + 1], None, ALU.add).then_inc(gk_dve.sem, 1)
        v.wait_ge(gk_dve.sem, gk_dve(l, 1))
        v.scalar_tensor_tensor(zb[:, 1, :], zb[:, 0, :], -1.0, zb[:, 0, :], ALU.mult, ALU.min)\
            .then_inc(gk_dve.sem, 1)
        v.wait_ge(rswap_s.sem, rswap_s(l, 16 * 8))
        for e in range(2):
            v.wait_ge(z_ev.sem, z_ev(l, 5))
            if e == 1:
                v.wait_ge(rrope.sem, rrope(l, 3))
            v.tensor_tensor(rt[:, 0, :], rqk[:, e, :], rcos[:, :], ALU.mult).then_inc(rrope.sem, 1)
            v.tensor_tensor(rt[:, 1, :], rswap[:, e, :], rsin[:, :], ALU.mult).then_inc(rrope.sem, 1)
            v.wait_ge(rrope.sem, rrope(l, 3 * e + 2))
            v.tensor_tensor(rqk[:, e, :], rt[:, 0, :], rt[:, 1, :], ALU.add).then_inc(rrope.sem, 1)
        v.wait_ge(z_ev.sem, z_ev(l, 6))
        v.wait_ge(rrope.sem, rrope(l, 6))
        rotate(v, kr_raw[:, :], kr_swap[:, :], mcos[:, :], msin[:, :], rt, kr_hi[:, :], kr_lo[:, :], krrope.sem,
               krrope(l, 0), lambda: v.wait_ge(krswap_s.sem, krswap_s(l, 64))).then_inc(krrope.sem, 1)
        v.wait_ge(gk_act.sem, gk_act(l, 2))
        v.scalar_tensor_tensor(zb[:, 0, :], zb[:, 0, :], 0.0, zb[:, 1, :], ALU.min, ALU.subtract)\
            .then_inc(gk_dve.sem, 1)
        v.wait_ge(gk_dve.sem, gk_dve(l, 3))
        v.tensor_tensor_scan(cum[:, :], scanmask[:, :], zb[:, 0, :], 0.0, ALU.mult, ALU.add).then_inc(gk_dve.sem, 1)
        norm_dve_sum(v, cqnorm, l)
        norm_dve_inverse(v, cqnorm, l)
        norm_dve_diagonals(v, cqnorm, l)
        norm_dve_sum(v, cknorm, l)
        norm_dve_scale(v, cqnorm, l, lambda k: cq[:, k, :], lambda k: p2[:, QN0 + k:QN0 + k + 1],
                       lambda k: cq_hi[:, k, :], lambda k: cq_lo[:, k, :])
        norm_dve_inverse(v, cknorm, l)
        norm_dve_diagonals(v, cknorm, l)
        norm_dve_scale(v, cknorm, l, lambda k: ckv[:, k, :], lambda k: p2[:, KN0 + k:KN0 + k + 1],
                       lambda k: ck_hi[:, k, :], lambda k: ck_lo[:, k, :])

        for b, (a, c) in enumerate(BLOCKS):
            v.wait_ge(ret_ps.sem, ret_ps(l, b + 1))
            v.tensor_tensor(pair[:, b, :, :], score_banks(b), decay[:, c - a, :, :], ALU.mult)\
                .then_inc(ret_at.sem, 1)

        def level(lv):
            if lv < 7:
                size = P >> lv
                blocks = cum[:, :].rearrange("p (n b) -> p n b", b=size)
                middle = blocks[:, :, size // 2 - 1:size // 2].to_broadcast([P, S // size, size])
                v.wait_ge(gk_dve.sem, gk_dve(l, 4))
                v.tensor_tensor(diff[:, lv % 2, :].rearrange("p (n b) -> p n b", b=size), blocks, middle,
                                ALU.subtract).then_inc(lev_d.sem, 1)
                v.wait_ge(lev_d.sem, lev_d(l, 2 * lv + 1))
                v.scalar_tensor_tensor(diff[:, lv % 2, :], diff[:, lv % 2, :], -1.0, diff[:, lv % 2, :],
                                       ALU.mult, ALU.min).then_inc(lev_d.sem, 1)

        def level_qk(lv):
            if lv < 7:
                v.wait_ge(lev_e.sem, lev_e(l, lv + 1))
                v.scalar_tensor_tensor(qe[:, lv % 2, :], gqk[:, 0, :], QK, edec[:, lv % 2, :], ALU.mult, ALU.mult)\
                    .then_inc(lev_q.sem, 1)
                v.tensor_tensor(ke[:, lv % 2, :], gqk[:, 1, :], edec[:, lv % 2, :], ALU.mult).then_inc(lev_q.sem, 1)
            else:
                v.tensor_scalar(qe[:, 1, :], gqk[:, 0, :], QK, None, ALU.mult).then_inc(lev_q.sem, 1)
                v.tensor_scalar(ke[:, 1, :], gqk[:, 1, :], 1.0, None, ALU.mult).then_inc(lev_q.sem, 1)

        level(0)
        level(1)
        level_qk(0)
        level_qk(1)
        v.wait_ge(ret_out.sem, ret_out(l, MH))
        for a in range(T):
            last = v.memset(pair[:, FIRST_BLOCK[a], :, :], 0.0)
        last.then_inc(zero_at.sem, 1)
        v.wait_ge(zero_at.sem, zero_at(l, 1))
        for lv in range(LEVELS):
            if lv + 2 < 7:
                level(lv + 2)
            for a in range(T):
                n = lv * T + a
                v.wait_ge(lev_ps.sem, lev_ps(l, n + 1))
                v.wait_ge(lev_at.sem, lev_at(l, n))
                gate(v, 6)
                v.copy_predicated(pair[:, FIRST_BLOCK[a], :, :],
                                  lmask[:, lv:lv + 1, :].to_broadcast([P, MH, P]),
                                  score_banks(n)).then_inc(lev_at.sem, 1)
            if lv + 2 < LEVELS:
                level_qk(lv + 2)
            if lv == 5:
                tiles = cum[:, :].rearrange("p (n b) -> p n b", b=P)
                v.tensor_tensor(diff[:, 1, :].rearrange("p (n b) -> p n b", b=P),
                                tiles[:, :, P - 1:P].to_broadcast([P, T, P]), tiles, ALU.subtract)\
                    .then_inc(lev_d.sem, 1)
        v.wait_ge(lev_e.sem, lev_e(l, 9))
        v.scalar_tensor_tensor(qe[:, 0, :], gqk[:, 0, :], QK, edec[:, 0, :], ALU.mult, ALU.mult).then_inc(lev_q.sem, 1)
        v.tensor_tensor(ke[:, 0, :], gqk[:, 1, :], edec[:, 1, :], ALU.mult).then_inc(lev_q.sem, 1)
        v.wait_ge(etot_s.sem, etot_s(l, 1))
        v.wait_ge(lev_q.sem, lev_q(l, 18))
        v.tensor_scalar(k3[:, 0, :], ke[:, 0, 0:P], etot[:, 1:2], None, ALU.mult).then_inc(k3_s.sem, 1)
        v.tensor_scalar(k3[:, 1, :], ke[:, 0, P:2 * P], etot[:, 2:3], None, ALU.mult).then_inc(k3_s.sem, 1)
        v.wait_ge(k3_s.sem, k3_s(l, 1))
        v.tensor_scalar(k3[:, 2, :], k3[:, 0, :], etot[:, 2:3], None, ALU.mult).then_inc(k3_s.sem, 1)
        for i in range(14):
            hi, lo = u_parts(i)
            v.wait_ge(u_hi.sem, u_hi(l, i + 1))
            if i in (4, 5):
                e = i - 4
                rotate(v, qr_raw[:, e, :], qr_swap[:, e, :], mcos[:, :], msin[:, :], rt, hi, lo, qrrope.sem,
                       qrrope(l, 4 * e), lambda: v.wait_ge(qrswap_s[e].sem, qrswap_s[e](l, 64)))\
                    .then_inc(u_lo.sem, 1)
            else:
                v.tensor_tensor(lo, bank[U_BANK[i]][:, :], f32(hi), ALU.subtract).then_inc(u_lo.sem, 1)

        attention_dve(v, mla, l, (128 + 64) ** -0.5, SCORE_BANKS, lambda t: causal[:, (3 - t) * P:S], causal_tiles,
                      mpt_hi, mpt_lo, None)
        v.wait_ge(hs_tot.sem, hs_tot(l, KD))
        v.tensor_scalar(st[:, 0, 0:16], bank[6][:, 0:16], 1.0 / 128, 1e-6, ALU.mult, ALU.add).then_inc(hs_var.sem, 1)
        v.tensor_scalar(st[:, 0, 16:48], bank[6][:, 16:48], 1.0 / 64, 1e-6, ALU.mult, ALU.add).then_inc(hs_var.sem, 1)
        v.wait_ge(hs_var.sem, hs_var(l, 2))
        v.reciprocal(st[:, 1, :], st[:, 0, :]).then_inc(hs_inv.sem, 1)
        v.wait_ge(hs_rstd.sem, hs_rstd(l, 1))
        refine_root(v, st[:, 2, :], st[:, 0, :], st[:, 1, :], hs_inv.sem, hs_inv(l, 1))

        def diagonals(k):
            v.wait_ge(hs_bc.sem, hs_bc(l, k - 1))
            for e in range(4 if k < 4 else 8):
                c = 4 * k + e if k < 4 else 16 + 8 * (k - 4) + e
                last = v.tensor_scalar(dg[:, k % 2, e, :], ident[:, :], st[:, 2, c:c + 1], None, ALU.mult)
            last.then_inc(hs_dg.sem, 1)

        def out_gain(k):
            return MO0 + k if k < 4 else GO0 + k - 4

        diagonals(0)
        for k in range(KD):
            if k + 1 < KD:
                diagonals(k + 1)
            gain = p2[:, out_gain(k):out_gain(k) + 1]
            v.wait_ge(hs_bc.sem, hs_bc(l, k + 1))
            v.wait_ge(hs_hi.sem, hs_hi(l, k - 1))
            v.scalar_tensor_tensor(hf[:, k % 2, :], yf[:, k, :], gain, bank[2 + k % 2][:, :], ALU.mult, ALU.mult)\
                .then_inc(hs_n.sem, 1)
            v.wait_ge(hs_n.sem, hs_n(l, k + 1))
            if k >= 4:
                v.tensor_tensor(hf[:, k % 2, :], hf[:, k % 2, :], gates[:, k - 4, :], ALU.mult).then_inc(hs_g.sem, 1)
                v.wait_ge(hs_g.sem, hs_g(l, k - 3))
            v.wait_ge(hs_hi.sem, hs_hi(l, k + 1))
            v.tensor_tensor(hl[:, k, :], hf[:, k % 2, :], f32(hh[:, k, :]), ALU.subtract).then_inc(hs_lo.sem, 1)

        def add_mix(d):
            products_done(v, mix2_chunk(l, OUT2_CHUNK + d))
            v.tensor_tensor(x[:, d, :], x[:, d, :], bank[d % 2][:, :], ALU.add).then_inc(out2_x.sem, 1)

        add_tiles(v, add_mix, ffn3norm, l, last=False)

    def ffn1_at(l):
        return lambda c, i=0: Chunk(0, C1, l, c, i)

    def ffn2_at(l):
        return lambda c, i=0: Chunk(0, C1, l, 61 + MIX1_CHUNKS + c, i)

    def ffn3_at(l):
        return lambda c, i=0: Chunk(L * C1, C2, l, MIX2_CHUNKS + c, i)

    CONST_LOADS = 7
    with nc.Block() as block:

        @block.sync
        def _(sp):
            sp.dma_start(rt[:, 1, :].bitcast(I32), pos_in.partition_broadcast(P)).then_inc(consts_in, 16)
            for dst, c0, c1 in ((ident[:, :], *CONST["ident"]), (causal[:, :], *CONST["causal"]),
                                (halfcol[:, :], *CONST["halfcol"]), (cols[:, :], *CONST["cols"])):
                sp.dma_start(dst, consts[:, c0:c1]).then_inc(consts_in, 16)
            for e in range(2):
                c0 = CONST["halves"][0] + e * P
                sp.dma_start(halves[:, e, :], consts[:, c0:c0 + P]).then_inc(consts_in, 16)
            sp.dma_start(memn[:, :, :], mem_in).then_inc(x_in_sem, 16)
            sp.dma_start(x[:, :, :], x_in).then_inc(x_in_sem, 16)
            sp.wait_ge(led, len(leads))
            with sp.Fori(0, L) as l:
                sp.wait_ge(ffn1.norm.lo.sem, ffn1.norm.lo(l, 0))
                sp.dma_start(p1[:, :], par1[l, :, :]).then_inc(par1_in.sem, 16)
                stack1_chunks(sp, l, load)
            with sp.Fori(0, L) as l:
                sp.wait_ge(finalnorm.scaled.sem, finalnorm.scaled(0, KD))
                sp.wait_ge(ffn3.x.sem, ffn3.x(l, 0))
                sp.dma_start(p2[:, :], par2[l, :, :]).then_inc(par2_in.sem, 16)
                sp.dma_start(cpar[:, :, :], convpar[l, :, :, :]).then_inc(cpar_in.sem, 16)
                for dst, name in ((mcos[:, :], "mcos"), (msin[:, :], "msin"), (rcos[:, :], "rcos"),
                                  (rsin[:, :], "rsin"), (scanmask[:, :], "scanmask")):
                    sp.dma_start(dst, consts[:, CONST[name][0]:CONST[name][1]]).then_inc(tables2_in.sem, 16)
                sp.dma_start(decay[:, :, :, :].rearrange("p d h q -> p (d h q)"),
                             consts[:, CONST["decay"][0]:CONST["decay"][1]]).then_inc(tables2_in.sem, 16)
                sp.dma_start(lmask[:, :, :].rearrange("p v q -> p (v q)").bitcast(I32), masks).then_inc(tables2_in.sem, 16)
                sp.dma_start(gw[0:16, :], gate_w[l, :, :]).then_inc(tables2_in.sem, 16)
                stack2_chunks(sp, l, load)
            for k in range(KD):
                sp.wait_ge(endnorm.scaled.sem, endnorm.scaled(0, k + 1))
                sp.dma_start(y_out[:, k, :], x[:, k, :]).then_inc(y_stored, 16)
            sp.wait_ge(y_stored, 16 * KD)

        @block.gpsimd
        def _(g):
            g.memset(one[:, :], 1.0).then_inc(setup, 1)
            for sem, lead in leads:
                g.sem_inc(sem, lead)
                g.sem_inc(led, 1)
            g.wait_ge(setup, 2)
            with g.Fori(0, L) as l:
                stack1_chunks(g, l, split, short_conv, shared=False)
            with g.Fori(0, L) as l:
                stack2_chunks(g, l, split)

        @block.scalar
        def _(act):
            act.wait_ge(led, len(leads))
            for e in range(2):
                act.wait_ge(tab, 17)
                act.activation((cos1, sin1)[e][:, :], rt[:, 2, :] if e == 0 else rbuf[:, 0, :], ACT.Sin)\
                    .then_inc(tab_sin, 1)
            act.wait_ge(x_in_sem, 32)
            norm_act(act, memnorm, 0, lambda k: memn[:, k, :], lambda a, k: None, width=M)
            with act.Fori(0, L) as l:
                def after_ffn2(a, k):
                    a.wait_ge(ffn2.x.sem, ffn2.x(l, k + 1 - KD))
                    if k == KD - 1:
                        a.wait_ge(par1_in.sem, par1_in(l, 16))

                ffn_act(act, ffn1, l, lambda k: par1_at(0, k), after_ffn2, False)
                mix1_act(act, l)
                xat_act(act, l)
                ffn_act(act, ffn2, l, lambda k: par1_at(4, k), lambda a, k: a.wait_ge(wo_x.sem, wo_x(l, k + 1)), False)
            norm_act(act, finalnorm, 0, x_tile, lambda a, k: a.wait_ge(ffn2.x.sem, ffn2.x(L - 1, k + 1)))
            act.wait_ge(finalnorm.scaled.sem, finalnorm.scaled(0, KD))
            with act.Fori(0, L) as l:
                mix2_act(act, l)
                act.wait_ge(cpar_in.sem, cpar_in(l, 16))
                ffn_act(act, ffn3, l, lambda k: p2[:, FN0 + k:FN0 + k + 1], lambda a, k: a.wait_ge(out2_x.sem, out2_x(l, k + 1)), True)
            norm_act(act, endnorm, 0, x_tile, lambda a, k: a.wait_ge(ffn3.x.sem, ffn3.x(L - 1, k + 1)))

        @block.vector
        def _(v):
            v.memset(ones[:, :], 1.0).then_inc(setup, 1)
            v.wait_ge(led, len(leads))
            v.wait_ge(consts_in, 16 * CONST_LOADS)
            steps = [0]

            def step(ins):
                steps[0] += 1
                ins.then_inc(tab, 1)
                v.wait_ge(tab, steps[0])

            pos, ang, turns = rt[:, 0, :], rt[:, 2, :], rbuf[:, 0, :]
            step(v.tensor_copy(pos, rt[:, 1, :].bitcast(I32)))
            step(v.tensor_scalar(ang, pos, cols[:, 0:1], None, ALU.mult))
            step(v.tensor_scalar(turns, ang, 1.0 / (2 * PI), ROUND, ALU.mult, ALU.add))
            step(v.tensor_scalar(turns, turns, -ROUND, None, ALU.add))
            for part in TWO_PI_PARTS:
                step(v.scalar_tensor_tensor(ang, turns, -part, ang, ALU.mult, ALU.add))
            over = rbuf[:, 1, :]
            step(v.tensor_scalar(over, ang, PI / 2, -2 * PI, ALU.is_gt, ALU.mult))
            step(v.tensor_scalar(turns, ang, PI, -PI, ALU.min, ALU.max))
            step(v.tensor_scalar(turns, turns, cols[:, 1:2], None, ALU.mult))
            step(v.tensor_scalar(ang, ang, PI / 2, None, ALU.add))
            step(v.tensor_tensor(ang, ang, over, ALU.add))
            step(v.tensor_scalar(ang, ang, PI, -PI, ALU.min, ALU.max))
            while steps[0] < 17:
                step(v.memset(over[:, 0:1], 0.0))
            v.wait_ge(x_in_sem, 32)
            norm_dve_sum(v, memnorm, 0, M)
            norm_dve(v, memnorm, 0, lambda k: memn[:, k, :], None, plain_dst=lambda k: memn[:, k, :], width=M)
            for k in range(KD - 1):
                norm_dve_sum_tile(v, ffn1norm, 0, k)
            with v.Fori(0, L) as l:
                v.wait_ge(par1_in.sem, par1_in(l, 16))
                ffn_dve(v, ffn1, l, ffn1_at(l), lambda k: par1_at(0, k), False, 0.5, mixnorm, l)
                mix1_dve(v, l)
                xat_dve(v, l)
                ffn_dve(v, ffn2, l, ffn2_at(l), lambda k: par1_at(4, k), False, 0.5, ffn1norm, l + 1,
                        sum_last=False)
            norm_dve_sum_tile(v, finalnorm, 0, KD - 1)
            norm_dve(v, finalnorm, 0, x_tile, lambda k: p1[:, FIN1 + k:FIN1 + k + 1], plain_dst=x_tile)
            v.wait_ge(finalnorm.scaled.sem, finalnorm.scaled(0, KD))
            norm_dve_sum(v, attnorm, 0)
            with v.Fori(0, L) as l:
                v.wait_ge(par2_in.sem, par2_in(l, 16))
                v.wait_ge(cpar_in.sem, cpar_in(l, 16))
                mix2_dve(v, l)
                ffn_dve(v, ffn3, l, ffn3_at(l), lambda k: p2[:, FN0 + k:FN0 + k + 1], True, 1.0, attnorm, l + 1)
            norm_dve(v, endnorm, 0, x_tile, lambda k: p2[:, FIN2 + k:FIN2 + k + 1], plain_dst=x_tile)

        @block.tensor
        def _(pe):
            pe.wait_ge(led, len(leads))
            pe.wait_ge(setup, 2)
            pe.wait_ge(consts_in, 16 * CONST_LOADS)
            norm_pe(pe, memnorm, 0)
            with pe.Fori(0, L) as l:
                ffn_pe(pe, ffn1, l, ffn1_at(l))
                mix1_pe(pe, l)
                xat_pe(pe, l)
                ffn_pe(pe, ffn2, l, ffn2_at(l))
            norm_pe(pe, finalnorm, 0)
            with pe.Fori(0, L) as l:
                mix2_pe(pe, l)
                ffn_pe(pe, ffn3, l, ffn3_at(l))
            norm_pe(pe, endnorm, 0)


CONST = {}
_at = 0
for _name, _width in (("ident", P), ("causal", S), ("halves", 2 * P), ("halfcol", 2), ("cols", 4), ("mcos", S),
                      ("msin", S), ("rcos", S), ("rsin", S), ("scanmask", S), ("decay", T * MH * P)):
    CONST[_name] = (_at, _at + _width)
    _at += _width
CONST_WIDTH = _at


def constants():
    c = np.zeros((P, CONST_WIDTH), np.float32)

    def put(name, a):
        c[:, CONST[name][0]:CONST[name][1]] = a

    row, col = np.arange(P)[:, None], np.arange(P)[None, :]
    put("ident", row == col)
    put("causal", np.concatenate([np.zeros((P, S - P)), np.where(col > row, MASKED, 0.0)], axis=1))
    put("halves", np.concatenate([np.broadcast_to(col < 64, (P, P)), np.broadcast_to(col >= 64, (P, P))], axis=1))
    put("halfcol", np.concatenate([row < 64, row >= 64], axis=1))

    def inverse_frequency(dim):
        return (10000.0 ** (-np.arange(0, dim, 2) / dim)).astype(np.float32)

    def rows_of(dim):
        r = np.arange(P) % dim
        return inverse_frequency(dim)[r % (dim // 2)], np.where(r < dim // 2, -1.0, 1.0).astype(np.float32)

    freq, sign = rows_of(64)
    put("cols", np.stack([freq, sign, sign * 0, sign * 0], axis=1))
    for cos, sin, dim in (("mcos", "msin", 64), ("rcos", "rsin", DK)):
        freq, sign = rows_of(dim)
        angle = freq[:, None] * np.arange(S, dtype=np.float32)[None, :]
        put(cos, np.cos(angle))
        put(sin, np.sin(angle) * sign[:, None])
    put("scanmask", np.broadcast_to(np.arange(S) % P != 0, (P, S)))
    log_g = np.log(1.0 - 2.0 ** (-5.0 - np.arange(MH)))
    dist = np.arange(T)[:, None, None, None] * P + col[0][None, None, None, :] - np.arange(P)[None, :, None, None]
    decay = np.where(dist >= 0, np.exp(log_g[None, None, :, None] * np.maximum(dist, 0)), 0.0) * DK ** -0.5
    put("decay", decay.transpose(1, 0, 2, 3).reshape(P, -1))
    masks = np.zeros((P, LEVELS, P), np.uint8)
    for lv in range(LEVELS - 1):
        size = P >> lv
        masks[:, lv, :] = ((row // size == col // size) & (row % size < size // 2) & (col % size >= size // 2))
    masks[:, LEVELS - 1, :] = row == col
    return c, masks.reshape(P, LEVELS * P).view(np.int32)


def layouts(inputs):
    a = {k: np.asarray(v) for k, v in inputs.items()}

    def rows(m):
        return m.reshape(-1, P, m.shape[-1]).transpose(1, 0, 2)

    def col_chunks(w):
        k, n = w.shape[0] // P, w.shape[1] // P
        return w.reshape(k, P, n, P).transpose(2, 1, 0, 3).reshape(n, P, k * P)

    def value_chunks(w):
        k = w.shape[0] // P
        return w.reshape(k // 2, 2, P, S).transpose(0, 2, 1, 3).reshape(k // 2, P, 2 * S)

    def gate_up(g, u):
        return np.concatenate([np.stack([col_chunks(g[l]), col_chunks(u[l])], axis=1).reshape(2 * KF, P, A)
                               for l in range(L)])

    def down(w):
        return np.concatenate([col_chunks(w[l]).reshape(KD, P, 2, DN).transpose(0, 2, 1, 3).reshape(2 * KD, P, DN)
                               for l in range(L)])

    def pieces(w, sizes):
        return np.split(w, np.cumsum(sizes)[:-1], axis=1)

    def columns(*vectors):
        return np.concatenate([v.reshape(-1, P).T for v in vectors], axis=1)

    mid, widx, par1 = [], [], []
    for l in range(L):
        a_val, a_gate, b_gate, c_gate, b_h, q, k, v, q_idx, k_idx, w_idx = pieces(
            a["w_in"][l], (256, 256, 256, 256, 256, 512, 512, 512, 256, 64, IDXH))
        mem_k, mem_v = a["xa_wkv"][l][:, :D], a["xa_wkv"][l][:, D:]
        gated = np.stack([col_chunks(a_val), col_chunks(a_gate)], axis=1).reshape(4, P, A)
        mid += [gated, col_chunks(q_idx), col_chunks(np.concatenate([k_idx, k_idx], axis=1)), col_chunks(k), col_chunks(q),
                col_chunks(c_gate), col_chunks(b_h), col_chunks(b_gate), value_chunks(v), col_chunks(a["w_out"][l]), col_chunks(mem_k), value_chunks(mem_v[:, :S]),
                value_chunks(mem_v[:, S:]), col_chunks(a["xa_wq"][l]), col_chunks(a["xa_wo"][l])]
        widx.append(rows(w_idx).reshape(P, 4 * KD))
        par1.append(columns(a["ffn1_norm"][l], a["mix_norm"][l], a["xa_norm"][l], a["mem_norm"][l], a["ffn2_norm"][l],
                            a["conf_dw"][l].reshape(-1), a["conf_dw_b"][l], a["conf_ln_g"][l], a["conf_ln_b"][l],
                            a["sc_dw"][l].reshape(-1), a["final_norm"]))
    mix2, par2, convpar = [], [], []
    for l in range(L):
        c_q, c_kv, k_r, g_q, g_k, g_v, g_lr, g_g, r_q, r_k, r_v, r_g = pieces(
            a["w_in_2"][l], (384, 256, 64, 128, 128, 256, 16, 256, 128, 128, 256, 256))
        g_lr = np.concatenate([g_lr, np.zeros((D, P - 16), np.float32)], axis=1)
        uq = a["mla_w_uq_2"][l].reshape(384, MH, 192)
        nope, rope = uq[:, :, :128].reshape(384, 512), uq[:, :, 128:].reshape(384, 256)
        ukv = a["mla_w_ukv_2"][l].reshape(256, MH, 256)
        uk, uv = ukv[:, :, :128].reshape(256, 512), ukv[:, :, 128:].reshape(256, 512)
        uq = col_chunks(np.concatenate([nope, rope], axis=1)).reshape(3, 2, P, 3 * P).transpose(0, 2, 1, 3)
        uq = np.concatenate([uq.reshape(3, P, 6 * P), np.zeros((3, P, A - 6 * P), np.float32)], axis=2)
        uk = col_chunks(uk).transpose(1, 0, 2).reshape(1, P, A)
        mix2 += [col_chunks(np.concatenate([g_lr, g_q, g_k, r_q, r_k, k_r, k_r, c_q, c_kv], axis=1)),
                 value_chunks(np.concatenate([g_v, r_v], axis=1)), col_chunks(np.concatenate([g_g, r_g], axis=1)),
                 uq, uk, value_chunks(uv), col_chunks(a["w_out_2"][l])]
        par2.append(columns(a["attn_norm_2"][l], a["mla_q_norm_2"][l], a["mla_kv_norm_2"][l], a["mla_out_norm_2"][l],
                            a["gla_b_gate_2"][l], a["gla_out_norm_2"][l], a["ret_out_norm_2"][l], a["ffn_norm_2"][l],
                            a["final_norm_2"]))
        convpar.append(np.concatenate([a["ffn_conv_w_2"][l], a["ffn_conv_b_2"][l][None]]).reshape(4, KF, P)
                       .transpose(2, 1, 0))
    consts, masks = constants()
    return {
        "x_in": rows(a["x"][0].T), "mem_in": rows(a["mem"][0].T), "pos_in": a["positions"].reshape(1, S),
        "par1": np.stack(par1), "par2": np.stack(par2), "convpar": np.stack(convpar), "consts": consts,
        "masks": masks, "gate_w": a["gla_w_gate_2"],
        "gu1": gate_up(a["ffn1_w_gate"], a["ffn1_w_up"]), "dn1": down(a["ffn1_w_down"]),
        "widx": np.stack(widx), "mid": np.concatenate(mid),
        "gu2": gate_up(a["ffn2_w_gate"], a["ffn2_w_up"]), "dn2": down(a["ffn2_w_down"]),
        "mix2": np.concatenate(mix2), "up2": gate_up(a["ffn_w_up_2"][:, :, :F], a["ffn_w_up_2"][:, :, F:]),
        "dn3": down(a["ffn_w_down_2"]),
    }


def kernel(**inputs):
    import concourse.bacc as bacc
    from concourse.bass_utils import run_bass_kernel_spmd

    nc = bacc.Bacc("TRN2", target_bir_lowering=False, num_devices=1)
    arrays, args = {}, []
    for name, a in layouts(inputs).items():
        arrays[name] = np.ascontiguousarray(a)
        args.append(nc.dram_tensor(name, a.shape, mybir.dt.from_np(a.dtype), kind="ExternalInput").ap())
    y = nc.dram_tensor("y_out", (P, KD, S), F32, kind="ExternalOutput").ap()
    program(nc, *args, y)
    out = run_bass_kernel_spmd(nc, [arrays], core_ids=[0]).results[0]["y_out"]
    return out.transpose(2, 1, 0).reshape(1, S, D)
```
